# Optimizing a Trainium2 kernel written in Bass

```python
import math
import jax, jax.numpy as jnp
from jax import lax
import numpy as np

D_MODEL = 1024
BATCH = 1
SEQ = 256
DEPTH = 2

GRID_W = 64
CTX_LEN = 256
RMS_EPS = 1e-6
N_MOD = 9
D_FF = 2816
POOL_WINDOWS = (2, 4, 8, 16)
POOL_GROUPS = len(POOL_WINDOWS)
POOL_DIM = D_MODEL // 2
POOL_GROUP_DIM = POOL_DIM // POOL_GROUPS
MLA_HEADS = D_MODEL // 128
QK_NOPE_DIM = 64
QK_ROPE_DIM = 32
QK_HEAD_DIM = QK_NOPE_DIM + QK_ROPE_DIM
V_HEAD_DIM = 64
Q_LORA_RANK = 768
KV_LORA_RANK = 256
ROPE_AXIS_DIM = QK_ROPE_DIM // 2
ROPE_THETA = 10000.0
ATTN_SCALE = 1.0 / math.sqrt(QK_HEAD_DIM)
QBLOCK = 128
AB_IN_DIM = POOL_DIM + Q_LORA_RANK + KV_LORA_RANK + QK_ROPE_DIM
AB_OUT_DIM = POOL_DIM + MLA_HEADS * V_HEAD_DIM
CONV_DIM = D_MODEL
CONV_WIDTH = 3
N_EVEN = (DEPTH + 1) // 2
N_ODD = DEPTH // 2

kernel_name = 'hybrid_pool_mla_shortconv_dit_block'

def rmsnorm(x, g):
    xf = x.astype(jnp.float32)
    y = xf * lax.rsqrt(jnp.mean(xf * xf, axis=-1, keepdims=True) + RMS_EPS)
    return (y * g.astype(jnp.float32)).astype(x.dtype)

def modulation(cond, w, b):
    m = jax.nn.silu(cond) @ w + b
    return m.reshape(cond.shape[0], 1, N_MOD, cond.shape[-1])

def adaln(s, gain, m, k):
    shift, scale, gate = m[:, :, 3 * k], m[:, :, 3 * k + 1], m[:, :, 3 * k + 2]
    return rmsnorm(s, gain) * (1 + scale) + shift, gate

def swiglu(u, wg, wu, wd):
    return (jax.nn.silu(u @ wg) * (u @ wu)) @ wd

def ffn_half(s, m, k, gain, wg, wu, wd):
    u, gate = adaln(s, gain, m, k)
    return s + 0.5 * gate * swiglu(u, wg, wu, wd)

def multiscale_pool(u, w_grp, scale):
    b, l, _ = u.shape
    uf = u.astype(jnp.float32).reshape(b, l, POOL_GROUPS, POOL_GROUP_DIM)
    cs = jnp.concatenate([jnp.zeros_like(uf[:, :1]), jnp.cumsum(uf, axis=1)], axis=1)
    t = jnp.arange(l)
    outs = []
    for gi, w in enumerate(POOL_WINDOWS):
        lo = jnp.clip(t - w // 2, 0, l - 1)
        hi = jnp.clip(t + (w - w // 2 - 1), 0, l - 1)
        win_sum = cs[:, hi + 1, gi] - cs[:, lo, gi]
        cnt = (hi - lo + 1).astype(jnp.float32)[None, :, None]
        outs.append(win_sum / cnt - uf[:, :, gi])
    p = jnp.stack(outs, axis=2).astype(u.dtype)
    y = jnp.einsum('blgc,gcd->blgd', p, w_grp).reshape(b, l, POOL_DIM)
    return y * scale

def axial_rope_tables(length):
    rows = length // GRID_W
    row = jnp.repeat(jnp.arange(rows), GRID_W).astype(jnp.float32)
    col = jnp.tile(jnp.arange(GRID_W), rows).astype(jnp.float32)
    freqs = jnp.power(ROPE_THETA, -jnp.arange(0, ROPE_AXIS_DIM, 2, dtype=jnp.float32) / ROPE_AXIS_DIM)
    ang_r = (row[:, None] * freqs)[:, None, :]
    ang_c = (col[:, None] * freqs)[:, None, :]
    return (jnp.cos(ang_r), jnp.sin(ang_r), jnp.cos(ang_c), jnp.sin(ang_c))

def rot_half(z, cos, sin):
    h = z.shape[-1] // 2
    z1, z2 = z[..., :h], z[..., h:]
    return jnp.concatenate([z1 * cos - z2 * sin, z2 * cos + z1 * sin], axis=-1)

def apply_axial_rope(z, tabs):
    cos_r, sin_r, cos_c, sin_c = (tb.astype(z.dtype) for tb in tabs)
    return jnp.concatenate([rot_half(z[..., :ROPE_AXIS_DIM], cos_r, sin_r),
                            rot_half(z[..., ROPE_AXIS_DIM:], cos_c, sin_c)], axis=-1)

def mla_queries(cq, q_norm_g, w_uq):
    b, l, _ = cq.shape
    q = (rmsnorm(cq, q_norm_g) @ w_uq).reshape(b, l, MLA_HEADS, QK_HEAD_DIM)
    return q[..., :QK_NOPE_DIM], q[..., QK_NOPE_DIM:]

def mla_keys_values(ckv, kv_norm_g, w_ukv):
    b, l, _ = ckv.shape
    kv = (rmsnorm(ckv, kv_norm_g) @ w_ukv).reshape(b, l, MLA_HEADS, QK_NOPE_DIM + V_HEAD_DIM)
    return kv[..., :QK_NOPE_DIM], kv[..., QK_NOPE_DIM:]

def mla_attention(q_nope, q_rope, k_nope, k_rope, v):
    b, l, h, _ = q_nope.shape
    nb = l // QBLOCK

    def to_blocks(z):
        return z.reshape(b, nb, QBLOCK, h, z.shape[-1]).swapaxes(0, 1)

    def block(args):
        qn, qr = args
        s = (jnp.einsum('bqhd,bkhd->bhqk', qn, k_nope, preferred_element_type=jnp.float32)
             + jnp.einsum('bqhr,bkr->bhqk', qr, k_rope, preferred_element_type=jnp.float32))
        p = jax.nn.softmax(s * ATTN_SCALE, axis=-1).astype(v.dtype)
        return jnp.einsum('bhqk,bkhd->bqhd', p, v)

    o = lax.map(block, (to_blocks(q_nope), to_blocks(q_rope)))
    return o.swapaxes(0, 1).reshape(b, l, h * V_HEAD_DIM)

def pool_mla_mixer(uh, ug, tabs, w_in, pool_w, pool_scale, q_norm_g, w_uq, kv_norm_g, w_ukv, w_out, ctx_out):
    cuts = [POOL_DIM, POOL_DIM + Q_LORA_RANK, POOL_DIM + Q_LORA_RANK + KV_LORA_RANK]
    pool_h, cq_h, ckv_h, kr_h = jnp.split(uh @ w_in, cuts, axis=-1)
    pool_g, cq_g, ckv_g, kr_g = jnp.split(ug @ w_in, cuts, axis=-1)
    qn_h, qr_h = mla_queries(cq_h, q_norm_g, w_uq)
    qr_h = apply_axial_rope(qr_h, tabs)
    kn_h, v_h = mla_keys_values(ckv_h, kv_norm_g, w_ukv)
    kr_h = apply_axial_rope(kr_h[:, :, None, :], tabs)[:, :, 0]
    kn_g, v_g = mla_keys_values(ckv_g, kv_norm_g, w_ukv)
    attn_h = mla_attention(qn_h, qr_h,
                           jnp.concatenate([kn_h, kn_g], axis=1),
                           jnp.concatenate([kr_h, kr_g], axis=1),
                           jnp.concatenate([v_h, v_g], axis=1))
    out_h = jnp.concatenate([multiscale_pool(pool_h, pool_w, pool_scale), attn_h], axis=-1) @ w_out
    out_g = None
    if ctx_out:
        qn_g, qr_g = mla_queries(cq_g, q_norm_g, w_uq)
        attn_g = mla_attention(qn_g, qr_g, kn_g, kr_g, v_g)
        out_g = jnp.concatenate([multiscale_pool(pool_g, pool_w, pool_scale), attn_g], axis=-1) @ w_out
    return out_h, out_g

def short_conv_mixer(u, w_in, conv_w, w_out):
    b_gate, c_gate, val = jnp.split(u @ w_in, 3, axis=-1)
    z = c_gate * val
    z = lax.conv_general_dilated(z, conv_w[:, None, :].astype(z.dtype), window_strides=(1,),
                                 padding=((CONV_WIDTH // 2, CONV_WIDTH // 2),),
                                 dimension_numbers=('NWC', 'WIO', 'NWC'),
                                 feature_group_count=z.shape[-1])
    return (b_gate * z) @ w_out

def setup_inputs(seed: int = 0) -> dict:
    key = jax.random.key(seed)
    ks = jax.random.split(key, 24)

    def nrm(k, shape, scale):
        return jax.random.normal(k, shape, jnp.float32) * scale

    D, F = D_MODEL, D_FF
    return {
        'x': nrm(ks[0], (BATCH, SEQ, D), 1.0),
        'c': nrm(ks[1], (BATCH, D), 1.0),
        'ctx': nrm(ks[2], (BATCH, CTX_LEN, D), 1.0),
        'c_ctx': nrm(ks[3], (D,), 1.0),
        'norm_g': 1.0 + nrm(ks[4], (DEPTH, 3, D), 0.02),
        'w_mod': nrm(ks[5], (DEPTH, D, N_MOD * D), 0.5 * D ** -0.5),
        'b_mod': nrm(ks[6], (DEPTH, N_MOD * D), 0.02),
        'ffn_w_gate': nrm(ks[7], (DEPTH, 2, D, F), D ** -0.5),
        'ffn_w_up': nrm(ks[8], (DEPTH, 2, D, F), D ** -0.5),
        'ffn_w_down': nrm(ks[9], (DEPTH, 2, F, D), F ** -0.5),
        'ab_w_in': nrm(ks[10], (N_EVEN, D, AB_IN_DIM), D ** -0.5),
        'pool_w': nrm(ks[11], (N_EVEN, POOL_GROUPS, POOL_GROUP_DIM, POOL_GROUP_DIM), POOL_GROUP_DIM ** -0.5),
        'pool_scale': 1.0 + nrm(ks[12], (N_EVEN, POOL_DIM), 0.1),
        'q_norm_g': 1.0 + nrm(ks[13], (N_EVEN, Q_LORA_RANK), 0.02),
        'w_uq': nrm(ks[14], (N_EVEN, Q_LORA_RANK, MLA_HEADS * QK_HEAD_DIM), Q_LORA_RANK ** -0.5),
        'kv_norm_g': 1.0 + nrm(ks[15], (N_EVEN, KV_LORA_RANK), 0.02),
        'w_ukv': nrm(ks[16], (N_EVEN, KV_LORA_RANK, MLA_HEADS * (QK_NOPE_DIM + V_HEAD_DIM)), KV_LORA_RANK ** -0.5),
        'ab_w_out': nrm(ks[17], (N_EVEN, AB_OUT_DIM, D), AB_OUT_DIM ** -0.5),
        'conv_w_in': nrm(ks[18], (N_ODD, D, 3 * CONV_DIM), D ** -0.5),
        'conv_w': nrm(ks[19], (N_ODD, CONV_WIDTH, CONV_DIM), CONV_WIDTH ** -0.5),
        'conv_w_out': nrm(ks[20], (N_ODD, CONV_DIM, D), CONV_DIM ** -0.5),
        'final_norm_g': 1.0 + nrm(ks[21], (D,), 0.02),
    }

def reference(x, c, ctx, c_ctx, norm_g, w_mod, b_mod, ffn_w_gate, ffn_w_up, ffn_w_down,
              ab_w_in, pool_w, pool_scale, q_norm_g, w_uq, kv_norm_g, w_ukv, ab_w_out,
              conv_w_in, conv_w, conv_w_out, final_norm_g):
    tabs = axial_rope_tables(x.shape[1])
    h, g = x, ctx
    cond_g = c_ctx[None, :]
    for i in range(DEPTH):
        last = i == DEPTH - 1
        even = i % 2 == 0
        j = i // 2
        ctx_out = not last
        need_g = even or ctx_out
        m_h = modulation(c, w_mod[i], b_mod[i])
        h = ffn_half(h, m_h, 0, norm_g[i, 0], ffn_w_gate[i, 0], ffn_w_up[i, 0], ffn_w_down[i, 0])
        if need_g:
            m_g = modulation(cond_g, w_mod[i], b_mod[i])
            g = ffn_half(g, m_g, 0, norm_g[i, 0], ffn_w_gate[i, 0], ffn_w_up[i, 0], ffn_w_down[i, 0])
        uh, gate_h = adaln(h, norm_g[i, 1], m_h, 1)
        out_g = None
        if even:
            ug, gate_g = adaln(g, norm_g[i, 1], m_g, 1)
            out_h, out_g = pool_mla_mixer(uh, ug, tabs, ab_w_in[j], pool_w[j], pool_scale[j],
                                          q_norm_g[j], w_uq[j], kv_norm_g[j], w_ukv[j], ab_w_out[j], ctx_out)
        else:
            out_h = short_conv_mixer(uh, conv_w_in[j], conv_w[j], conv_w_out[j])
            if ctx_out:
                ug, gate_g = adaln(g, norm_g[i, 1], m_g, 1)
                out_g = short_conv_mixer(ug, conv_w_in[j], conv_w[j], conv_w_out[j])
        h = h + gate_h * out_h
        h = ffn_half(h, m_h, 2, norm_g[i, 2], ffn_w_gate[i, 1], ffn_w_up[i, 1], ffn_w_down[i, 1])
        if ctx_out:
            g = g + gate_g * out_g
            g = ffn_half(g, m_g, 2, norm_g[i, 2], ffn_w_gate[i, 1], ffn_w_up[i, 1], ffn_w_down[i, 1])
    return rmsnorm(h, final_norm_g)


_drawn_inputs = setup_inputs


def setup_inputs(seed=0):
    import zlib

    import numpy as np

    out = dict(_drawn_inputs(seed))
    spreads = {}
    factors = {'ctx': 4.654,
     'norm_g': 3.898,
     'q_norm_g': 8.0,
     'w_uq': 2.669,
     'kv_norm_g': 8.0,
     'final_norm_g': 2.765}
    for name, (base, spread) in spreads.items():
        noise = np.random.default_rng([zlib.crc32(name.encode()), seed]).standard_normal(out[name].shape)
        drawn = base * np.exp(spread * noise) if base else spread * noise
        out[name] = __import__('jax').numpy.asarray(drawn.astype(out[name].dtype))
    for name, factor in factors.items():
        out[name] = (out[name] * factor).astype(out[name].dtype)
    return out
```

```python
import numpy as np
import concourse.bass as bass
from concourse import mybir
from contextlib import ExitStack

D, T, FF = 1024, 256, 2816
P = 128
KT = D // P
STEPS = FF // (2 * P)
CH = 2048
RING = 3
FFN_CHUNKS = 3 * STEPS
MIX_CHUNKS, CONV_CHUNKS = 16, 16
HEADS, NOPE, ROPE, VD = 8, 64, 32, 64
QR, KVR = 768 // P, 256 // P
PAIRS = HEADS // 2
EPS = 1e-6
ATTN_SCALE = 1.0 / float(np.sqrt(NOPE + ROPE))
WINDOWS = (2, 4, 8, 16)
PAD = 8
PW = T + 2 * PAD
LAYERS, NMOD = 2, 9
HALVES = 2 * NMOD
HALF = 512

PARAM = {}
_at = 0
for _name, _n in (("norm_g", LAYERS * 3 * KT), ("b_mod", LAYERS * NMOD * KT), ("pool_scale", 4), ("q_norm_g", QR),
                  ("kv_norm_g", KVR), ("conv_w", 3 * KT), ("final_norm_g", KT), ("cond", 2 * KT)):
    PARAM[_name] = _at
    _at += _n
N_PARAM = _at

PASS = [0, 33, 82, 115, 164]
MIX, CONV = 66, 148
N_CHUNKS = 197
START_HALVES = 4


def ring(n, i=0):
    return n % RING, i + (n // RING + 1)


def mod_ops(half):
    return 2 * KT if half < HALVES else KT


def mod_steps_before(half):
    return sum(mod_ops(h) for h in range(START_HALVES, half))


def build(nc, stream, w_mod, x_h, x_g, params, consts, inv_count, out):
    f32, f32r = mybir.dt.float32, mybir.dt.float32r
    ALU, ACT, AX = mybir.AluOpType, mybir.ActivationFunctionType, mybir.AxisListType
    ADD, SUB, MUL = ALU.add, ALU.subtract, ALU.mult
    place = [16512]

    def sb(name, shape, dt, at=None):
        size = 4 * int(np.prod(shape[1:]))
        if at is None:
            at = place[0]
            place[0] += (size + 31) // 32 * 32
        t = nc.alloc_sbuf_tensor_at(name, shape, dt, offset=at)
        where[name] = at
        return t

    where = {}
    raw = sb("raw", [P, RING, CH], f32)
    w_hi = sb("w_hi", [P, RING, CH], f32r)
    w_lo = sb("w_lo", [P, RING, CH], f32r)
    mod_raw = sb("mod_raw", [P, 2, 4, HALF], f32)
    mod_acc = sb("mod_acc", [P, 2, HALF], f32)
    resid = sb("resid", [P, 2, KT, T], f32)
    u_hi = sb("u_hi", [P, KT, 2 * T], f32r)
    u_lo = sb("u_lo", [P, KT, 2 * T], f32r)
    scratch = sb("scratch", [P, KT, T], f32)
    silu = sb("silu", [P, 2 * T], f32)
    prod = sb("prod", [P, 2 * T], f32)
    hid_hi = sb("hid_hi", [P, 2 * T], f32r)
    hid_lo = sb("hid_lo", [P, 2 * T], f32r)
    kvn_hi = sb("kvn_hi", [P, KVR, 2 * T], f32r)
    kvn_lo = sb("kvn_lo", [P, KVR, 2 * T], f32r)
    mix_hi = sb("mix_hi", [P, KT, T], f32r)
    mix_lo = sb("mix_lo", [P, KT, T], f32r)
    region_q = sb("cq", [P, 10 * T], f32)
    region_kv = sb("ckv_region", [P, 8 * T], f32)
    std = sb("std", [P, T], f32)
    rstd = sb("rstd", [P, T], f32)
    par = sb("par", [P, N_PARAM], f32)
    con = sb("con", [P, P + 2 * T], f32)
    ones = sb("ones", [P, P], f32)
    zeros = sb("zeros", [P, T], f32r)
    mod_out = sb("mod_out", [P, LAYERS * NMOD * KT, 2], f32)
    coef = sb("coef", [P, 4, KT], f32)
    cond = sb("cond", [P, KT, 2], f32)
    eps = sb("eps", [P, 1], f32)
    stat = sb("stat", [P, 4, 16], f32)
    assert place[0] <= nc.sbuf_usable_end, place[0]

    cq = region_q[:, 0:QR * T].rearrange("p (k t) -> p k t", k=QR)
    q_f = sb("q_f", [P, 2 * T], f32, where["cq"])
    rope_a = sb("rope_a", [P, 2 * T], f32, where["cq"] + 8 * T)
    rope_b = sb("rope_b", [P, 2 * T], f32, where["cq"] + 16 * T)
    q_hi = sb("q_hi", [P, 2 * T], f32r, where["cq"] + 24 * T)
    q_lo = sb("q_lo", [P, 2 * T], f32r, where["cq"] + 32 * T)
    ckv = region_kv[:, 0:4 * T].rearrange("p (k t) -> p k t", k=KVR)
    ckv_sq = region_kv[:, 4 * T:8 * T].rearrange("p (k t) -> p k t", k=KVR)
    k_hi = sb("k_hi", [P, 2, 2 * T], f32r, where["ckv_region"])
    k_lo = sb("k_lo", [P, 2, 2 * T], f32r, where["ckv_region"] + 16 * T)
    cq_sq = sb("cq_sq", [P, QR, T], f32, where["mix_hi"])
    inv_cnt = sb("inv_cnt", [P, 4, T], f32, where["mix_lo"])
    kv_std = sb("kv_std", [P, 2 * T], f32, where["scratch"])
    kv_rstd = sb("kv_rstd", [P, 2 * T], f32, where["scratch"] + 8 * T)
    kr_f = sb("kr_f", [P, 2 * T], f32, where["scratch"] + 16 * T)
    v_hi = sb("v_hi", [P, 2 * T], f32r, where["scratch"])
    v_lo = sb("v_lo", [P, 2 * T], f32r, where["scratch"] + 8 * T)
    qn_hi = sb("qn_hi", [P, QR, T], f32r, where["u_hi"])
    qn_lo = sb("qn_lo", [P, QR, T], f32r, where["u_hi"] + 4 * QR * T)
    probs = sb("probs", [P, 2, 2 * T], f32, where["u_hi"] + 8 * QR * T)
    pt_hi = sb("pt_hi", [P, 2, 4, T], f32r, where["u_lo"])
    pt_lo = sb("pt_lo", [P, 2, 4, T], f32r, where["u_lo"] + 32 * T)
    pad_x = sb("pad_x", [P, 4, PW], f32, where["mod_raw"])
    win2 = sb("win2", [P, 4, PW], f32, where["mod_raw"] + 16 * PW)
    win4 = sb("win4", [P, 3, PW], f32, where["mod_raw"] + 32 * PW)
    win8 = sb("win8", [P, 2, PW], f32, where["mod_raw"] + 44 * PW)
    win16 = sb("win16", [P, 1, PW], f32, where["mod_raw"] + 52 * PW)
    p_hi = sb("p_hi", [P, 4, T], f32r, where["silu"])
    p_lo = sb("p_lo", [P, 4, T], f32r, where["silu"] + 16 * T)
    z_pad = sb("z_pad", [P, 2, T + 2], f32, where["scratch"])
    conv_1 = sb("conv_1", [P, 2, T], f32, where["scratch"] + 3072)
    conv_2 = sb("conv_2", [P, 2, T], f32, where["scratch"] + 5120)

    def col(name, k=0, n=1):
        return par[:, PARAM[name] + k:PARAM[name] + k + n]

    def shift(layer, kind, c, k=0, n=1, which=0):
        at = layer * NMOD * KT + (3 * kind + which) * KT + k
        return mod_out[:, at:at + n, c]

    JOINS = [(0, None, (0, 0)), (1, None, (0, 0)), (0, (0, 0, 0.5), (0, 1)), (1, (0, 0, 0.5), (0, 1)),
             (0, (0, 1, 1.0), (0, 2)), (0, (0, 2, 0.5), (1, 0)), (0, (1, 0, 0.5), (1, 1)),
             (0, (1, 1, 1.0), (1, 2)), (0, (1, 2, 0.5), None)]

    ctx = ExitStack()
    with ctx:
        psum = ctx.enter_context(nc.psum_tensor("psum", [P, 8, 512], f32))
        GATE, UP, MODB, SSQ = 4, 5, 6, 7

        def sem(name):
            return ctx.enter_context(nc.semaphore(name))

        raw_arrived = [sem(f"raw_arrived{s}") for s in range(RING)]
        hi_ready = sem("hi_ready")
        lo_ready = [sem(f"lo_ready{s}") for s in range(RING)]
        multiplied = sem("multiplied")
        mod_arrived = [sem("mod_arrived0"), sem("mod_arrived1")]
        mod_used = [sem("mod_used0"), sem("mod_used1")]
        mod_reduced = sem("mod_reduced")
        mod_written = sem("mod_written")
        inputs_in = sem("inputs_in")
        context_in = sem("context_in")
        params_in = sem("params_in")
        inv_in = sem("inv_in")
        consts_set = sem("consts_set")
        cond_ready = sem("cond_ready")
        acc_ready, resid_done, sq_done, ssq_done, std_done, rstd_done = (
            sem(n) for n in ("acc_ready", "resid_done", "sq_done", "ssq_done", "std_done", "rstd_done"))
        t_done, u_hi_done, u_lo_done = sem("t_done"), sem("u_hi_done"), sem("u_lo_done")
        silu_done, prod_done, hid_hi_done, hid_lo_done = (
            sem(n) for n in ("silu_done", "prod_done", "hid_hi_done", "hid_lo_done"))
        dve_step, mod_step = sem("dve_step"), sem("mod_step")
        act_step = sem("act_step")
        pool_step = sem("pool_step")
        pad_zeroed, pool_copied, pooled, p_hi_done, p_lo_done = (
            sem(n) for n in ("pad_zeroed", "pool_copied", "pooled", "p_hi_done", "p_lo_done"))
        kv_sq_done, kv_ssq_done, kv_std_done, kv_t_done, kv_hi_done, kv_lo_done = (
            sem(n) for n in ("kv_sq_done", "kv_ssq_done", "kv_std_done", "kv_t_done", "kv_hi_done", "kv_lo_done"))
        q_sq_done, q_ssq_done, q_std_done, q_t_done, qn_hi_done, qn_lo_done = (
            sem(n) for n in ("q_sq_done", "q_ssq_done", "q_std_done", "q_t_done", "qn_hi_done", "qn_lo_done"))
        kr_done, kr_hi_done, kr_lo_done = sem("kr_done"), sem("kr_hi_done"), sem("kr_lo_done")
        q_proj, k_proj, q_nope, q_roped, q_hi_done, q_lo_done = (
            sem(n) for n in ("q_proj", "k_proj", "q_nope", "q_roped", "q_hi_done", "q_lo_done"))
        k_hi_done, k_lo_done, v_hi_done, v_lo_done = (sem(n) for n in ("k_hi_done", "k_lo_done", "v_hi_done", "v_lo_done"))
        scored, neg_max, exp_done, p_normal, p_turned, pt_hi_done, pt_lo_done = (
            sem(n) for n in ("scored", "neg_max", "exp_done", "p_normal", "p_turned", "pt_hi_done", "pt_lo_done"))
        pv_done, attn_hi_done, attn_lo_done = sem("pv_done"), sem("attn_hi_done"), sem("attn_lo_done")
        pool_hi_done, pool_lo_done = sem("pool_hi_done"), sem("pool_lo_done")
        c_copied, z_done, conv_done, conv_hi_done, conv_lo_done = (
            sem(n) for n in ("c_copied", "z_done", "conv_done", "conv_hi_done", "conv_lo_done"))
        stored = sem("stored")

        block = ctx.enter_context(nc.Block())

        def turned_hi(act, r, a):
            for b in range(2):
                n = 4 * r + 2 * a + b
                act.wait_ge(p_turned, n + 1)
                act.activation(pt_hi[:, a, 2 * b:2 * b + 2, :],
                               psum[:, 2 * a + b, :].rearrange("p (k t) -> p k t", k=2), ACT.Copy).then_inc(pt_hi_done, 1)

        def split_step(dve, split_lo, hidden_product, hidden_low, b, k):
            for j in (3, 4):
                if (b + j) % RING == 1:
                    split_lo(b + j)
            dve.wait_ge(multiplied, b + 3)
            hidden_product(k)
            hidden_low(k)
            if (b + 5) % RING == 1:
                split_lo(b + 5)

        def turned_lo(dve, r, a):
            for b in range(2):
                n = 4 * r + 2 * a + b
                dve.wait_ge(pt_hi_done, n + 1)
                dve.tensor_tensor(pt_lo[:, a, 2 * b:2 * b + 2, :],
                                  psum[:, 2 * a + b, :].rearrange("p (k t) -> p k t", k=2),
                                  pt_hi[:, a, 2 * b:2 * b + 2, :].bitcast(f32), SUB).then_inc(pt_lo_done, 1)

        @block.sync
        def _(sp):
            def load(n, row, i=0):
                slot, uses = ring(n, i)
                if n >= RING:
                    sp.wait_ge(lo_ready[slot], uses - 1)
                sp.dma_start(raw[:, slot, :], stream[row]).then_inc(raw_arrived[slot], 16)

            def load_mod(half, i=0):
                for kh in range(2):
                    if half > START_HALVES:
                        sp.wait_ge(mod_step, i * mod_ops(half - 1) + mod_steps_before(half - 1)
                                   + mod_ops(half - 1) // 2 * (kh + 1))
                    elif half > 0:
                        sp.wait_ge(mod_used[kh], half)
                    sp.dma_start(mod_raw[:, kh, :, :], w_mod[(i + half) * 2 + kh]).then_inc(mod_arrived[kh], 16)

            sp.dma_start(par[:, :], params).then_inc(params_in, 16)
            sp.dma_start(con[:, :], consts).then_inc(params_in, 16)
            load_mod(0)
            sp.dma_start(resid[:, 0, :, :], x_h).then_inc(inputs_in, 16)
            for half in range(1, START_HALVES):
                load_mod(half)
                load(half - 1, half - 1)
            sp.dma_start(resid[:, 1, :, :], x_g).then_inc(context_in, 16)
            sp.dma_start(inv_cnt[:, :, :], inv_count).then_inc(inv_in, 16)
            load_mod(START_HALVES)
            for n in range(3, 6):
                load(n, n)
            with sp.Fori(0, 9) as i:
                for j in range(RING):
                    load(6 + j, i * RING + (6 + j), i)
                load_mod(START_HALVES + 1, i)
            with sp.Fori(0, 4) as i:
                for j in range(RING):
                    load(33 + j, i * RING + j, i)
                load_mod(14, i)
            with sp.Fori(0, 7) as i:
                for j in range(RING):
                    load(45 + j, i * RING + (12 + j), i)
            with sp.Fori(0, 5) as i:
                for j in range(RING):
                    load(66 + j, i * RING + (33 + j), i)
            sp.wait_ge(p_hi_done, 1)
            sp.wait_ge(p_lo_done, 1)
            load_mod(HALVES)
            for n in range(81, 84):
                load(n, n - 33)
            with sp.Fori(0, 17) as i:
                for j in range(RING):
                    load(84 + j, i * RING + (51 + j), i)
                load_mod(HALVES + 1, i)
            with sp.Fori(0, 20) as i:
                for j in range(RING):
                    load(135 + j, i * RING + (102 + j), i)
            for n in (195, 196):
                load(n, n - 33)
            for j in range(KT // 2):
                sp.wait_ge(t_done, 8 * KT + 2 * j + 2)
                sp.dma_start(out[:, 2 * j:2 * j + 2, :], scratch[:, 2 * j:2 * j + 2, :]).then_inc(stored, 16)
            sp.wait_ge(stored, 16 * (KT // 2))

        @block.scalar
        def _(act):
            def split_hi(n, i=0):
                slot, uses = ring(n, i)
                if n >= RING:
                    act.wait_ge(multiplied, i * RING + (n - RING + 1))
                act.wait_ge(raw_arrived[slot], uses * 16)
                act.activation(w_hi[:, slot, :], raw[:, slot, :], ACT.Copy).then_inc(hi_ready, 1)

            def square_stream(e):
                who = JOINS[e][0]
                if e < 2:
                    act.wait_ge((inputs_in, context_in)[e], 16)
                if e > 0:
                    act.wait_ge(u_lo_done, KT * e)
                for j in range(KT // 2):
                    if e >= 2:
                        act.wait_ge(resid_done, (e - 2) * 4 + j + 1)
                    act.activation(scratch[:, 2 * j:2 * j + 2, :], resid[:, who, 2 * j:2 * j + 2, :],
                                   ACT.Square).then_inc(sq_done, 1)

            def normalise_hi(e):
                who, _, norm = JOINS[e]
                act.wait_ge(ssq_done, e + 1)
                if e > 0:
                    act.wait_ge(rstd_done, e)
                act.activation(std[:, :], psum[:, SSQ, 0:T], ACT.Sqrt, bias=eps[:, :],
                               scale=1.0 / D).then_inc(std_done, 1)
                if norm is None:
                    return
                for j in range(KT):
                    act.wait_ge(t_done, KT * e + j + 1)
                    act.activation(u_hi[:, j, who * T:who * T + T], scratch[:, j, :], ACT.Identity,
                                   bias=shift(*norm, who, j)).then_inc(u_hi_done, 1)

            def silu_gate(k):
                act.activation(silu[:, :], psum[:, GATE, :], ACT.Silu).then_inc(silu_done, 1)

            def hidden_hi(k):
                act.wait_ge(prod_done, k + 1)
                act.activation(hid_hi[:, :], prod[:, :], ACT.Copy).then_inc(hid_hi_done, 1)

            def ffn(p, inner=None):
                b = PASS[p]
                act.wait_ge(multiplied, b + 1)
                if p > 0:
                    act.wait_ge(prod_done, STEPS * p)
                silu_gate(STEPS * p)
                split_hi(b + 3)
                split_hi(b + 4)
                hidden_hi(STEPS * p)
                if inner is not None:
                    square_stream(inner) if inner == 1 else None
                    normalise_hi(inner)
                with act.Fori(0, STEPS - 1) as i:
                    act.wait_ge(multiplied, i * RING + (b + 3))
                    silu_gate(None)
                    split_hi(b + 5, i)
                    split_hi(b + 6, i)
                    hidden_hi(i + (STEPS * p + 1))
                    split_hi(b + 7, i)

            act.wait_ge(params_in, 32)
            act.activation(cond[:, :, :], col("cond", 0, 2 * KT).rearrange("p (k c) -> p k c", c=2),
                           ACT.Silu).then_inc(cond_ready, 1)
            act.wait_ge(consts_set, 3)
            square_stream(0)
            for n in range(RING):
                split_hi(n)
            normalise_hi(0)
            ffn(0, inner=1)
            square_stream(2)
            split_hi(PASS[1] + 2)
            ffn(1, inner=2)

            square_stream(3)
            split_hi(MIX + 2)
            for i in range(2):
                act.wait_ge(multiplied, MIX + i + 1)
                act.wait_ge(pad_zeroed, 1)
                act.activation(pad_x[:, 2 * i:2 * i + 2, PAD:PAD + T],
                               psum[:, 4 + i, :].rearrange("p (a t) -> p a t", a=2), ACT.Copy).then_inc(pool_copied, 1)
                split_hi(MIX + 3 + i)
            normalise_hi(3)
            act.wait_ge(multiplied, MIX + 3)
            for i, bank in enumerate((6, 0)):
                act.activation(ckv[:, i, :], psum[:, bank, :], ACT.Copy).then_inc(act_step, 1)
                act.activation(ckv_sq[:, i, :], psum[:, bank, :], ACT.Square).then_inc(kv_sq_done, 1)
            split_hi(MIX + 5)
            split_hi(MIX + 6)
            act.wait_ge(kv_ssq_done, 1)
            act.wait_ge(u_lo_done, 4 * KT)
            act.activation(kv_std[:, :], psum[:, 5, :], ACT.Sqrt, bias=eps[:, :],
                           scale=1.0 / (KVR * P)).then_inc(kv_std_done, 1)
            for i in range(KVR):
                act.wait_ge(kv_t_done, i + 1)
                act.activation(kvn_hi[:, i, :], ckv_sq[:, i, :], ACT.Copy).then_inc(kv_hi_done, 1)
            for i in range(QR // 2):
                act.wait_ge(multiplied, MIX + 5 + i)
                view = psum[:, (2, 3, 4)[i], :].rearrange("p (a t) -> p a t", a=2)
                act.activation(cq[:, 2 * i:2 * i + 2, :], view, ACT.Copy).then_inc(act_step, 1)
                act.activation(cq_sq[:, 2 * i:2 * i + 2, :], view, ACT.Square).then_inc(q_sq_done, 1)
                split_hi(MIX + 7 + i)
                if i == 1:
                    act.wait_ge(kr_done, 1)
                    act.wait_ge(kv_lo_done, KVR)
                    for a in range(2):
                        act.activation(k_hi[NOPE:NOPE + ROPE, a, :], kr_f[NOPE:NOPE + ROPE, :],
                                       ACT.Copy).then_inc(kr_hi_done, 1)
            act.wait_ge(q_ssq_done, 1)
            act.activation(std[:, :], psum[:, 6, 0:T], ACT.Sqrt, bias=eps[:, :],
                           scale=1.0 / (QR * P)).then_inc(q_std_done, 1)
            for i in range(QR):
                act.wait_ge(q_t_done, i + 1)
                act.activation(qn_hi[:, i, :], cq_sq[:, i, :], ACT.Copy).then_inc(qn_hi_done, 1)
            act.wait_ge(pooled, 1)
            act.activation(p_hi[:, :, :], win2[:, :, PAD:PAD + T], ACT.Copy).then_inc(p_hi_done, 1)

            for r in range(PAIRS):
                act.wait_ge(q_proj, r + 1)
                if r > 0:
                    act.wait_ge(q_lo_done, r)
                act.activation(q_f[0:NOPE, :], psum[0:NOPE, 0, :], ACT.Copy).then_inc(q_nope, 1)
                for a in range(2):
                    act.wait_ge(k_proj, 2 * r + a + 1)
                    act.activation(k_hi[0:NOPE, a, :], psum[0:NOPE, 1 + a, :], ACT.Copy).then_inc(k_hi_done, 1)
                act.wait_ge(q_nope, r + 1)
                act.wait_ge(q_roped, r + 1)
                act.activation(q_hi[0:NOPE + ROPE, :], q_f[0:NOPE + ROPE, :], ACT.Copy).then_inc(q_hi_done, 1)
                act.wait_ge(multiplied, MIX + 8 + r)
                act.wait_ge(kr_lo_done, 2)
                act.activation(v_hi[:, :], psum[:, 3, :], ACT.Copy).then_inc(v_hi_done, 1)
                for a in range(2):
                    for qt in range(2):
                        n = 4 * r + 2 * a + qt
                        act.wait_ge(neg_max, n + 1)
                        if n >= 2:
                            act.wait_ge(p_turned, 2 * (n // 2))
                        act.activation(probs[:, qt, :], psum[:, 4 + 2 * a + qt, :], ACT.Exp,
                                       bias=stat[:, 0, n:n + 1], scale=ATTN_SCALE,
                                       accum_out=stat[:, 1, n:n + 1]).then_inc(exp_done, 1)
                    if a == 1:
                        turned_hi(act, r, 0)
                turned_hi(act, r, 1)
                act.wait_ge(pv_done, r + 1)
                for a in range(2):
                    act.activation(mix_hi[a * VD:a * VD + VD, 4 + r, :], psum[a * VD:a * VD + VD, 4, a * T:a * T + T],
                                   ACT.Copy).then_inc(attn_hi_done, 1)
                split_hi(MIX + 10 + r)

            act.wait_ge(multiplied, MIX + 12)
            for g in range(4):
                act.activation(mix_hi[:, g, :], psum[:, 5 + g // 2, (g % 2) * T:(g % 2) * T + T], ACT.Identity,
                               scale=col("pool_scale", g)).then_inc(pool_hi_done, 1)
            for n in range(MIX + 14, MIX + 18):
                split_hi(n)
            square_stream(4)
            split_hi(PASS[2] + 2)
            normalise_hi(4)
            ffn(2)
            square_stream(5)
            normalise_hi(5)
            split_hi(PASS[3] + 2)
            ffn(3)
            square_stream(6)
            normalise_hi(6)
            split_hi(CONV + 2)

            with act.Fori(0, KT // 2) as i:
                act.wait_ge(multiplied, i * RING + (CONV + 1))
                act.activation(silu[:, :], psum[:, GATE, :], ACT.Copy).then_inc(c_copied, 1)
                split_hi(CONV + 3, i)
                split_hi(CONV + 4, i)
                split_hi(CONV + 5, i)
                act.wait_ge(conv_done, i + 1)
                act.activation(mix_hi[:, bass.ds(i * 2, 2), :], prod[:, :].rearrange("p (a t) -> p a t", a=2),
                               ACT.Copy).then_inc(conv_hi_done, 1)
            for n in range(CONV + 15, CONV + 18):
                split_hi(n)
            square_stream(7)
            split_hi(PASS[4] + 2)
            normalise_hi(7)
            ffn_last = PASS[4]
            act.wait_ge(multiplied, ffn_last + 1)
            silu_gate(None)
            split_hi(ffn_last + 3)
            split_hi(ffn_last + 4)
            hidden_hi(STEPS * 4)
            with act.Fori(0, STEPS - 2) as i:
                act.wait_ge(multiplied, i * RING + (ffn_last + 3))
                silu_gate(None)
                split_hi(ffn_last + 5, i)
                split_hi(ffn_last + 6, i)
                hidden_hi(i + (STEPS * 4 + 1))
                split_hi(ffn_last + 7, i)
            act.wait_ge(multiplied, ffn_last + 30)
            silu_gate(None)
            split_hi(ffn_last + 32)
            hidden_hi(STEPS * 5 - 1)
            square_stream(8)
            normalise_hi(8)

        @block.vector
        def _(dve):
            steps = [0]

            def settle(ins):
                steps[0] += 1
                ins.then_inc(dve_step, 1)
                dve.wait_ge(dve_step, steps[0])

            def split_lo(n, i=0):
                slot, uses = ring(n, i)
                dve.wait_ge(hi_ready, i * RING + (n + 1))
                dve.tensor_tensor(w_lo[:, slot, :], raw[:, slot, :], w_hi[:, slot, :].bitcast(f32),
                                  SUB).then_inc(lo_ready[slot], 1)

            def gather(e):
                who, (layer, kind, factor), _ = JOINS[e]
                gate = coef[:, 2, :]
                source, first_chunk = {2: (0, PASS[0] + 32), 3: (1, PASS[1] + 32), 4: (-1, MIX + 12), 5: (2, PASS[2] + 32),
                                       6: (3, PASS[3] + 32), 7: (-1, CONV + 12), 8: (4, PASS[4] + 32)}[e]
                settle(dve.tensor_scalar(gate, shift(layer, kind, who, 0, KT, 2), factor, None, MUL))
                for j in range(KT // 2):
                    if source < 0:
                        dve.wait_ge(multiplied, first_chunk + j + 1)
                    elif j < 3:
                        dve.wait_ge(acc_ready, 3 * source + j + 1)
                    else:
                        dve.wait_ge(multiplied, first_chunk + 1)
                    for a in range(2):
                        k = 2 * j + a
                        last = dve.scalar_tensor_tensor(resid[:, who, k, :], psum[:, j, a * T:a * T + T],
                                                        gate[:, k:k + 1], resid[:, who, k, :], MUL, ADD)
                    last.then_inc(resid_done, 1)

            def normalise(e):
                who, _, norm = JOINS[e]
                dve.wait_ge(resid_done, 4 * (e - 1)) if e >= 2 else None
                if norm is not None:
                    layer, kind = norm
                    gain = coef[:, 3, :]
                    settle(dve.scalar_tensor_tensor(gain, shift(layer, kind, who, 0, KT, 1), 1.0,
                                                    col("norm_g", (layer * 3 + kind) * KT, KT), ADD, MUL))
                else:
                    gain = col("final_norm_g", 0, KT)
                dve.wait_ge(std_done, e + 1)
                dve.reciprocal(rstd[:, :], std[:, :]).then_inc(rstd_done, 1)
                dve.wait_ge(rstd_done, e + 1)

                def scaled(j):
                    dve.scalar_tensor_tensor(scratch[:, j, :], resid[:, who, j, :], gain[:, j:j + 1],
                                             rstd[:, :], MUL, MUL).then_inc(t_done, 1)

                scaled(0)
                for j in range(KT):
                    if j + 1 < KT:
                        scaled(j + 1)
                    if norm is None:
                        continue
                    dve.wait_ge(u_hi_done, KT * e + j + 1)
                    at = slice(who * T, who * T + T)
                    dve.scalar_tensor_tensor(u_lo[:, j, at], scratch[:, j, :], shift(*norm, who, j),
                                             u_hi[:, j, at].bitcast(f32), ADD, SUB).then_inc(u_lo_done, 1)

            def write_mod(done, half, conds, i=0):
                dve.wait_ge(mod_reduced, done)
                dst = mod_out[:, bass.ds((i + half) * 4, 4), 0:conds]
                src = psum[:, MODB, 0:8].rearrange("p (k c) -> p k c", c=2)[:, :, 0:conds]
                for c in range(conds):
                    last = dve.tensor_tensor(dst[:, :, c], src[:, :, c],
                                             par[:, bass.ds((i + half) * 4 + PARAM["b_mod"], 4)], ADD)
                last.then_inc(mod_written, 1)

            def sum_mod(half, conds, i=0):
                base = mod_steps_before(half)
                for kt in range(KT):
                    kh, k = kt // 4, kt % 4
                    if k == 0:
                        dve.wait_ge(mod_arrived[kh], (i + (half + 1)) * 16)
                    for c in range(conds):
                        at = base + kt * conds + c
                        w = mod_raw[:, kh, k, :]
                        if kt == 0:
                            ins = dve.tensor_scalar(mod_acc[:, c, :], w, cond[:, kt, c:c + 1], None, MUL)
                        else:
                            dve.wait_ge(mod_step, i * (KT * conds) + (at - conds + 1))
                            ins = dve.scalar_tensor_tensor(mod_acc[:, c, :], w, cond[:, kt, c:c + 1],
                                                           mod_acc[:, c, :], MUL, ADD)
                        ins.then_inc(mod_step, 1)

            def hidden_product(k):
                dve.wait_ge(silu_done, k + 1)
                dve.tensor_tensor(prod[:, :], silu[:, :], psum[:, UP, :], MUL).then_inc(prod_done, 1)

            def hidden_low(k):
                dve.wait_ge(hid_hi_done, k + 1)
                dve.tensor_tensor(hid_lo[:, :], prod[:, :], hid_hi[:, :].bitcast(f32), SUB).then_inc(hid_lo_done, 1)

            def ffn_steps(p, first, count, mod=None):
                b = PASS[p] + 2 + 3 * (first - 1)
                with dve.Fori(0, count) as i:
                    if mod is not None:
                        half, conds, done = mod
                        write_mod(i + done, half - 1, conds, i)
                        dve.wait_ge(mod_written, i + (done + 1))
                        sum_mod(half, conds, i)
                    for j in (3, 4):
                        if (b + j) % RING == 1:
                            split_lo(b + j, i)
                    dve.wait_ge(multiplied, i * RING + (b + 3))
                    hidden_product(i + (STEPS * p + first))
                    hidden_low(i + (STEPS * p + first))
                    if (b + 5) % RING == 1:
                        split_lo(b + 5, i)

            dve.memset(ones[:, :], 1.0).then_inc(consts_set, 1)
            dve.memset(zeros[:, :].bitcast(f32), 0.0).then_inc(consts_set, 1)
            dve.memset(eps[:, :], EPS).then_inc(consts_set, 1)
            dve.wait_ge(params_in, 32)
            dve.wait_ge(mod_used[1], START_HALVES)
            for c in range(2):
                last = dve.tensor_tensor(mod_out[:, 0:4 * START_HALVES, c],
                                         psum[:, MODB, 0:8 * START_HALVES].rearrange("p (k c) -> p k c", c=2)[:, :, c],
                                         col("b_mod", 0, 4 * START_HALVES), ADD)
            last.then_inc(mod_written, 1)
            dve.wait_ge(mod_written, 1)
            normalise(0)

            dve.wait_ge(cond_ready, 1)
            sum_mod(4, 2)
            dve.wait_ge(multiplied, PASS[0] + 2)
            hidden_product(0)
            hidden_low(0)
            normalise(1)
            ffn_steps(0, 1, STEPS - 1, mod=(5, 2, 1))
            write_mod(11, 14, 2)
            dve.wait_ge(mod_written, 12)
            gather(2)

            dve.wait_ge(multiplied, PASS[1] + 2)
            hidden_product(STEPS)
            hidden_low(STEPS)
            normalise(2)
            sum_mod(15, 2)
            split_step(dve, split_lo, hidden_product, hidden_low, PASS[1] + 2, STEPS + 1)
            ffn_steps(1, 2, 2, mod=(16, 2, 12))
            write_mod(14, 17, 2)
            dve.wait_ge(mod_written, 15)
            ffn_steps(1, 4, STEPS - 4)
            gather(3)

            normalise(3)
            dve.wait_ge(u_lo_done, 4 * KT)
            dve.wait_ge(multiplied, MIX + 4)
            rope_rows, swap_rows = slice(NOPE, NOPE + ROPE), slice(NOPE + ROPE, P)
            dve.tensor_tensor(rope_a[rope_rows, 0:T], psum[rope_rows, 1, 0:T], con[rope_rows, P:P + T],
                              MUL).then_inc(dve_step, 1)
            dve.tensor_tensor(rope_b[rope_rows, 0:T], psum[swap_rows, 1, 0:T], con[swap_rows, P:P + T],
                              MUL).then_inc(dve_step, 1)
            steps[0] += 2
            dve.wait_ge(dve_step, steps[0])
            dve.tensor_tensor(kr_f[rope_rows, 0:T], rope_a[rope_rows, 0:T], rope_b[rope_rows, 0:T], ADD)
            dve.tensor_copy(kr_f[rope_rows, T:2 * T], psum[rope_rows, 1, T:2 * T]).then_inc(kr_done, 1)
            dve.wait_ge(kv_std_done, 1)
            settle(dve.reciprocal(kv_rstd[:, :], kv_std[:, :]))
            for i in range(KVR):
                dve.scalar_tensor_tensor(ckv_sq[:, i, :], ckv[:, i, :], col("kv_norm_g", i), kv_rstd[:, :],
                                         MUL, MUL).then_inc(kv_t_done, 1)
            for i in range(KVR):
                dve.wait_ge(kv_hi_done, i + 1)
                dve.tensor_tensor(kvn_lo[:, i, :], ckv_sq[:, i, :], kvn_hi[:, i, :].bitcast(f32),
                                  SUB).then_inc(kv_lo_done, 1)
            for a in range(2):
                dve.wait_ge(kr_hi_done, a + 1)
                dve.tensor_tensor(k_lo[rope_rows, a, :], kr_f[rope_rows, :], k_hi[rope_rows, a, :].bitcast(f32),
                                  SUB).then_inc(kr_lo_done, 1)
            dve.wait_ge(q_std_done, 1)
            settle(dve.reciprocal(rstd[:, :], std[:, :]))
            for i in range(QR):
                dve.scalar_tensor_tensor(cq_sq[:, i, :], cq[:, i, :], col("q_norm_g", i), rstd[:, :],
                                         MUL, MUL).then_inc(q_t_done, 1)
            for i in range(QR):
                dve.wait_ge(qn_hi_done, i + 1)
                dve.tensor_tensor(qn_lo[:, i, :], cq_sq[:, i, :], qn_hi[:, i, :].bitcast(f32),
                                  SUB).then_inc(qn_lo_done, 1)

            for r in range(PAIRS):
                dve.wait_ge(q_proj, r + 1)
                dve.tensor_tensor(rope_a[rope_rows, :], psum[rope_rows, 0, :], con[rope_rows, P:P + 2 * T],
                                  MUL).then_inc(dve_step, 1)
                dve.tensor_tensor(rope_b[rope_rows, :], psum[swap_rows, 0, :], con[swap_rows, P:P + 2 * T],
                                  MUL).then_inc(dve_step, 1)
                steps[0] += 2
                dve.wait_ge(dve_step, steps[0])
                dve.tensor_tensor(q_f[rope_rows, :], rope_a[rope_rows, :], rope_b[rope_rows, :],
                                  ADD).then_inc(q_roped, 1)
                for a in range(2):
                    dve.wait_ge(k_hi_done, 2 * r + a + 1)
                    dve.tensor_tensor(k_lo[0:NOPE, a, :], psum[0:NOPE, 1 + a, :], k_hi[0:NOPE, a, :].bitcast(f32),
                                      SUB).then_inc(k_lo_done, 1)
                dve.wait_ge(q_hi_done, r + 1)
                dve.tensor_tensor(q_lo[0:NOPE + ROPE, :], q_f[0:NOPE + ROPE, :], q_hi[0:NOPE + ROPE, :].bitcast(f32),
                                  SUB).then_inc(q_lo_done, 1)
                dve.wait_ge(v_hi_done, r + 1)
                dve.tensor_tensor(v_lo[:, :], psum[:, 3, :], v_hi[:, :].bitcast(f32), SUB).then_inc(v_lo_done, 1)
                for n in range(4 * r, 4 * r + 4):
                    dve.wait_ge(scored, n + 1)
                    settle(dve.reduce_max(stat[:, 2, n:n + 1], psum[:, 4 + n % 4, :], AX.X))
                    dve.tensor_scalar(stat[:, 0, n:n + 1], stat[:, 2, n:n + 1], -ATTN_SCALE, None,
                                      MUL).then_inc(neg_max, 1)
                for a in range(2):
                    for qt in range(2):
                        n = 4 * r + 2 * a + qt
                        dve.wait_ge(exp_done, n + 1)
                        settle(dve.reciprocal(stat[:, 3, n:n + 1], stat[:, 1, n:n + 1]))
                        dve.tensor_scalar(probs[:, qt, :], probs[:, qt, :], stat[:, 3, n:n + 1], None,
                                          MUL).then_inc(p_normal, 1)
                    if a == 1:
                        turned_lo(dve, r, 0)
                turned_lo(dve, r, 1)
                dve.wait_ge(attn_hi_done, 2 * r + 2)
                for a in range(2):
                    rows = slice(a * VD, a * VD + VD)
                    last = dve.tensor_tensor(mix_lo[rows, 4 + r, :], psum[rows, 4, a * T:a * T + T],
                                             mix_hi[rows, 4 + r, :].bitcast(f32), SUB)
                last.then_inc(attn_lo_done, 1)
            for g in range(4):
                dve.wait_ge(pool_hi_done, 4)
                dve.scalar_tensor_tensor(mix_lo[:, g, :], psum[:, 5 + g // 2, (g % 2) * T:(g % 2) * T + T],
                                         col("pool_scale", g), mix_hi[:, g, :].bitcast(f32), MUL,
                                         SUB).then_inc(pool_lo_done, 1)
            gather(4)
            normalise(4)

            sum_mod(18, 1)
            dve.wait_ge(multiplied, PASS[2] + 2)
            hidden_product(2 * STEPS)
            hidden_low(2 * STEPS)
            ffn_steps(2, 1, STEPS - 1, mod=(19, 1, 15))
            write_mod(25, 28, 1)
            dve.wait_ge(mod_written, 26)
            gather(5)
            normalise(5)
            dve.wait_ge(multiplied, PASS[3] + 2)
            hidden_product(3 * STEPS)
            hidden_low(3 * STEPS)
            sum_mod(29, 1)
            split_step(dve, split_lo, hidden_product, hidden_low, PASS[3] + 2, 3 * STEPS + 1)
            ffn_steps(3, 2, 6, mod=(30, 1, 26))
            write_mod(32, 35, 1)
            dve.wait_ge(mod_written, 33)
            ffn_steps(3, 8, STEPS - 8)
            gather(6)
            normalise(6)

            dve.wait_ge(u_lo_done, 7 * KT)
            settle(dve.memset(z_pad[:, :, :], 0.0))
            with dve.Fori(0, KT // 2) as i:
                dve.wait_ge(c_copied, i + 1)
                dve.wait_ge(multiplied, i * RING + (CONV + 2))
                dve.tensor_tensor(z_pad[:, :, 1:1 + T], silu[:, :].rearrange("p (a t) -> p a t", a=2),
                                  psum[:, UP, :].rearrange("p (a t) -> p a t", a=2), MUL).then_inc(z_done, 1)
                dve.wait_ge(z_done, i + 1)

                def tap(a, d):
                    return par[:, bass.ds(i * 6 + (PARAM["conv_w"] + 3 * a + d), 1)]

                for a in range(2):
                    dve.tensor_scalar(conv_1[:, a, :], z_pad[:, a, 0:T], tap(a, 0), None, MUL).then_inc(mod_step, 1)
                base = mod_steps_before(2 * HALVES)
                for d, src, dst in ((1, conv_1, conv_2), (2, conv_2, conv_1)):
                    for a in range(2):
                        dve.wait_ge(mod_step, i * 6 + (base + 2 * d - 1 + a))
                        dve.scalar_tensor_tensor(dst[:, a, :], z_pad[:, a, d:d + T], tap(a, d), src[:, a, :],
                                                 MUL, ADD).then_inc(mod_step, 1)
                dve.wait_ge(mod_step, i * 6 + (base + 6))
                dve.wait_ge(multiplied, i * RING + (CONV + 3))
                dve.tensor_tensor(prod[:, :].rearrange("p (a t) -> p a t", a=2), conv_1[:, :, :],
                                  psum[:, 6, :].rearrange("p (a t) -> p a t", a=2), MUL).then_inc(conv_done, 1)
                dve.wait_ge(conv_hi_done, i + 1)
                at = bass.ds(i * 2, 2)
                dve.tensor_tensor(mix_lo[:, at, :], prod[:, :].rearrange("p (a t) -> p a t", a=2),
                                  mix_hi[:, at, :].bitcast(f32), SUB).then_inc(conv_lo_done, 1)
            gather(7)
            normalise(7)

            dve.wait_ge(multiplied, PASS[4] + 2)
            hidden_product(4 * STEPS)
            hidden_low(4 * STEPS)
            b = PASS[4]
            with dve.Fori(0, STEPS - 2) as i:
                for j in (5, 6):
                    if (b + j) % RING == 1:
                        split_lo(b + j, i)
                dve.wait_ge(multiplied, i * RING + (b + 5))
                hidden_product(i + (STEPS * 4 + 1))
                hidden_low(i + (STEPS * 4 + 1))
                if (b + 7) % RING == 1:
                    split_lo(b + 7, i)
            if (b + 32) % RING == 1:
                split_lo(b + 32)
            dve.wait_ge(multiplied, b + 32)
            hidden_product(STEPS * 5 - 1)
            hidden_low(STEPS * 5 - 1)
            gather(8)
            normalise(8)

        @block.gpsimd
        def _(pool):
            steps = [0]

            def settle(ins):
                steps[0] += 1
                ins.then_inc(pool_step, 1)
                pool.wait_ge(pool_step, steps[0])

            def split_lo(n, i=0):
                slot, uses = ring(n, i)
                pool.wait_ge(hi_ready, i * RING + (n + 1))
                pool.tensor_tensor(w_lo[:, slot, :], raw[:, slot, :], w_hi[:, slot, :].bitcast(f32),
                                   SUB).then_inc(lo_ready[slot], 1)

            def pass_lo(p, bodies=STEPS - 1):
                split_lo(PASS[p] + 3)
                split_lo(PASS[p] + 4)
                with pool.Fori(0, bodies) as i:
                    for n in range(PASS[p] + 5, PASS[p] + 8):
                        if n % RING != 1:
                            split_lo(n, i)

            for n in range(RING):
                split_lo(n)
            pass_lo(0)
            split_lo(PASS[1] + 2)
            pass_lo(1)
            pool.wait_ge(mod_step, mod_steps_before(HALVES))
            pool.memset(pad_x[:, :, :], 0.0).then_inc(pad_zeroed, 1)
            for n in range(MIX + 2, MIX + 7):
                split_lo(n)
            pool.wait_ge(pool_copied, 2)
            settle(pool.tensor_tensor(win2[:, :, 1:PW], pad_x[:, :, 0:PW - 1], pad_x[:, :, 1:PW], ADD))
            settle(pool.tensor_tensor(win4[:, :, 2:PW - 1], win2[:, 1:4, 1:PW - 2], win2[:, 1:4, 3:PW], ADD))
            settle(pool.tensor_tensor(win8[:, :, 4:PW - 3], win4[:, 1:3, 2:PW - 5], win4[:, 1:3, 6:PW - 1], ADD))
            settle(pool.tensor_tensor(win16[:, :, 8:PW - 7], win8[:, 1:2, 4:PW - 11], win8[:, 1:2, 12:PW - 3], ADD))
            pool.wait_ge(inv_in, 16)
            inner = slice(PAD, PAD + T)
            for g, w in enumerate((win2[:, 0, :], win4[:, 0, :], win8[:, 0, :], win16[:, 0, :])):
                last = pool.tensor_tensor(win2[:, g, inner], w[:, inner], inv_cnt[:, g, :], MUL)
            settle(last)
            pool.tensor_tensor(win2[:, :, inner], win2[:, :, inner], pad_x[:, :, inner], SUB).then_inc(pooled, 1)
            for n in range(MIX + 7, MIX + 10):
                split_lo(n)
            pool.wait_ge(p_hi_done, 1)
            pool.tensor_tensor(p_lo[:, :, :], win2[:, :, inner], p_hi[:, :, :].bitcast(f32), SUB).then_inc(p_lo_done, 1)
            for n in range(MIX + 10, MIX + 19):
                split_lo(n)
            pass_lo(2)
            split_lo(PASS[3] + 2)
            pass_lo(3)
            for n in range(CONV + 2, CONV + 6):
                split_lo(n)
            with pool.Fori(0, 3) as i:
                for j in range(RING):
                    split_lo(CONV + 6 + j, i)
            for n in range(CONV + 15, CONV + 19):
                split_lo(n)
            pass_lo(4, STEPS - 2)
            if (PASS[4] + 32) % RING != 1:
                split_lo(PASS[4] + 32)

        @block.tensor
        def _(pe):
            def three(out, w_at, x_at, first, last, shared=False, start=None):
                begin = first if start is None else start
                pe.matmul(out, w_at[0], x_at[0], start=begin, stop=False, skip_group_check=shared)
                pe.matmul(out, w_at[0], x_at[1], start=False, stop=False, skip_group_check=shared)
                return pe.matmul(out, w_at[1], x_at[0], start=False, stop=last, skip_group_check=shared)

            def weights(slot, at):
                return w_hi[:, slot, at:at + P], w_lo[:, slot, at:at + P]

            def arrived(n, i=0):
                slot, uses = ring(n, i)
                pe.wait_ge(lo_ready[slot], uses)
                return slot

            def stream_in(k, who, width=T):
                at = slice(who * T, who * T + width)
                return u_hi[:, k, at], u_lo[:, k, at]

            def project(n, bank, who, i=0, fresh=None):
                slot = arrived(n, i)
                if fresh is None:
                    for a in range(2):
                        for k in range(KT):
                            last = three(psum[:, bank, a * T:a * T + T], weights(slot, k * 256 + a * P),
                                         stream_in(k, who), k == 0, k == KT - 1)
                else:
                    for k in range(KT):
                        pe.wait_ge(u_lo_done, KT * fresh + k + 1)
                        for a in range(2):
                            last = three(psum[:, bank, a * T:a * T + T], weights(slot, k * 256 + a * P),
                                         stream_in(k, who), k == 0, k == KT - 1, True, k == 0 and a == 0)
                last.then_inc(multiplied, 1)

            def down(n, i=0, signal=False):
                slot = arrived(n, i)
                for j in range(KT):
                    for a in range(2):
                        last = three(psum[:, j // 2, (j % 2) * T:(j % 2) * T + T], weights(slot, a * D + j * P),
                                     (hid_hi[:, a * T:a * T + T], hid_lo[:, a * T:a * T + T]),
                                     False, signal and a == 1, True)
                    if signal and j % 2 == 1 and j < KT - 1:
                        last.then_inc(acc_ready, 1)
                last.then_inc(multiplied, 1)

            def clear_acc():
                for j in range(4):
                    for a in range(2):
                        pe.matmul(psum[:, j, a * T:a * T + T], zeros[:, 0:P], zeros[:, :], start=a == 0, stop=False,
                                  skip_group_check=True)

            def sum_squares(e):
                for j in range(KT):
                    if j % 2 == 0:
                        pe.wait_ge(sq_done, 4 * e + j // 2 + 1)
                    last = pe.matmul(psum[:, SSQ, 0:T], ones[:, :], scratch[:, j, :], start=j == 0, stop=j == KT - 1)
                last.then_inc(ssq_done, 1)

            def reduce_mod(half, conds, i=0):
                pe.wait_ge(mod_step, i * mod_ops(half) + mod_steps_before(half + 1))
                for k in range(4):
                    for c in range(conds):
                        last = pe.matmul(psum[:, MODB, 2 * k + c:2 * k + c + 1], mod_acc[:, c, k * P:k * P + P],
                                         ones[:, 0:1], start=True, stop=True)
                last.then_inc(mod_reduced, 1)

            def ffn_step0(p, who, fresh=None):
                b = PASS[p]
                project(b, GATE, who, fresh=fresh)
                project(b + 1, UP, who)

            def ffn_steps(p, who, first, count, mod=None):
                b = PASS[p] + 2 + 3 * (first - 1)
                with pe.Fori(0, count) as i:
                    pe.wait_ge(silu_done, i + (STEPS * p + first))
                    project(b, GATE, who, i)
                    pe.wait_ge(hid_lo_done, i + (STEPS * p + first))
                    down(b + 1, i)
                    project(b + 2, UP, who, i)
                    if mod is not None:
                        reduce_mod(mod[0], mod[1], i)

            def ffn_end(p, e):
                pe.wait_ge(hid_lo_done, STEPS * (p + 1))
                down(PASS[p] + FFN_CHUNKS - 1, signal=True)

            pe.wait_ge(consts_set, 3)
            pe.wait_ge(cond_ready, 1)
            for half in range(START_HALVES):
                for kh in range(2):
                    pe.wait_ge(mod_arrived[kh], 16 * (half + 1))
                    for k in range(4):
                        for c4 in range(4):
                            at = half * 8 + 2 * c4
                            last = pe.matmul(psum[:, MODB, at:at + 2], mod_raw[:, kh, k, c4 * P:c4 * P + P],
                                             cond[:, kh * 4 + k, :], start=half == 0 and kh == 0 and k == 0 and c4 == 0,
                                             stop=kh == 1 and k == 3, skip_group_check=True)
                    last.then_inc(mod_used[kh], 1)
                if half == 0:
                    sum_squares(0)

            ffn_step0(0, 0, fresh=0)
            sum_squares(1)
            clear_acc()
            reduce_mod(4, 2)
            ffn_steps(0, 0, 1, STEPS - 1, mod=(5, 2))
            ffn_end(0, 2)
            pe.wait_ge(u_lo_done, 2 * KT)
            ffn_step0(1, 1)
            sum_squares(2)
            clear_acc()
            ffn_steps(1, 1, 1, 3, mod=(15, 2))
            ffn_steps(1, 1, 4, STEPS - 4)
            ffn_end(1, 3)

            pe.wait_ge(u_lo_done, 3 * KT)
            project(MIX, 4, 0)
            project(MIX + 1, 5, 0)
            sum_squares(3)
            pe.wait_ge(u_lo_done, 4 * KT)
            slot = arrived(MIX + 2)
            for a, bank in enumerate((6, 0)):
                for k in range(KT):
                    last = three(psum[:, bank, :], weights(slot, k * 256 + a * P), stream_in(k, 0, 2 * T),
                                 k == 0, k == KT - 1)
            last.then_inc(multiplied, 1)
            slot = arrived(MIX + 3)
            for k in range(KT):
                last = three(psum[:, 1, :], weights(slot, k * P), stream_in(k, 0, 2 * T), k == 0, k == KT - 1)
            last.then_inc(multiplied, 1)
            pe.wait_ge(pool_copied, 2)
            pe.wait_ge(kv_sq_done, 2)
            for i in range(KVR):
                last = pe.matmul(psum[:, 5, :], ones[:, :], ckv_sq[:, i, :], start=i == 0, stop=i == KVR - 1)
            last.then_inc(kv_ssq_done, 1)
            for i in range(QR // 2):
                project(MIX + 4 + i, (2, 3, 4)[i], 0)
            for i in range(QR):
                if i % 2 == 0:
                    pe.wait_ge(q_sq_done, i // 2 + 1)
                last = pe.matmul(psum[:, 6, 0:T], ones[:, :], cq_sq[:, i, :], start=i == 0, stop=i == QR - 1)
            last.then_inc(q_ssq_done, 1)
            pe.wait_ge(kv_lo_done, KVR)
            pe.wait_ge(kr_lo_done, 2)

            for r in range(PAIRS):
                slot = arrived(MIX + 7 + r)
                if r > 0:
                    pe.wait_ge(pt_lo_done, 4 * r)
                for a in range(2):
                    for k in range(QR):
                        if r == 0 and a == 0:
                            pe.wait_ge(qn_lo_done, k + 1)
                        last = three(psum[:, 0, a * T:a * T + T], weights(slot, k * 256 + a * P),
                                     (qn_hi[:, k, :], qn_lo[:, k, :]), k == 0, k == QR - 1)
                last.then_inc(q_proj, 1)
                kv_at = QR * 256
                for a in range(2):
                    for k in range(KVR):
                        last = three(psum[:, 1 + a, :], weights(slot, kv_at + k * 256 + a * P),
                                     (kvn_hi[:, k, :], kvn_lo[:, k, :]), k == 0, k == KVR - 1)
                    last.then_inc(k_proj, 1)
                for t in range(4):
                    for k in range(KVR):
                        at = kv_at + k * 256
                        cols = [w[:, slot, at:at + 256].rearrange("p (a d) -> p a d", a=2)[:, :, NOPE:NOPE + VD]
                                for w in (w_hi, w_lo)]
                        rows = [w[:, k, t * P:t * P + P] for w in (kvn_hi, kvn_lo)]
                        last = three(psum[:, 3, t * P:t * P + P].rearrange("p (a d) -> p a d", a=2), rows, cols,
                                     k == 0, k == KVR - 1)
                last.then_inc(multiplied, 1)
                pe.wait_ge(q_lo_done, r + 1)
                if r > 0:
                    pe.wait_ge(attn_lo_done, r)
                rows = slice(0, NOPE + ROPE)
                for a in range(2):
                    pe.wait_ge(k_lo_done, 2 * r + a + 1)
                    for qt in range(2):
                        at = slice(a * T + qt * P, a * T + qt * P + P)
                        last = three(psum[:, 4 + 2 * a + qt, :], (q_hi[rows, at], q_lo[rows, at]),
                                     (k_hi[rows, a, :], k_lo[rows, a, :]), True, True)
                        last.then_inc(scored, 1)
                pe.wait_ge(v_lo_done, r + 1)
                for a in range(2):
                    pe.wait_ge(p_normal, 4 * r + 2 * a + 2)
                    for b in range(2):
                        for kt in range(2):
                            for qt in range(2):
                                at = kt * T + qt * P
                                key = (2 * b + kt) * P
                                last = pe.transpose(psum[:, 2 * a + b, at:at + P], probs[:, qt, key:key + P], con[:, 0:P])
                        last.then_inc(p_turned, 1)
                for a in range(2):
                    for kt in range(4):
                        pe.wait_ge(pt_lo_done, 4 * r + 2 * a + kt // 2 + 1)
                        last = three(psum[:, 4, a * T:a * T + T],
                                     (v_hi[:, kt * P:kt * P + P], v_lo[:, kt * P:kt * P + P]),
                                     (pt_hi[:, a, kt, :], pt_lo[:, a, kt, :]), kt == 0, kt == 3)
                last.then_inc(pv_done, 1)

            slot = arrived(MIX + 11)
            pe.wait_ge(p_lo_done, 1)
            for g in range(4):
                last = three(psum[:, 5 + g // 2, (g % 2) * T:(g % 2) * T + T], weights(slot, g * P),
                             (p_hi[:, g, :], p_lo[:, g, :]), True, True)
            last.then_inc(multiplied, 1)

            def project_out(base, e, order):
                for i in range(4):
                    slot = arrived(base + i)
                    for a in range(2):
                        for k in order:
                            if e == 4 and i == 0 and a == 0 and k < 4:
                                pe.wait_ge(pool_lo_done, k + 1)
                            last = three(psum[:, i, a * T:a * T + T], weights(slot, k * 256 + a * P),
                                         (mix_hi[:, k, :], mix_lo[:, k, :]), k == order[0], k == order[-1])
                    last.then_inc(multiplied, 1)

            pe.wait_ge(pt_lo_done, 16)
            pe.wait_ge(attn_lo_done, 4)
            project_out(MIX + 12, 4, [4, 5, 6, 7, 0, 1, 2, 3])
            sum_squares(4)

            ffn_step0(2, 0, fresh=4)
            clear_acc()
            reduce_mod(18, 1)
            ffn_steps(2, 0, 1, STEPS - 1, mod=(19, 1))
            ffn_end(2, 5)
            sum_squares(5)
            ffn_step0(3, 0, fresh=5)
            clear_acc()
            ffn_steps(3, 0, 1, 7, mod=(29, 1))
            ffn_steps(3, 0, 8, STEPS - 8)
            ffn_end(3, 6)
            sum_squares(6)

            pe.wait_ge(u_lo_done, 7 * KT)
            for k, bank in enumerate((GATE, UP, 6)):
                project(CONV + k, bank, 0)
            with pe.Fori(0, KT // 2 - 1) as i:
                pe.wait_ge(c_copied, i + 1)
                project(CONV + 3, GATE, 0, i)
                pe.wait_ge(z_done, i + 1)
                project(CONV + 4, UP, 0, i)
                pe.wait_ge(conv_done, i + 1)
                project(CONV + 5, 6, 0, i)
            pe.wait_ge(conv_lo_done, KT // 2)
            project_out(CONV + 12, 7, list(range(KT)))
            sum_squares(7)
            ffn_step0(4, 0, fresh=7)
            clear_acc()
            ffn_steps(4, 0, 1, STEPS - 1)
            ffn_end(4, 8)
            sum_squares(8)


def _tiles(a):
    return a.reshape(a.shape[0] // P, P, a.shape[1]).transpose(1, 0, 2)


def _ffn_chunks(gate, up, down):
    gate, up, down = _tiles(gate), _tiles(up), _tiles(down)
    g = [gate[:, :, 256 * s:256 * s + 256].reshape(P, CH) for s in range(STEPS)]
    u = [up[:, :, 256 * s:256 * s + 256].reshape(P, CH) for s in range(STEPS)]
    d = [down[:, 2 * s:2 * s + 2, :].reshape(P, CH) for s in range(STEPS)]
    order = [g[0], u[0]]
    for s in range(1, STEPS):
        order += [g[s], d[s - 1], u[s]]
    return order + [d[-1]]


def _column_chunks(w):
    w = _tiles(w)
    return [np.ascontiguousarray(w[:, :, c:c + 256]).reshape(P, CH) for c in range(0, w.shape[2], 256)]


def _padded(w):
    w = w.reshape(P, -1)
    return np.concatenate([w, np.zeros((P, CH - w.shape[1]), w.dtype)], axis=1)


def _swap(w):
    return np.concatenate([w[..., 8:16], w[..., 0:8], w[..., 24:32], w[..., 16:24]], axis=-1)


def kernel(**inputs):
    import concourse.bacc as _bacc
    from concourse.bass_utils import run_bass_kernel_spmd as _run

    a = {k: np.asarray(v) for k, v in inputs.items()}
    w_in = a["ab_w_in"][0]
    pool_in, cq_in, ckv_in, kr_in = w_in[:, 0:512], w_in[:, 512:1280], w_in[:, 1280:1536], w_in[:, 1536:1568]
    kr = _tiles(np.concatenate([np.zeros((D, NOPE), w_in.dtype), kr_in, _swap(kr_in)], axis=1))
    w_uq = a["w_uq"][0].reshape(QR * P, HEADS, NOPE + ROPE)
    w_uq = np.concatenate([w_uq, _swap(w_uq[:, :, NOPE:])], axis=2)
    w_ukv = a["w_ukv"][0].reshape(KVR * P, HEADS, NOPE + VD)
    heads = []
    for r in range(PAIRS):
        q = _tiles(w_uq[:, 2 * r:2 * r + 2].reshape(QR * P, 256)).reshape(P, QR * 256)
        kv = _tiles(w_ukv[:, 2 * r:2 * r + 2].reshape(KVR * P, 256)).reshape(P, KVR * 256)
        heads.append(np.concatenate([q, kv], axis=1))
    b_c_val = [_column_chunks(a["conv_w_in"][0][:, D * m:D * m + D]) for m in range(3)]
    chunks = _ffn_chunks(a["ffn_w_gate"][0, 0], a["ffn_w_up"][0, 0], a["ffn_w_down"][0, 0])
    chunks += _column_chunks(pool_in) + _column_chunks(ckv_in) + [_padded(kr)] + _column_chunks(cq_in) + heads
    chunks += [_padded(a["pool_w"][0].transpose(1, 0, 2))] + _column_chunks(a["ab_w_out"][0])
    chunks += _ffn_chunks(a["ffn_w_gate"][0, 1], a["ffn_w_up"][0, 1], a["ffn_w_down"][0, 1])
    chunks += _ffn_chunks(a["ffn_w_gate"][1, 0], a["ffn_w_up"][1, 0], a["ffn_w_down"][1, 0])
    for i in range(4):
        chunks += [b_c_val[1][i], b_c_val[2][i], b_c_val[0][i]]
    chunks += _column_chunks(a["conv_w_out"][0])
    chunks += _ffn_chunks(a["ffn_w_gate"][1, 1], a["ffn_w_up"][1, 1], a["ffn_w_down"][1, 1])
    stream = np.stack(chunks)
    w_mod = a["w_mod"].reshape(LAYERS, 2, 4, P, HALVES, HALF).transpose(0, 4, 1, 3, 2, 5)
    w_mod = np.ascontiguousarray(w_mod).reshape(LAYERS * HALVES * 2, P, 4, HALF)

    def feature_major(x):
        return np.ascontiguousarray(x.reshape(T, KT, P).transpose(2, 1, 0))

    def columns(v):
        return v.reshape(-1, P).T

    cond = np.stack([a["c"][0], a["c_ctx"]]).reshape(2, KT, P).transpose(2, 1, 0).reshape(P, 2 * KT)
    conv_w = a["conv_w"][0].reshape(3, KT, P).transpose(2, 1, 0).reshape(P, 3 * KT)
    params = np.ascontiguousarray(np.concatenate(
        [columns(a["norm_g"]), columns(a["b_mod"]), columns(a["pool_scale"]), columns(a["q_norm_g"]),
         columns(a["kv_norm_g"]), conv_w, columns(a["final_norm_g"]), cond], axis=1))

    f = np.float32
    freqs = np.power(f(10000.0), -np.arange(0, 16, 2, dtype=f) / f(16))
    token = np.arange(T)
    table = np.zeros((P, T), f)
    for d in range(ROPE):
        pos = (token // 64 if d < 16 else token % 64).astype(f)
        angle = (pos * freqs[d % 8]).astype(f)
        table[NOPE + d] = np.cos(angle)
        table[NOPE + ROPE + d] = np.sin(angle) if d % 16 >= 8 else -np.sin(angle)
    consts = np.ascontiguousarray(np.concatenate([np.eye(P, dtype=f), table, table], axis=1))
    inv = np.zeros((4, T), f)
    for g, w in enumerate(WINDOWS):
        lo, hi = np.clip(token - w // 2, 0, T - 1), np.clip(token + (w - w // 2 - 1), 0, T - 1)
        inv[g] = f(1) / (hi - lo + 1).astype(f)
    inv = np.ascontiguousarray(np.broadcast_to(inv, (P, 4, T)))

    nc = _bacc.Bacc("TRN2", target_bir_lowering=False, num_devices=1)
    arrays = {"in_stream": stream, "in_w_mod": w_mod, "in_x": feature_major(a["x"][0]),
              "in_ctx": feature_major(a["ctx"][0]), "in_params": params, "in_consts": consts, "in_inv": inv}
    aps = [nc.dram_tensor(k, v.shape, mybir.dt.from_np(v.dtype), kind="ExternalInput").ap() for k, v in arrays.items()]
    result = nc.dram_tensor("out_h", (P, KT, T), mybir.dt.float32, kind="ExternalOutput").ap()
    build(nc, *aps, result)
    got = _run(nc, [arrays], core_ids=[0]).results[0]["out_h"]
    return np.ascontiguousarray(got.transpose(2, 1, 0)).reshape(1, T, D)
```

```python
import numpy as np
import concourse.bass as bass
from concourse import mybir
from contextlib import ExitStack

D, T, FF = 1024, 256, 2816
P = 128
KT = D // P
STEPS = FF // (2 * P)
CH = 2048
RING = 3
FFN_CHUNKS = 3 * STEPS
MIX_CHUNKS, CONV_CHUNKS = 16, 16
HEADS, NOPE, ROPE, VD = 8, 64, 32, 64
QR, KVR = 768 // P, 256 // P
PAIRS = HEADS // 2
EPS = 1e-6
ATTN_SCALE = 1.0 / float(np.sqrt(NOPE + ROPE))
WINDOWS = (2, 4, 8, 16)
PAD = 8
PW = T + 2 * PAD
LAYERS, NMOD = 2, 9
HALVES = 2 * NMOD
HALF = 512

PARAM = {}
_at = 0
for _name, _n in (("norm_g", LAYERS * 3 * KT), ("b_mod", LAYERS * NMOD * KT), ("pool_scale", 4), ("q_norm_g", QR),
                  ("kv_norm_g", KVR), ("conv_w", 3 * KT), ("final_norm_g", KT), ("cond", 2 * KT)):
    PARAM[_name] = _at
    _at += _n
N_PARAM = _at

PASS = [0, 33, 82, 115, 164]
MIX, CONV = 66, 148
N_CHUNKS = 197
START_HALVES = 4


def ring(n, i=0):
    return n % RING, i + (n // RING + 1)


def mod_ops(half):
    return 2 * KT if half < HALVES else KT


def mod_steps_before(half):
    return sum(mod_ops(h) for h in range(START_HALVES, half))


def build(nc, stream, w_mod, x_h, x_g, params, consts, inv_count, out):
    f32, f32r = mybir.dt.float32, mybir.dt.float32r
    ALU, ACT, AX = mybir.AluOpType, mybir.ActivationFunctionType, mybir.AxisListType
    ADD, SUB, MUL = ALU.add, ALU.subtract, ALU.mult
    place = [16512]

    def sb(name, shape, dt, at=None):
        size = 4 * int(np.prod(shape[1:]))
        if at is None:
            at = place[0]
            place[0] += (size + 31) // 32 * 32
        t = nc.alloc_sbuf_tensor_at(name, shape, dt, offset=at)
        where[name] = at
        return t

    where = {}
    raw = sb("raw", [P, RING, CH], f32)
    w_hi = sb("w_hi", [P, RING, CH], f32r)
    w_lo = sb("w_lo", [P, RING, CH], f32r)
    mod_raw = sb("mod_raw", [P, 2, 4, HALF], f32)
    mod_acc = sb("mod_acc", [P, 2, HALF], f32)
    resid = sb("resid", [P, 2, KT, T], f32)
    u_hi = sb("u_hi", [P, KT, 2 * T], f32r)
    u_lo = sb("u_lo", [P, KT, 2 * T], f32r)
    scratch = sb("scratch", [P, KT, T], f32)
    silu = sb("silu", [P, 2 * T], f32)
    prod = sb("prod", [P, 2 * T], f32)
    hid_hi = sb("hid_hi", [P, 2 * T], f32r)
    hid_lo = sb("hid_lo", [P, 2 * T], f32r)
    kvn_hi = sb("kvn_hi", [P, KVR, 2 * T], f32r)
    kvn_lo = sb("kvn_lo", [P, KVR, 2 * T], f32r)
    mix_hi = sb("mix_hi", [P, KT, T], f32r)
    mix_lo = sb("mix_lo", [P, KT, T], f32r)
    region_q = sb("cq", [P, 10 * T], f32)
    region_kv = sb("ckv_region", [P, 8 * T], f32)
    std = sb("std", [P, T], f32)
    rstd = sb("rstd", [P, T], f32)
    par = sb("par", [P, N_PARAM], f32)
    con = sb("con", [P, P + 2 * T], f32)
    ones = sb("ones", [P, P], f32)
    zeros = sb("zeros", [P, T], f32r)
    mod_out = sb("mod_out", [P, LAYERS * NMOD * KT, 2], f32)
    coef = sb("coef", [P, 4, KT], f32)
    cond = sb("cond", [P, KT, 2], f32)
    eps = sb("eps", [P, 1], f32)
    table = sb("table", [P, 2], f32)
    stat = sb("stat", [P, 4, 16], f32)
    mod_sum = sb("mod_sum", [P, 4, 2], f32)
    assert place[0] <= nc.sbuf_usable_end, place[0]

    cq = region_q[:, 0:QR * T].rearrange("p (k t) -> p k t", k=QR)
    q_f = sb("q_f", [P, 2 * T], f32, where["cq"])
    rope_a = sb("rope_a", [P, 2 * T], f32, where["cq"] + 8 * T)
    rope_b = sb("rope_b", [P, 2 * T], f32, where["cq"] + 16 * T)
    q_hi = sb("q_hi", [P, 2 * T], f32r, where["cq"] + 24 * T)
    q_lo = sb("q_lo", [P, 2 * T], f32r, where["cq"] + 32 * T)
    ckv = region_kv[:, 0:4 * T].rearrange("p (k t) -> p k t", k=KVR)
    ckv_sq = region_kv[:, 4 * T:8 * T].rearrange("p (k t) -> p k t", k=KVR)
    k_hi = sb("k_hi", [P, 2, 2 * T], f32r, where["ckv_region"])
    k_lo = sb("k_lo", [P, 2, 2 * T], f32r, where["ckv_region"] + 16 * T)
    cq_sq = sb("cq_sq", [P, QR, T], f32, where["mix_hi"])
    inv_cnt = sb("inv_cnt", [P, 4, T], f32, where["mix_lo"])
    kv_std = sb("kv_std", [P, 2 * T], f32, where["scratch"])
    kv_rstd = sb("kv_rstd", [P, 2 * T], f32, where["scratch"] + 8 * T)
    kr_f = sb("kr_f", [P, 2 * T], f32, where["scratch"] + 16 * T)
    v_hi = sb("v_hi", [P, 2, 2 * T], f32r, where["scratch"])
    v_lo = sb("v_lo", [P, 2, 2 * T], f32r, where["scratch"] + 16 * T)
    qn_hi = sb("qn_hi", [P, QR, T], f32r, where["u_hi"])
    qn_lo = sb("qn_lo", [P, QR, T], f32r, where["u_hi"] + 4 * QR * T)
    probs = [sb("probs0", [P, 2, 2 * T], f32, where["u_hi"] + 8 * QR * T),
             sb("probs1", [P, 2, 2 * T], f32, where["mod_raw"] + 32 * PW)]
    pt_hi = sb("pt_hi", [P, 2, 4, T], f32r, where["u_lo"])
    pt_lo = sb("pt_lo", [P, 2, 4, T], f32r, where["u_lo"] + 32 * T)
    pad_x = sb("pad_x", [P, 4, PW], f32, where["mod_raw"])
    win2 = sb("win2", [P, 4, PW], f32, where["mod_raw"] + 16 * PW)
    win4 = sb("win4", [P, 3, PW], f32, where["mod_raw"] + 32 * PW)
    win8 = sb("win8", [P, 2, PW], f32, where["mod_raw"] + 44 * PW)
    win16 = sb("win16", [P, 1, PW], f32, where["mod_raw"] + 52 * PW)
    start_row = sb("start_row", [2, 4, HALF], f32, where["silu"])
    p_hi = sb("p_hi", [P, 4, T], f32r, where["silu"])
    p_lo = sb("p_lo", [P, 4, T], f32r, where["silu"] + 16 * T)
    z_pad = sb("z_pad", [P, 2, T + 2], f32, where["scratch"])
    conv_1 = sb("conv_1", [P, 2, T], f32, where["scratch"] + 3072)
    conv_2 = sb("conv_2", [P, 2, T], f32, where["scratch"] + 5120)

    def col(name, k=0, n=1):
        return par[:, PARAM[name] + k:PARAM[name] + k + n]

    def shift(layer, kind, c, k=0, n=1, which=0):
        at = layer * NMOD * KT + (3 * kind + which) * KT + k
        return mod_out[:, at:at + n, c]

    JOINS = [(0, None, (0, 0)), (1, None, (0, 0)), (0, (0, 0, 0.5), (0, 1)), (1, (0, 0, 0.5), (0, 1)),
             (0, (0, 1, 1.0), (0, 2)), (0, (0, 2, 0.5), (1, 0)), (0, (1, 0, 0.5), (1, 1)),
             (0, (1, 1, 1.0), (1, 2)), (0, (1, 2, 0.5), None)]

    ctx = ExitStack()
    with ctx:
        psum = ctx.enter_context(nc.psum_tensor("psum", [P, 8, 512], f32))
        GATE, UP, MODB, SSQ = 4, 5, 6, 7

        def sem(name):
            return ctx.enter_context(nc.semaphore(name))

        raw_arrived = [sem(f"raw_arrived{s}") for s in range(RING)]
        hi_ready = sem("hi_ready")
        lo_ready = [sem(f"lo_ready{s}") for s in range(RING)]
        multiplied = sem("multiplied")
        mod_arrived = [sem("mod_arrived0"), sem("mod_arrived1")]
        mod_used = [sem("mod_used0"), sem("mod_used1")]
        start_rows, start_turned = sem("start_rows"), sem("start_turned")
        mod_reduced, mod_summed = sem("mod_reduced"), sem("mod_summed")
        mod_written = sem("mod_written")
        inputs_in = sem("inputs_in")
        context_in = sem("context_in")
        params_in = sem("params_in")
        inv_in = sem("inv_in")
        consts_set = sem("consts_set")
        cond_ready = sem("cond_ready")
        acc_ready, resid_done, sq_done, ssq_done, std_done, rstd_done = (
            sem(n) for n in ("acc_ready", "resid_done", "sq_done", "ssq_done", "std_done", "rstd_done"))
        t_done, u_hi_done, u_lo_done = sem("t_done"), sem("u_hi_done"), sem("u_lo_done")
        silu_done, prod_done, hid_hi_done, hid_lo_done = (
            sem(n) for n in ("silu_done", "prod_done", "hid_hi_done", "hid_lo_done"))
        dve_step, mod_step = sem("dve_step"), sem("mod_step")
        act_step = sem("act_step")
        pool_step = sem("pool_step")
        pad_zeroed, pool_copied, pooled, p_hi_done, p_lo_done = (
            sem(n) for n in ("pad_zeroed", "pool_copied", "pooled", "p_hi_done", "p_lo_done"))
        kv_sq_done, kv_ssq_done, kv_std_done, kv_t_done, kv_hi_done, kv_lo_done = (
            sem(n) for n in ("kv_sq_done", "kv_ssq_done", "kv_std_done", "kv_t_done", "kv_hi_done", "kv_lo_done"))
        q_sq_done, q_ssq_done, q_std_done, q_t_done, qn_hi_done, qn_lo_done = (
            sem(n) for n in ("q_sq_done", "q_ssq_done", "q_std_done", "q_t_done", "qn_hi_done", "qn_lo_done"))
        kr_done, kr_hi_done, kr_lo_done = sem("kr_done"), sem("kr_hi_done"), sem("kr_lo_done")
        q_proj, k_proj, q_nope, q_roped, q_hi_done, q_lo_done = (
            sem(n) for n in ("q_proj", "k_proj", "q_nope", "q_roped", "q_hi_done", "q_lo_done"))
        k_hi_done, k_lo_done, v_hi_done, v_lo_done = (sem(n) for n in ("k_hi_done", "k_lo_done", "v_hi_done", "v_lo_done"))
        v_proj = sem("v_proj")
        scored, neg_max, exp_done, p_normal, p_turned, pt_hi_done, pt_lo_done = (
            sem(n) for n in ("scored", "neg_max", "exp_done", "p_normal", "p_turned", "pt_hi_done", "pt_lo_done"))
        pv_done, attn_hi_done, attn_lo_done = sem("pv_done"), sem("attn_hi_done"), sem("attn_lo_done")
        pool_hi_done, pool_lo_done = sem("pool_hi_done"), sem("pool_lo_done")
        c_copied, z_done, conv_done, conv_hi_done, conv_lo_done = (
            sem(n) for n in ("c_copied", "z_done", "conv_done", "conv_hi_done", "conv_lo_done"))
        stored = sem("stored")

        block = ctx.enter_context(nc.Block())

        def turned_hi(act, r, a):
            for b in range(2):
                n = 4 * r + 2 * a + b
                act.wait_ge(p_turned, n + 1)
                act.activation(pt_hi[:, a, 2 * b:2 * b + 2, :],
                               psum[:, 4 + 2 * a + b, :].rearrange("p (k t) -> p k t", k=2), ACT.Copy).then_inc(pt_hi_done, 1)

        def split_step(dve, split_lo, hidden_product, hidden_low, b, k):
            for j in (3, 4):
                if (b + j) % RING == 1:
                    split_lo(b + j)
            dve.wait_ge(multiplied, b + 3)
            hidden_product(k)
            hidden_low(k)
            if (b + 5) % RING == 1:
                split_lo(b + 5)

        def turned_lo(dve, r, a):
            for b in range(2):
                n = 4 * r + 2 * a + b
                dve.wait_ge(pt_hi_done, n + 1)
                dve.tensor_tensor(pt_lo[:, a, 2 * b:2 * b + 2, :],
                                  psum[:, 4 + 2 * a + b, :].rearrange("p (k t) -> p k t", k=2),
                                  pt_hi[:, a, 2 * b:2 * b + 2, :].bitcast(f32), SUB).then_inc(pt_lo_done, 1)

        @block.sync
        def _(sp):
            def load(n, row, i=0):
                slot, uses = ring(n, i)
                if n >= RING:
                    sp.wait_ge(lo_ready[slot], uses - 1)
                sp.dma_start(raw[:, slot, :], stream[row]).then_inc(raw_arrived[slot], 16)

            def load_mod(half):
                for kh in range(2):
                    if half > 0:
                        sp.wait_ge(mod_used[kh], half)
                    sp.dma_start(mod_raw[:, kh, :, :], w_mod[half * 2 + kh]).then_inc(mod_arrived[kh], 16)

            sp.dma_start(par[:, :], params).then_inc(params_in, 16)
            sp.dma_start(con[:, :], consts).then_inc(params_in, 16)
            load_mod(0)
            sp.dma_start(resid[:, 0, :, :], x_h).then_inc(inputs_in, 16)
            for half in range(1, START_HALVES):
                load_mod(half)
                load(half - 1, half - 1)
            sp.dma_start(resid[:, 1, :, :], x_g).then_inc(context_in, 16)
            sp.dma_start(inv_cnt[:, :, :], inv_count).then_inc(inv_in, 16)
            load_mod(START_HALVES)
            with sp.Fori(0, 10) as i:
                for j in range(RING):
                    load(3 + j, i * RING + (3 + j), i)
            with sp.Fori(0, 11) as i:
                for j in range(RING):
                    load(33 + j, i * RING + j, i)
            with sp.Fori(0, 5) as i:
                for j in range(RING):
                    load(66 + j, i * RING + (33 + j), i)
            sp.wait_ge(p_lo_done, 1)
            sp.wait_ge(p_turned, 4 * PAIRS)
            for kh in range(2):
                sp.dma_start(mod_raw[:, kh, :, :], w_mod[HALVES * 2 + kh]).then_inc(mod_arrived[kh], 16)
            with sp.Fori(0, 18) as i:
                for j in range(RING):
                    load(81 + j, i * RING + (48 + j), i)
            with sp.Fori(0, 20) as i:
                for j in range(RING):
                    load(135 + j, i * RING + (102 + j), i)
            for n in (195, 196):
                load(n, n - 33)
            for j in range(KT // 2):
                sp.wait_ge(t_done, 8 * KT + 2 * j + 2)
                sp.dma_start(out[:, 2 * j:2 * j + 2, :], scratch[:, 2 * j:2 * j + 2, :]).then_inc(stored, 16)
            sp.wait_ge(stored, 16 * (KT // 2))

        @block.scalar
        def _(act):
            def split_hi(n, i=0):
                slot, uses = ring(n, i)
                if n >= RING:
                    act.wait_ge(multiplied, i * RING + (n - RING + 1))
                act.wait_ge(raw_arrived[slot], uses * 16)
                act.activation(w_hi[:, slot, :], raw[:, slot, :], ACT.Copy).then_inc(hi_ready, 1)

            def fetch(func):
                act.activation(table[:, 0:1] if func == ACT.Silu else table[:, 1:2], eps[:, :], func)

            def load_mod(half, kh, i=0):
                act.wait_ge(mod_step, i * mod_ops(half) + mod_steps_before(half) + mod_ops(half) // 2 * (kh + 1))
                act.dma_start(mod_raw[:, kh, :, :], w_mod[(i + (half + 1)) * 2 + kh]).then_inc(mod_arrived[kh], 16)

            def square_stream(e):
                who = JOINS[e][0]
                if e < 2:
                    act.wait_ge((inputs_in, context_in)[e], 16)
                if e > 0:
                    act.wait_ge(u_lo_done, KT * e)
                for j in range(KT // 2):
                    if e >= 2:
                        act.wait_ge(resid_done, (e - 2) * 4 + j + 1)
                    act.activation(scratch[:, 2 * j:2 * j + 2, :], resid[:, who, 2 * j:2 * j + 2, :],
                                   ACT.Square).then_inc(sq_done, 1)

            def deviation(e):
                act.wait_ge(ssq_done, e + 1)
                if e > 0:
                    act.wait_ge(rstd_done, e)
                act.activation(std[:, :], psum[:, SSQ, 0:T], ACT.Sqrt, bias=eps[:, :],
                               scale=1.0 / D).then_inc(std_done, 1)

            def modulated_hi(e):
                who, _, norm = JOINS[e]
                for j in range(KT):
                    act.wait_ge(t_done, KT * e + j + 1)
                    act.activation(u_hi[:, j, who * T:who * T + T], scratch[:, j, :], ACT.Identity,
                                   bias=shift(*norm, who, j)).then_inc(u_hi_done, 1)

            def silu_gate():
                act.activation(silu[:, :], psum[:, GATE, :], ACT.Silu).then_inc(silu_done, 1)

            def hidden_hi(k):
                act.wait_ge(prod_done, k + 1)
                act.activation(hid_hi[:, :], prod[:, :], ACT.Copy).then_inc(hid_hi_done, 1)

            def ffn_steps(p, first, count, half=None):
                b = PASS[p] + 2 + 3 * (first - 1)
                with act.Fori(0, count) as i:
                    act.wait_ge(multiplied, i * RING + (b + 1))
                    silu_gate()
                    split_hi(b + 3, i)
                    split_hi(b + 4, i)
                    if half is not None:
                        load_mod(half, 0, i)
                    hidden_hi(i + (STEPS * p + first))
                    split_hi(b + 5, i)
                    if half is not None:
                        load_mod(half, 1, i)

            def ffn_step0(p, inner=None, half=None):
                b = PASS[p]
                act.wait_ge(multiplied, b + 1)
                if p > 0:
                    act.wait_ge(prod_done, STEPS * p)
                silu_gate()
                split_hi(b + 3)
                if inner is not None:
                    deviation(inner)
                    fetch(ACT.Silu)
                split_hi(b + 4)
                if half is not None:
                    load_mod(half, 0)
                hidden_hi(STEPS * p)
                if half is not None:
                    load_mod(half, 1)
                if inner is not None:
                    modulated_hi(inner)

            def pool_copy(i):
                if i > 0:
                    act.wait_ge(multiplied, MIX + i + 1)
                act.activation(pad_x[:, 2 * i:2 * i + 2, PAD:PAD + T],
                               psum[:, 4 + i, :].rearrange("p (a t) -> p a t", a=2), ACT.Copy).then_inc(pool_copied, 1)

            def query_copy(i, chunk, bank):
                act.wait_ge(multiplied, chunk + 1)
                view = psum[:, bank, :].rearrange("p (a t) -> p a t", a=2)
                act.activation(cq[:, 2 * i:2 * i + 2, :], view, ACT.Copy).then_inc(act_step, 1)
                act.activation(cq_sq[:, 2 * i:2 * i + 2, :], view, ACT.Square).then_inc(q_sq_done, 1)

            act.wait_ge(params_in, 32)
            act.activation(cond[:, :, :], col("cond", 0, 2 * KT).rearrange("p (k c) -> p k c", c=2),
                           ACT.Silu).then_inc(cond_ready, 1)
            act.wait_ge(consts_set, 3)
            square_stream(0)
            deviation(0)
            for n in range(RING):
                split_hi(n)
            for half in range(START_HALVES):
                act.wait_ge(mod_used[1], half + 1)
                act.activation(start_row[:, half, :], psum[0:2, half, :], ACT.Copy).then_inc(start_rows, 1)
            modulated_hi(0)
            square_stream(1)
            ffn_step0(0, inner=1, half=4)
            ffn_steps(0, 1, STEPS - 1, half=5)
            square_stream(2)
            split_hi(PASS[1] + 2)
            ffn_step0(1, inner=2)
            ffn_steps(1, 1, 2, half=15)
            ffn_steps(1, 3, STEPS - 3)
            fetch(ACT.Sqrt)

            square_stream(3)
            split_hi(MIX + 2)
            act.wait_ge(multiplied, MIX + 1)
            act.wait_ge(pad_zeroed, 1)
            pool_copy(0)
            split_hi(MIX + 3)
            deviation(3)
            pool_copy(1)
            modulated_hi(3)
            split_hi(MIX + 4)
            for i in range(2):
                query_copy(i, MIX + 2 + i, 2 + i)
                split_hi(MIX + 5 + i)
            act.wait_ge(multiplied, MIX + 5)
            for i, bank in enumerate((6, 0)):
                act.activation(ckv[:, i, :], psum[:, bank, :], ACT.Copy).then_inc(act_step, 1)
                act.activation(ckv_sq[:, i, :], psum[:, bank, :], ACT.Square).then_inc(kv_sq_done, 1)
            split_hi(MIX + 7)
            act.wait_ge(kv_ssq_done, 1)
            act.wait_ge(u_lo_done, 4 * KT)
            act.activation(kv_std[:, :], psum[:, 5, :], ACT.Sqrt, bias=eps[:, :],
                           scale=1.0 / (KVR * P)).then_inc(kv_std_done, 1)
            split_hi(MIX + 8)
            for i in range(KVR):
                act.wait_ge(kv_t_done, i + 1)
                act.activation(kvn_hi[:, i, :], ckv_sq[:, i, :], ACT.Copy).then_inc(kv_hi_done, 1)
            query_copy(2, MIX + 6, 4)
            act.wait_ge(q_ssq_done, 1)
            act.activation(std[:, :], psum[:, 6, 0:T], ACT.Sqrt, bias=eps[:, :],
                           scale=1.0 / (QR * P)).then_inc(q_std_done, 1)
            act.wait_ge(kr_done, 1)
            act.wait_ge(kv_lo_done, KVR)
            for a in range(2):
                act.activation(k_hi[NOPE:NOPE + ROPE, a, :], kr_f[NOPE:NOPE + ROPE, :],
                               ACT.Copy).then_inc(kr_hi_done, 1)
            for i in range(QR):
                act.wait_ge(q_t_done, i + 1)
                act.activation(qn_hi[:, i, :], cq_sq[:, i, :], ACT.Copy).then_inc(qn_hi_done, 1)
            split_hi(MIX + 9)
            act.wait_ge(pooled, 1)
            act.activation(p_hi[:, :, :], win2[:, :, PAD:PAD + T], ACT.Copy).then_inc(p_hi_done, 1)
            fetch(ACT.Exp)

            def projected_hi(r):
                for a in range(2):
                    act.wait_ge(k_proj, 2 * r + a + 1)
                    act.activation(k_hi[0:NOPE, a, :], psum[0:NOPE, 1 + a, :], ACT.Copy).then_inc(k_hi_done, 1)
                act.wait_ge(v_proj, r + 1)
                act.wait_ge(kr_lo_done, 2)
                act.activation(v_hi[:, r % 2, :], psum[:, 3, :], ACT.Copy).then_inc(v_hi_done, 1)
                act.wait_ge(multiplied, MIX + 8 + r)
                if r > 0:
                    act.wait_ge(q_lo_done, r)
                act.activation(q_f[0:NOPE, :], psum[0:NOPE, 0, :], ACT.Copy).then_inc(q_nope, 1)
                act.wait_ge(q_nope, r + 1)
                act.wait_ge(q_roped, r + 1)
                act.activation(q_hi[0:NOPE + ROPE, :], q_f[0:NOPE + ROPE, :], ACT.Copy).then_inc(q_hi_done, 1)

            projected_hi(0)
            for r in range(PAIRS):
                for a in range(2):
                    for qt in range(2):
                        n = 4 * r + 2 * a + qt
                        act.wait_ge(neg_max, n + 1)
                        if r > 0:
                            act.wait_ge(p_turned, 4 * (r - 1) + 2 * a + 2)
                        act.activation(probs[a][:, qt, :], psum[:, 4 + 2 * a + qt, :], ACT.Exp,
                                       bias=stat[:, 0, n:n + 1], scale=ATTN_SCALE,
                                       accum_out=stat[:, 1, n:n + 1]).then_inc(exp_done, 1)
                split_hi(MIX + 10 + r)
                for a in range(2):
                    turned_hi(act, r, a)
                if r + 1 < PAIRS:
                    projected_hi(r + 1)
                act.wait_ge(pv_done, r + 1)
                for a in range(2):
                    act.activation(mix_hi[a * VD:a * VD + VD, 4 + r, :], psum[a * VD:a * VD + VD, 3, a * T:a * T + T],
                                   ACT.Copy).then_inc(attn_hi_done, 1)

            act.wait_ge(multiplied, MIX + 12)
            for g in range(4):
                act.activation(mix_hi[:, g, :], psum[:, 5 + g // 2, (g % 2) * T:(g % 2) * T + T], ACT.Identity,
                               scale=col("pool_scale", g)).then_inc(pool_hi_done, 1)
            for n in range(MIX + 14, MIX + 18):
                split_hi(n)
            fetch(ACT.Sqrt)
            square_stream(4)
            deviation(4)
            modulated_hi(4)
            split_hi(PASS[2] + 2)
            ffn_step0(2, half=18)
            ffn_steps(2, 1, STEPS - 1, half=19)
            fetch(ACT.Sqrt)
            square_stream(5)
            deviation(5)
            modulated_hi(5)
            split_hi(PASS[3] + 2)
            ffn_step0(3)
            ffn_steps(3, 1, 6, half=29)
            ffn_steps(3, 7, STEPS - 7)
            fetch(ACT.Sqrt)
            square_stream(6)
            deviation(6)
            modulated_hi(6)
            split_hi(CONV + 2)

            with act.Fori(0, KT // 2) as i:
                act.wait_ge(multiplied, i * RING + (CONV + 1))
                act.activation(silu[:, :], psum[:, GATE, :], ACT.Copy).then_inc(c_copied, 1)
                split_hi(CONV + 3, i)
                split_hi(CONV + 4, i)
                split_hi(CONV + 5, i)
                act.wait_ge(conv_done, i + 1)
                act.activation(mix_hi[:, bass.ds(i * 2, 2), :], prod[:, :].rearrange("p (a t) -> p a t", a=2),
                               ACT.Copy).then_inc(conv_hi_done, 1)
            for n in range(CONV + 15, CONV + 18):
                split_hi(n)
            fetch(ACT.Sqrt)
            square_stream(7)
            deviation(7)
            modulated_hi(7)
            split_hi(PASS[4] + 2)
            ffn_step0(4)
            ffn_steps(4, 1, STEPS - 2)
            b = PASS[4] + 29
            act.wait_ge(multiplied, b + 1)
            silu_gate()
            split_hi(b + 3)
            hidden_hi(STEPS * 5 - 1)
            fetch(ACT.Sqrt)
            square_stream(8)
            deviation(8)

        @block.vector
        def _(dve):
            steps = [0]

            def settle(ins):
                steps[0] += 1
                ins.then_inc(dve_step, 1)
                dve.wait_ge(dve_step, steps[0])

            def split_lo(n, i=0):
                slot, uses = ring(n, i)
                dve.wait_ge(hi_ready, i * RING + (n + 1))
                dve.tensor_tensor(w_lo[:, slot, :], raw[:, slot, :], w_hi[:, slot, :].bitcast(f32),
                                  SUB).then_inc(lo_ready[slot], 1)

            def gather(e):
                who, (layer, kind, factor), _ = JOINS[e]
                gate = coef[:, 2, :]
                source, first_chunk = {2: (0, PASS[0] + 32), 3: (1, PASS[1] + 32), 4: (-1, MIX + 12), 5: (2, PASS[2] + 32),
                                       6: (3, PASS[3] + 32), 7: (-1, CONV + 12), 8: (4, PASS[4] + 32)}[e]
                settle(dve.tensor_scalar(gate, shift(layer, kind, who, 0, KT, 2), factor, None, MUL))
                for j in range(KT // 2):
                    if source < 0:
                        dve.wait_ge(multiplied, first_chunk + j + 1)
                    elif j < 3:
                        dve.wait_ge(acc_ready, 3 * source + j + 1)
                    else:
                        dve.wait_ge(multiplied, first_chunk + 1)
                    for a in range(2):
                        k = 2 * j + a
                        last = dve.scalar_tensor_tensor(resid[:, who, k, :], psum[:, j, a * T:a * T + T],
                                                        gate[:, k:k + 1], resid[:, who, k, :], MUL, ADD)
                    last.then_inc(resid_done, 1)

            def inverse_rms(e):
                dve.wait_ge(std_done, e + 1)
                dve.reciprocal(rstd[:, :], std[:, :]).then_inc(rstd_done, 1)

            def modulate(e):
                who, _, norm = JOINS[e]
                dve.wait_ge(resid_done, 4 * (e - 1)) if e >= 2 else None
                if norm is not None:
                    layer, kind = norm
                    gain = coef[:, 3, :]
                    settle(dve.scalar_tensor_tensor(gain, shift(layer, kind, who, 0, KT, 1), 1.0,
                                                    col("norm_g", (layer * 3 + kind) * KT, KT), ADD, MUL))
                else:
                    gain = col("final_norm_g", 0, KT)
                if e > 0:
                    inverse_rms(e)
                dve.wait_ge(rstd_done, e + 1)

                def scaled(j):
                    dve.scalar_tensor_tensor(scratch[:, j, :], resid[:, who, j, :], gain[:, j:j + 1],
                                             rstd[:, :], MUL, MUL).then_inc(t_done, 1)

                scaled(0)
                for j in range(KT):
                    if j + 1 < KT:
                        scaled(j + 1)
                    if norm is None:
                        continue
                    dve.wait_ge(u_hi_done, KT * e + j + 1)
                    at = slice(who * T, who * T + T)
                    dve.scalar_tensor_tensor(u_lo[:, j, at], scratch[:, j, :], shift(*norm, who, j),
                                             u_hi[:, j, at].bitcast(f32), ADD, SUB).then_inc(u_lo_done, 1)

            def write_mod(done, half, conds, i=0):
                dve.wait_ge(mod_reduced, done)
                for c in range(conds):
                    last = dve.reduce_sum(mod_sum[:, :, c], psum[:, MODB + c, :].rearrange("p (k q) -> p k q", k=4), AX.X)
                last.then_inc(mod_summed, 1)
                dve.wait_ge(mod_summed, done)
                for c in range(conds):
                    last = dve.tensor_tensor(mod_out[:, bass.ds((i + half) * 4, 4), c], mod_sum[:, :, c],
                                             par[:, bass.ds((i + half) * 4 + PARAM["b_mod"], 4)], ADD)
                last.then_inc(mod_written, 1)

            def sum_mod(half, conds, i=0):
                base = mod_steps_before(half)
                for kt in range(KT):
                    kh, k = kt // 4, kt % 4
                    if k == 0:
                        dve.wait_ge(mod_arrived[kh], (i + (half + 1)) * 16)
                    for c in range(conds):
                        at = base + kt * conds + c
                        w = mod_raw[:, kh, k, :]
                        if kt == 0:
                            ins = dve.tensor_scalar(mod_acc[:, c, :], w, cond[:, kt, c:c + 1], None, MUL)
                        else:
                            dve.wait_ge(mod_step, i * (KT * conds) + (at - conds + 1))
                            ins = dve.scalar_tensor_tensor(mod_acc[:, c, :], w, cond[:, kt, c:c + 1],
                                                           mod_acc[:, c, :], MUL, ADD)
                        ins.then_inc(mod_step, 1)

            def hidden_product(k):
                dve.wait_ge(silu_done, k + 1)
                dve.tensor_tensor(prod[:, :], silu[:, :], psum[:, UP, :], MUL).then_inc(prod_done, 1)

            def hidden_low(k):
                dve.wait_ge(hid_hi_done, k + 1)
                dve.tensor_tensor(hid_lo[:, :], prod[:, :], hid_hi[:, :].bitcast(f32), SUB).then_inc(hid_lo_done, 1)

            def ffn_steps(p, first, count, mod=None):
                b = PASS[p] + 2 + 3 * (first - 1)
                with dve.Fori(0, count) as i:
                    if mod is not None:
                        half, conds, done = mod
                        write_mod(i + done, half - 1, conds, i)
                        dve.wait_ge(mod_written, i + (done + 1))
                        sum_mod(half, conds, i)
                    for j in (3, 4):
                        if (b + j) % RING == 1:
                            split_lo(b + j, i)
                    dve.wait_ge(multiplied, i * RING + (b + 3))
                    hidden_product(i + (STEPS * p + first))
                    hidden_low(i + (STEPS * p + first))
                    if (b + 5) % RING == 1:
                        split_lo(b + 5, i)

            dve.memset(ones[:, :], 1.0).then_inc(consts_set, 1)
            dve.memset(zeros[:, :].bitcast(f32), 0.0).then_inc(consts_set, 1)
            dve.memset(eps[:, :], EPS).then_inc(consts_set, 1)
            inverse_rms(0)
            dve.wait_ge(params_in, 32)
            dve.wait_ge(start_turned, 1)
            for c in range(2):
                last = dve.tensor_tensor(mod_out[:, 0:4 * START_HALVES, c],
                                         psum[:, MODB, 0:8 * START_HALVES].rearrange("p (k c) -> p k c", c=2)[:, :, c],
                                         col("b_mod", 0, 4 * START_HALVES), ADD)
            last.then_inc(mod_written, 1)
            dve.wait_ge(mod_written, 1)
            modulate(0)

            dve.wait_ge(cond_ready, 1)
            sum_mod(4, 2)
            dve.wait_ge(multiplied, PASS[0] + 2)
            hidden_product(0)
            hidden_low(0)
            modulate(1)
            ffn_steps(0, 1, STEPS - 1, mod=(5, 2, 1))
            write_mod(11, 14, 2)
            dve.wait_ge(mod_written, 12)
            gather(2)

            dve.wait_ge(multiplied, PASS[1] + 2)
            hidden_product(STEPS)
            hidden_low(STEPS)
            modulate(2)
            sum_mod(15, 2)
            split_step(dve, split_lo, hidden_product, hidden_low, PASS[1] + 2, STEPS + 1)
            ffn_steps(1, 2, 2, mod=(16, 2, 12))
            write_mod(14, 17, 2)
            dve.wait_ge(mod_written, 15)
            ffn_steps(1, 4, STEPS - 4)
            gather(3)

            modulate(3)
            dve.wait_ge(u_lo_done, 4 * KT)
            dve.wait_ge(kv_std_done, 1)
            settle(dve.reciprocal(kv_rstd[:, :], kv_std[:, :]))
            for i in range(KVR):
                dve.scalar_tensor_tensor(ckv_sq[:, i, :], ckv[:, i, :], col("kv_norm_g", i), kv_rstd[:, :],
                                         MUL, MUL).then_inc(kv_t_done, 1)
            dve.wait_ge(multiplied, MIX + 6)
            rope_rows, swap_rows = slice(NOPE, NOPE + ROPE), slice(NOPE + ROPE, P)
            kr_a, kr_b = prod[rope_rows, 0:T], prod[rope_rows, T:2 * T]
            dve.tensor_tensor(kr_a, psum[rope_rows, 1, 0:T], con[rope_rows, P:P + T], MUL)
            settle(dve.tensor_tensor(kr_b, psum[swap_rows, 1, 0:T], con[swap_rows, P:P + T], MUL))
            dve.tensor_tensor(kr_f[rope_rows, 0:T], kr_a, kr_b, ADD)
            dve.tensor_copy(kr_f[rope_rows, T:2 * T], psum[rope_rows, 1, T:2 * T]).then_inc(kr_done, 1)
            for i in range(KVR):
                dve.wait_ge(kv_hi_done, i + 1)
                dve.tensor_tensor(kvn_lo[:, i, :], ckv_sq[:, i, :], kvn_hi[:, i, :].bitcast(f32),
                                  SUB).then_inc(kv_lo_done, 1)
            dve.wait_ge(q_std_done, 1)
            settle(dve.reciprocal(rstd[:, :], std[:, :]))
            for i in range(QR):
                dve.scalar_tensor_tensor(cq_sq[:, i, :], cq[:, i, :], col("q_norm_g", i), rstd[:, :],
                                         MUL, MUL).then_inc(q_t_done, 1)
            for a in range(2):
                dve.wait_ge(kr_hi_done, a + 1)
                dve.tensor_tensor(k_lo[rope_rows, a, :], kr_f[rope_rows, :], k_hi[rope_rows, a, :].bitcast(f32),
                                  SUB).then_inc(kr_lo_done, 1)
            for i in range(QR):
                dve.wait_ge(qn_hi_done, i + 1)
                dve.tensor_tensor(qn_lo[:, i, :], cq_sq[:, i, :], qn_hi[:, i, :].bitcast(f32),
                                  SUB).then_inc(qn_lo_done, 1)

            def projected_lo(r):
                for a in range(2):
                    dve.wait_ge(k_hi_done, 2 * r + a + 1)
                    dve.tensor_tensor(k_lo[0:NOPE, a, :], psum[0:NOPE, 1 + a, :], k_hi[0:NOPE, a, :].bitcast(f32),
                                      SUB).then_inc(k_lo_done, 1)
                dve.wait_ge(v_hi_done, r + 1)
                dve.tensor_tensor(v_lo[:, r % 2, :], psum[:, 3, :], v_hi[:, r % 2, :].bitcast(f32),
                                  SUB).then_inc(v_lo_done, 1)
                dve.wait_ge(multiplied, MIX + 8 + r)
                dve.tensor_tensor(rope_a[rope_rows, :], psum[rope_rows, 0, :], con[rope_rows, P:P + 2 * T], MUL)
                settle(dve.tensor_tensor(rope_b[rope_rows, :], psum[swap_rows, 0, :], con[swap_rows, P:P + 2 * T], MUL))
                dve.tensor_tensor(q_f[rope_rows, :], rope_a[rope_rows, :], rope_b[rope_rows, :],
                                  ADD).then_inc(q_roped, 1)
                dve.wait_ge(q_hi_done, r + 1)
                dve.tensor_tensor(q_lo[0:NOPE + ROPE, :], q_f[0:NOPE + ROPE, :], q_hi[0:NOPE + ROPE, :].bitcast(f32),
                                  SUB).then_inc(q_lo_done, 1)

            projected_lo(0)
            for r in range(PAIRS):
                for n in range(4 * r, 4 * r + 4):
                    dve.wait_ge(scored, n + 1)
                    settle(dve.reduce_max(stat[:, 2, n:n + 1], psum[:, 4 + n % 4, :], AX.X))
                    dve.tensor_scalar(stat[:, 0, n:n + 1], stat[:, 2, n:n + 1], -ATTN_SCALE, None,
                                      MUL).then_inc(neg_max, 1)
                for a in range(2):
                    for qt in range(2):
                        n = 4 * r + 2 * a + qt
                        dve.wait_ge(exp_done, n + 1)
                        settle(dve.reciprocal(stat[:, 3, n:n + 1], stat[:, 1, n:n + 1]))
                        dve.tensor_scalar(probs[a][:, qt, :], probs[a][:, qt, :], stat[:, 3, n:n + 1], None,
                                          MUL).then_inc(p_normal, 1)
                for a in range(2):
                    turned_lo(dve, r, a)
                if r + 1 < PAIRS:
                    projected_lo(r + 1)
                dve.wait_ge(attn_hi_done, 2 * r + 2)
                for a in range(2):
                    rows = slice(a * VD, a * VD + VD)
                    last = dve.tensor_tensor(mix_lo[rows, 4 + r, :], psum[rows, 3, a * T:a * T + T],
                                             mix_hi[rows, 4 + r, :].bitcast(f32), SUB)
                last.then_inc(attn_lo_done, 1)
            for g in range(4):
                dve.wait_ge(pool_hi_done, 4)
                dve.scalar_tensor_tensor(mix_lo[:, g, :], psum[:, 5 + g // 2, (g % 2) * T:(g % 2) * T + T],
                                         col("pool_scale", g), mix_hi[:, g, :].bitcast(f32), MUL,
                                         SUB).then_inc(pool_lo_done, 1)
            gather(4)
            modulate(4)

            sum_mod(18, 1)
            dve.wait_ge(multiplied, PASS[2] + 2)
            hidden_product(2 * STEPS)
            hidden_low(2 * STEPS)
            ffn_steps(2, 1, STEPS - 1, mod=(19, 1, 15))
            write_mod(25, 28, 1)
            dve.wait_ge(mod_written, 26)
            gather(5)
            modulate(5)
            dve.wait_ge(multiplied, PASS[3] + 2)
            hidden_product(3 * STEPS)
            hidden_low(3 * STEPS)
            sum_mod(29, 1)
            split_step(dve, split_lo, hidden_product, hidden_low, PASS[3] + 2, 3 * STEPS + 1)
            ffn_steps(3, 2, 6, mod=(30, 1, 26))
            write_mod(32, 35, 1)
            dve.wait_ge(mod_written, 33)
            ffn_steps(3, 8, STEPS - 8)
            gather(6)
            modulate(6)

            dve.wait_ge(u_lo_done, 7 * KT)
            settle(dve.memset(z_pad[:, :, :], 0.0))
            with dve.Fori(0, KT // 2) as i:
                dve.wait_ge(c_copied, i + 1)
                dve.wait_ge(multiplied, i * RING + (CONV + 2))
                dve.tensor_tensor(z_pad[:, :, 1:1 + T], silu[:, :].rearrange("p (a t) -> p a t", a=2),
                                  psum[:, UP, :].rearrange("p (a t) -> p a t", a=2), MUL).then_inc(z_done, 1)
                dve.wait_ge(z_done, i + 1)

                def tap(a, d):
                    return par[:, bass.ds(i * 6 + (PARAM["conv_w"] + 3 * a + d), 1)]

                for a in range(2):
                    dve.tensor_scalar(conv_1[:, a, :], z_pad[:, a, 0:T], tap(a, 0), None, MUL).then_inc(mod_step, 1)
                base = mod_steps_before(2 * HALVES)
                for d, src, dst in ((1, conv_1, conv_2), (2, conv_2, conv_1)):
                    for a in range(2):
                        dve.wait_ge(mod_step, i * 6 + (base + 2 * d - 1 + a))
                        dve.scalar_tensor_tensor(dst[:, a, :], z_pad[:, a, d:d + T], tap(a, d), src[:, a, :],
                                                 MUL, ADD).then_inc(mod_step, 1)
                dve.wait_ge(mod_step, i * 6 + (base + 6))
                dve.wait_ge(multiplied, i * RING + (CONV + 3))
                dve.tensor_tensor(prod[:, :].rearrange("p (a t) -> p a t", a=2), conv_1[:, :, :],
                                  psum[:, 6, :].rearrange("p (a t) -> p a t", a=2), MUL).then_inc(conv_done, 1)
                dve.wait_ge(conv_hi_done, i + 1)
                at = bass.ds(i * 2, 2)
                dve.tensor_tensor(mix_lo[:, at, :], prod[:, :].rearrange("p (a t) -> p a t", a=2),
                                  mix_hi[:, at, :].bitcast(f32), SUB).then_inc(conv_lo_done, 1)
            gather(7)
            modulate(7)

            dve.wait_ge(multiplied, PASS[4] + 2)
            hidden_product(4 * STEPS)
            hidden_low(4 * STEPS)
            b = PASS[4]
            with dve.Fori(0, STEPS - 2) as i:
                for j in (5, 6):
                    if (b + j) % RING == 1:
                        split_lo(b + j, i)
                dve.wait_ge(multiplied, i * RING + (b + 5))
                hidden_product(i + (STEPS * 4 + 1))
                hidden_low(i + (STEPS * 4 + 1))
                if (b + 7) % RING == 1:
                    split_lo(b + 7, i)
            if (b + 32) % RING == 1:
                split_lo(b + 32)
            dve.wait_ge(multiplied, b + 32)
            hidden_product(STEPS * 5 - 1)
            hidden_low(STEPS * 5 - 1)
            gather(8)
            modulate(8)

        @block.gpsimd
        def _(pool):
            steps = [0]

            def settle(ins):
                steps[0] += 1
                ins.then_inc(pool_step, 1)
                pool.wait_ge(pool_step, steps[0])

            def split_lo(n, i=0):
                slot, uses = ring(n, i)
                pool.wait_ge(hi_ready, i * RING + (n + 1))
                pool.tensor_tensor(w_lo[:, slot, :], raw[:, slot, :], w_hi[:, slot, :].bitcast(f32),
                                   SUB).then_inc(lo_ready[slot], 1)

            def pass_lo(p, bodies=STEPS - 1):
                split_lo(PASS[p] + 3)
                split_lo(PASS[p] + 4)
                with pool.Fori(0, bodies) as i:
                    for n in range(PASS[p] + 5, PASS[p] + 8):
                        if n % RING != 1:
                            split_lo(n, i)

            for n in range(RING):
                split_lo(n)
            pass_lo(0)
            split_lo(PASS[1] + 2)
            pass_lo(1)
            pool.wait_ge(mod_step, mod_steps_before(HALVES))
            pool.memset(pad_x[:, :, :], 0.0).then_inc(pad_zeroed, 1)
            for n in range(MIX + 2, MIX + 7):
                split_lo(n)
            pool.wait_ge(pool_copied, 2)
            settle(pool.tensor_tensor(win2[:, :, 1:PW], pad_x[:, :, 0:PW - 1], pad_x[:, :, 1:PW], ADD))
            settle(pool.tensor_tensor(win4[:, :, 2:PW - 1], win2[:, 1:4, 1:PW - 2], win2[:, 1:4, 3:PW], ADD))
            settle(pool.tensor_tensor(win8[:, :, 4:PW - 3], win4[:, 1:3, 2:PW - 5], win4[:, 1:3, 6:PW - 1], ADD))
            settle(pool.tensor_tensor(win16[:, :, 8:PW - 7], win8[:, 1:2, 4:PW - 11], win8[:, 1:2, 12:PW - 3], ADD))
            pool.wait_ge(inv_in, 16)
            inner = slice(PAD, PAD + T)
            for g, w in enumerate((win2[:, 0, :], win4[:, 0, :], win8[:, 0, :], win16[:, 0, :])):
                last = pool.tensor_tensor(win2[:, g, inner], w[:, inner], inv_cnt[:, g, :], MUL)
            settle(last)
            pool.tensor_tensor(win2[:, :, inner], win2[:, :, inner], pad_x[:, :, inner], SUB).then_inc(pooled, 1)
            for n in range(MIX + 7, MIX + 10):
                split_lo(n)
            pool.wait_ge(p_hi_done, 1)
            pool.tensor_tensor(p_lo[:, :, :], win2[:, :, inner], p_hi[:, :, :].bitcast(f32), SUB).then_inc(p_lo_done, 1)
            for n in range(MIX + 10, MIX + 19):
                split_lo(n)
            pass_lo(2)
            split_lo(PASS[3] + 2)
            pass_lo(3)
            for n in range(CONV + 2, CONV + 6):
                split_lo(n)
            with pool.Fori(0, 3) as i:
                for j in range(RING):
                    split_lo(CONV + 6 + j, i)
            for n in range(CONV + 15, CONV + 19):
                split_lo(n)
            pass_lo(4, STEPS - 2)
            if (PASS[4] + 32) % RING != 1:
                split_lo(PASS[4] + 32)

        @block.tensor
        def _(pe):
            def three(out, w_at, x_at, first, last, shared=False, start=None):
                begin = first if start is None else start
                pe.matmul(out, w_at[0], x_at[0], start=begin, stop=False, skip_group_check=shared)
                pe.matmul(out, w_at[0], x_at[1], start=False, stop=False, skip_group_check=shared)
                return pe.matmul(out, w_at[1], x_at[0], start=False, stop=last, skip_group_check=shared)

            def weights(slot, at):
                return w_hi[:, slot, at:at + P], w_lo[:, slot, at:at + P]

            def arrived(n, i=0):
                slot, uses = ring(n, i)
                pe.wait_ge(lo_ready[slot], uses)
                return slot

            def stream_in(k, who, width=T):
                at = slice(who * T, who * T + width)
                return u_hi[:, k, at], u_lo[:, k, at]

            def project(n, bank, who, i=0, fresh=None):
                slot = arrived(n, i)
                if fresh is None:
                    for a in range(2):
                        for k in range(KT):
                            last = three(psum[:, bank, a * T:a * T + T], weights(slot, k * 256 + a * P),
                                         stream_in(k, who), k == 0, k == KT - 1)
                else:
                    for k in range(KT):
                        pe.wait_ge(u_lo_done, KT * fresh + k + 1)
                        for a in range(2):
                            last = three(psum[:, bank, a * T:a * T + T], weights(slot, k * 256 + a * P),
                                         stream_in(k, who), k == 0, k == KT - 1, True, k == 0 and a == 0)
                last.then_inc(multiplied, 1)

            def down(n, i=0, signal=False):
                slot = arrived(n, i)
                for j in range(KT):
                    for a in range(2):
                        last = three(psum[:, j // 2, (j % 2) * T:(j % 2) * T + T], weights(slot, a * D + j * P),
                                     (hid_hi[:, a * T:a * T + T], hid_lo[:, a * T:a * T + T]),
                                     False, signal and a == 1, True)
                    if signal and j % 2 == 1 and j < KT - 1:
                        last.then_inc(acc_ready, 1)
                last.then_inc(multiplied, 1)

            def clear_acc():
                for j in range(4):
                    for a in range(2):
                        pe.matmul(psum[:, j, a * T:a * T + T], zeros[:, 0:P], zeros[:, :], start=a == 0, stop=False,
                                  skip_group_check=True)

            def sum_squares(e):
                for j in range(KT):
                    if j % 2 == 0:
                        pe.wait_ge(sq_done, 4 * e + j // 2 + 1)
                    last = pe.matmul(psum[:, SSQ, 0:T], ones[:, :], scratch[:, j, :], start=j == 0, stop=j == KT - 1)
                last.then_inc(ssq_done, 1)

            def reduce_mod(half, conds, i=0):
                pe.wait_ge(mod_step, i * mod_ops(half) + mod_steps_before(half + 1))
                for c in range(conds):
                    for k in range(4):
                        last = pe.transpose(psum[:, MODB + c, k * P:k * P + P], mod_acc[:, c, k * P:k * P + P], con[:, 0:P])
                last.then_inc(mod_reduced, 1)

            def ffn_step0(p, who, fresh=None):
                b = PASS[p]
                project(b, GATE, who, fresh=fresh)
                project(b + 1, UP, who)

            def ffn_steps(p, who, first, count, mod=None):
                b = PASS[p] + 2 + 3 * (first - 1)
                with pe.Fori(0, count) as i:
                    pe.wait_ge(silu_done, i + (STEPS * p + first))
                    project(b, GATE, who, i)
                    pe.wait_ge(hid_lo_done, i + (STEPS * p + first))
                    down(b + 1, i)
                    project(b + 2, UP, who, i)
                    if mod is not None:
                        reduce_mod(mod[0], mod[1], i)

            def ffn_end(p, e):
                pe.wait_ge(hid_lo_done, STEPS * (p + 1))
                down(PASS[p] + FFN_CHUNKS - 1, signal=True)

            pe.wait_ge(consts_set, 3)
            pe.wait_ge(cond_ready, 1)
            for half in range(START_HALVES):
                for kh in range(2):
                    pe.wait_ge(mod_arrived[kh], 16 * (half + 1))
                    for k in range(4):
                        last = pe.matmul(psum[0:2, half, :], cond[:, kh * 4 + k, :], mod_raw[:, kh, k, :],
                                         start=kh == 0 and k == 0, stop=kh == 1 and k == 3)
                    last.then_inc(mod_used[kh], 1)
                if half == 0:
                    sum_squares(0)
            pe.wait_ge(params_in, 32)
            for half in range(START_HALVES):
                pe.wait_ge(start_rows, half + 1)
                for k in range(4):
                    at = half * 8 + 2 * k
                    last = pe.transpose(psum[:, MODB, at:at + 2], start_row[:, half, k * P:k * P + P], con[0:2, 0:2])
            last.then_inc(start_turned, 1)

            ffn_step0(0, 0, fresh=0)
            sum_squares(1)
            clear_acc()
            pe.wait_ge(std_done, 2)
            reduce_mod(4, 2)
            ffn_steps(0, 0, 1, STEPS - 1, mod=(5, 2))
            ffn_end(0, 2)
            pe.wait_ge(u_lo_done, 2 * KT)
            ffn_step0(1, 1)
            sum_squares(2)
            clear_acc()
            ffn_steps(1, 1, 1, 3, mod=(15, 2))
            ffn_steps(1, 1, 4, STEPS - 4)
            ffn_end(1, 3)

            pe.wait_ge(u_lo_done, 3 * KT)
            project(MIX, 4, 0)
            sum_squares(3)
            project(MIX + 1, 5, 0)
            project(MIX + 2, 2, 0)
            project(MIX + 3, 3, 0)
            pe.wait_ge(u_lo_done, 4 * KT)
            slot = arrived(MIX + 4)
            for a, bank in enumerate((6, 0)):
                for k in range(KT):
                    last = three(psum[:, bank, :], weights(slot, k * 256 + a * P), stream_in(k, 0, 2 * T),
                                 k == 0, k == KT - 1)
            last.then_inc(multiplied, 1)
            slot = arrived(MIX + 5)
            for k in range(KT):
                last = three(psum[:, 1, :], weights(slot, k * P), stream_in(k, 0, 2 * T), k == 0, k == KT - 1)
            last.then_inc(multiplied, 1)
            pe.wait_ge(pool_copied, 2)
            pe.wait_ge(kv_sq_done, 2)
            for i in range(KVR):
                last = pe.matmul(psum[:, 5, :], ones[:, :], ckv_sq[:, i, :], start=i == 0, stop=i == KVR - 1)
            last.then_inc(kv_ssq_done, 1)
            project(MIX + 6, 4, 0)
            for i in range(QR):
                if i % 2 == 0:
                    pe.wait_ge(q_sq_done, i // 2 + 1)
                last = pe.matmul(psum[:, 6, 0:T], ones[:, :], cq_sq[:, i, :], start=i == 0, stop=i == QR - 1)
            last.then_inc(q_ssq_done, 1)

            def project_pair(r):
                slot = arrived(MIX + 7 + r)
                kv_at = QR * 256
                if r == 0:
                    pe.wait_ge(kr_done, 1)
                    pe.wait_ge(kv_lo_done, KVR)
                else:
                    pe.wait_ge(k_lo_done, 2 * r)
                for a in range(2):
                    for k in range(KVR):
                        last = three(psum[:, 1 + a, :], weights(slot, kv_at + k * 256 + a * P),
                                     (kvn_hi[:, k, :], kvn_lo[:, k, :]), k == 0, k == KVR - 1)
                    last.then_inc(k_proj, 1)
                if r > 1:
                    pe.wait_ge(attn_lo_done, r - 1)
                for t in range(4):
                    for k in range(KVR):
                        at = kv_at + k * 256
                        cols = [w[:, slot, at:at + 256].rearrange("p (a d) -> p a d", a=2)[:, :, NOPE:NOPE + VD]
                                for w in (w_hi, w_lo)]
                        rows = [w[:, k, t * P:t * P + P] for w in (kvn_hi, kvn_lo)]
                        last = three(psum[:, 3, t * P:t * P + P].rearrange("p (a d) -> p a d", a=2), rows, cols,
                                     k == 0, k == KVR - 1)
                last.then_inc(v_proj, 1)
                if r > 0:
                    pe.wait_ge(q_lo_done, r)
                for a in range(2):
                    for k in range(QR):
                        if r == 0 and a == 0:
                            pe.wait_ge(qn_lo_done, k + 1)
                        last = three(psum[:, 0, a * T:a * T + T], weights(slot, k * 256 + a * P),
                                     (qn_hi[:, k, :], qn_lo[:, k, :]), k == 0, k == QR - 1)
                last.then_inc(multiplied, 1)

            def score_pair(r):
                rows = slice(0, NOPE + ROPE)
                pe.wait_ge(q_lo_done, r + 1)
                if r == 0:
                    pe.wait_ge(kr_lo_done, 2)
                else:
                    pe.wait_ge(pt_lo_done, 4 * r)
                for a in range(2):
                    pe.wait_ge(k_lo_done, 2 * r + a + 1)
                    for qt in range(2):
                        at = slice(a * T + qt * P, a * T + qt * P + P)
                        last = three(psum[:, 4 + 2 * a + qt, :], (q_hi[rows, at], q_lo[rows, at]),
                                     (k_hi[rows, a, :], k_lo[rows, a, :]), True, True)
                        last.then_inc(scored, 1)

            def attend_pair(r):
                for a in range(2):
                    pe.wait_ge(p_normal, 4 * r + 2 * a + 2)
                    for b in range(2):
                        for kt in range(2):
                            for qt in range(2):
                                at = kt * T + qt * P
                                key = (2 * b + kt) * P
                                last = pe.transpose(psum[:, 4 + 2 * a + b, at:at + P], probs[a][:, qt, key:key + P],
                                                    con[:, 0:P])
                        last.then_inc(p_turned, 1)
                pe.wait_ge(v_lo_done, min(r + 2, PAIRS))
                for a in range(2):
                    for kt in range(4):
                        pe.wait_ge(pt_lo_done, 4 * r + 2 * a + kt // 2 + 1)
                        last = three(psum[:, 3, a * T:a * T + T],
                                     (v_hi[:, r % 2, kt * P:kt * P + P], v_lo[:, r % 2, kt * P:kt * P + P]),
                                     (pt_hi[:, a, kt, :], pt_lo[:, a, kt, :]), kt == 0, kt == 3)
                last.then_inc(pv_done, 1)

            project_pair(0)
            score_pair(0)
            for r in range(PAIRS):
                if r + 1 < PAIRS:
                    project_pair(r + 1)
                attend_pair(r)
                if r + 1 < PAIRS:
                    score_pair(r + 1)

            slot = arrived(MIX + 11)
            pe.wait_ge(p_lo_done, 1)
            for g in range(4):
                last = three(psum[:, 5 + g // 2, (g % 2) * T:(g % 2) * T + T], weights(slot, g * P),
                             (p_hi[:, g, :], p_lo[:, g, :]), True, True)
            last.then_inc(multiplied, 1)

            def project_out(base, e, order):
                for i in range(4):
                    slot = arrived(base + i)
                    for a in range(2):
                        for k in order:
                            if e == 4 and i == 0 and a == 0 and k < 4:
                                pe.wait_ge(pool_lo_done, k + 1)
                            last = three(psum[:, i, a * T:a * T + T], weights(slot, k * 256 + a * P),
                                         (mix_hi[:, k, :], mix_lo[:, k, :]), k == order[0], k == order[-1])
                    last.then_inc(multiplied, 1)

            pe.wait_ge(attn_lo_done, 4)
            project_out(MIX + 12, 4, [4, 5, 6, 7, 0, 1, 2, 3])
            sum_squares(4)

            ffn_step0(2, 0, fresh=4)
            clear_acc()
            reduce_mod(18, 1)
            ffn_steps(2, 0, 1, STEPS - 1, mod=(19, 1))
            ffn_end(2, 5)
            sum_squares(5)
            ffn_step0(3, 0, fresh=5)
            clear_acc()
            ffn_steps(3, 0, 1, 7, mod=(29, 1))
            ffn_steps(3, 0, 8, STEPS - 8)
            ffn_end(3, 6)
            sum_squares(6)

            pe.wait_ge(u_lo_done, 7 * KT)
            for k, bank in enumerate((GATE, UP, 6)):
                project(CONV + k, bank, 0)
            with pe.Fori(0, KT // 2 - 1) as i:
                pe.wait_ge(c_copied, i + 1)
                project(CONV + 3, GATE, 0, i)
                pe.wait_ge(z_done, i + 1)
                project(CONV + 4, UP, 0, i)
                pe.wait_ge(conv_done, i + 1)
                project(CONV + 5, 6, 0, i)
            pe.wait_ge(conv_lo_done, KT // 2)
            project_out(CONV + 12, 7, list(range(KT)))
            sum_squares(7)
            ffn_step0(4, 0, fresh=7)
            clear_acc()
            ffn_steps(4, 0, 1, STEPS - 1)
            ffn_end(4, 8)
            sum_squares(8)


def _tiles(a):
    return a.reshape(a.shape[0] // P, P, a.shape[1]).transpose(1, 0, 2)


def _ffn_chunks(gate, up, down):
    gate, up, down = _tiles(gate), _tiles(up), _tiles(down)
    g = [gate[:, :, 256 * s:256 * s + 256].reshape(P, CH) for s in range(STEPS)]
    u = [up[:, :, 256 * s:256 * s + 256].reshape(P, CH) for s in range(STEPS)]
    d = [down[:, 2 * s:2 * s + 2, :].reshape(P, CH) for s in range(STEPS)]
    order = [g[0], u[0]]
    for s in range(1, STEPS):
        order += [g[s], d[s - 1], u[s]]
    return order + [d[-1]]


def _column_chunks(w):
    w = _tiles(w)
    return [np.ascontiguousarray(w[:, :, c:c + 256]).reshape(P, CH) for c in range(0, w.shape[2], 256)]


def _padded(w):
    w = w.reshape(P, -1)
    return np.concatenate([w, np.zeros((P, CH - w.shape[1]), w.dtype)], axis=1)


def _swap(w):
    return np.concatenate([w[..., 8:16], w[..., 0:8], w[..., 24:32], w[..., 16:24]], axis=-1)


def kernel(**inputs):
    import concourse.bacc as _bacc
    from concourse.bass_utils import run_bass_kernel_spmd as _run

    a = {k: np.asarray(v) for k, v in inputs.items()}
    w_in = a["ab_w_in"][0]
    pool_in, cq_in, ckv_in, kr_in = w_in[:, 0:512], w_in[:, 512:1280], w_in[:, 1280:1536], w_in[:, 1536:1568]
    kr = _tiles(np.concatenate([np.zeros((D, NOPE), w_in.dtype), kr_in, _swap(kr_in)], axis=1))
    w_uq = a["w_uq"][0].reshape(QR * P, HEADS, NOPE + ROPE)
    w_uq = np.concatenate([w_uq, _swap(w_uq[:, :, NOPE:])], axis=2)
    w_ukv = a["w_ukv"][0].reshape(KVR * P, HEADS, NOPE + VD)
    heads = []
    for r in range(PAIRS):
        q = _tiles(w_uq[:, 2 * r:2 * r + 2].reshape(QR * P, 256)).reshape(P, QR * 256)
        kv = _tiles(w_ukv[:, 2 * r:2 * r + 2].reshape(KVR * P, 256)).reshape(P, KVR * 256)
        heads.append(np.concatenate([q, kv], axis=1))
    b_c_val = [_column_chunks(a["conv_w_in"][0][:, D * m:D * m + D]) for m in range(3)]
    chunks = _ffn_chunks(a["ffn_w_gate"][0, 0], a["ffn_w_up"][0, 0], a["ffn_w_down"][0, 0])
    cq_chunks = _column_chunks(cq_in)
    chunks += _column_chunks(pool_in) + cq_chunks[:2] + _column_chunks(ckv_in) + [_padded(kr)] + cq_chunks[2:] + heads
    chunks += [_padded(a["pool_w"][0].transpose(1, 0, 2))] + _column_chunks(a["ab_w_out"][0])
    chunks += _ffn_chunks(a["ffn_w_gate"][0, 1], a["ffn_w_up"][0, 1], a["ffn_w_down"][0, 1])
    chunks += _ffn_chunks(a["ffn_w_gate"][1, 0], a["ffn_w_up"][1, 0], a["ffn_w_down"][1, 0])
    for i in range(4):
        chunks += [b_c_val[1][i], b_c_val[2][i], b_c_val[0][i]]
    chunks += _column_chunks(a["conv_w_out"][0])
    chunks += _ffn_chunks(a["ffn_w_gate"][1, 1], a["ffn_w_up"][1, 1], a["ffn_w_down"][1, 1])
    stream = np.stack(chunks)
    w_mod = a["w_mod"].reshape(LAYERS, 2, 4, P, HALVES, HALF).transpose(0, 4, 1, 3, 2, 5)
    w_mod = np.ascontiguousarray(w_mod).reshape(LAYERS * HALVES * 2, P, 4, HALF)

    def feature_major(x):
        return np.ascontiguousarray(x.reshape(T, KT, P).transpose(2, 1, 0))

    def columns(v):
        return v.reshape(-1, P).T

    cond = np.stack([a["c"][0], a["c_ctx"]]).reshape(2, KT, P).transpose(2, 1, 0).reshape(P, 2 * KT)
    conv_w = a["conv_w"][0].reshape(3, KT, P).transpose(2, 1, 0).reshape(P, 3 * KT)
    params = np.ascontiguousarray(np.concatenate(
        [columns(a["norm_g"]), columns(a["b_mod"]), columns(a["pool_scale"]), columns(a["q_norm_g"]),
         columns(a["kv_norm_g"]), conv_w, columns(a["final_norm_g"]), cond], axis=1))

    f = np.float32
    freqs = np.power(f(10000.0), -np.arange(0, 16, 2, dtype=f) / f(16))
    token = np.arange(T)
    table = np.zeros((P, T), f)
    for d in range(ROPE):
        pos = (token // 64 if d < 16 else token % 64).astype(f)
        angle = (pos * freqs[d % 8]).astype(f)
        table[NOPE + d] = np.cos(angle)
        table[NOPE + ROPE + d] = np.sin(angle) if d % 16 >= 8 else -np.sin(angle)
    consts = np.ascontiguousarray(np.concatenate([np.eye(P, dtype=f), table, table], axis=1))
    inv = np.zeros((4, T), f)
    for g, w in enumerate(WINDOWS):
        lo, hi = np.clip(token - w // 2, 0, T - 1), np.clip(token + (w - w // 2 - 1), 0, T - 1)
        inv[g] = f(1) / (hi - lo + 1).astype(f)
    inv = np.ascontiguousarray(np.broadcast_to(inv, (P, 4, T)))

    nc = _bacc.Bacc("TRN2", target_bir_lowering=False, num_devices=1)
    arrays = {"in_stream": stream, "in_w_mod": w_mod, "in_x": feature_major(a["x"][0]),
              "in_ctx": feature_major(a["ctx"][0]), "in_params": params, "in_consts": consts, "in_inv": inv}
    aps = [nc.dram_tensor(k, v.shape, mybir.dt.from_np(v.dtype), kind="ExternalInput").ap() for k, v in arrays.items()]
    result = nc.dram_tensor("out_h", (P, KT, T), mybir.dt.float32, kind="ExternalOutput").ap()
    build(nc, *aps, result)
    got = _run(nc, [arrays], core_ids=[0]).results[0]["out_h"]
    return np.ascontiguousarray(got.transpose(2, 1, 0)).reshape(1, T, D)
```

```python
import numpy as np
import concourse.bass as bass
from concourse import mybir
from contextlib import ExitStack

D, T, FF = 1024, 256, 2816
P = 128
KT = D // P
STEPS = FF // (2 * P)
BLOCK = 3
CH = 2048
RING = 3
MIX_CHUNKS, CONV_CHUNKS = 16, 16
HEADS, NOPE, ROPE, VD = 8, 64, 32, 64
QR, KVR = 768 // P, 256 // P
PAIRS = HEADS // 2
EPS = 1e-6
ATTN_SCALE = 1.0 / float(np.sqrt(NOPE + ROPE))
WINDOWS = (2, 4, 8, 16)
PAD = 8
PW = T + 2 * PAD
LAYERS, NMOD = 2, 9
HALVES = 2 * NMOD
HALF = 512

PARAM = {}
_at = 0
for _name, _n in (("norm_g", LAYERS * 3 * KT), ("b_mod", LAYERS * NMOD * KT), ("pool_scale", 4), ("q_norm_g", QR),
                  ("kv_norm_g", KVR), ("conv_w", 3 * KT), ("final_norm_g", KT), ("cond", 2 * KT)):
    PARAM[_name] = _at
    _at += _n
N_PARAM = _at

PASS = [0, 49, 82, 131]
MIX, CONV = 33, 115
N_CHUNKS = 164
START_HALVES = 4
MOD = {0: (4, 1, (0, 1, 2, 3, 4)), 1: (20, 2, (1, 4)), 2: (28, 2, (1, 4)), 3: (36, 0, ())}
BOTH = MOD[1][0]
TAKEN = {0: 1, "mix": 33, 1: 41, 2: 73, "conv": 105, 3: 113}


def mod_slot(p, position):
    first, ahead, positions = MOD[p]
    return first + ahead + positions.index(position), len(positions)


def ring(n, i=0):
    return n % RING, i + (n // RING + 1)


def conditions(half):
    return 2 if half < BOTH else 1


def mod_ops(half):
    return conditions(half) * KT


def mod_steps_before(half):
    return sum(mod_ops(h) for h in range(START_HALVES, half))


def build(nc, stream, w_mod, x_h, x_g, params, consts, inv_count, out):
    f32, f32r = mybir.dt.float32, mybir.dt.float32r
    ALU, ACT, AX = mybir.AluOpType, mybir.ActivationFunctionType, mybir.AxisListType
    ADD, SUB, MUL = ALU.add, ALU.subtract, ALU.mult
    place = [16512]

    def sb(name, shape, dt, at=None):
        size = 4 * int(np.prod(shape[1:]))
        if at is None:
            at = place[0]
            place[0] += (size + 31) // 32 * 32
        t = nc.alloc_sbuf_tensor_at(name, shape, dt, offset=at)
        where[name] = at
        return t

    where = {}
    raw = sb("raw", [P, RING, CH], f32)
    w_hi = sb("w_hi", [P, RING, CH], f32r)
    w_lo = sb("w_lo", [P, RING, CH], f32r)
    mod_raw = sb("mod_raw", [P, 2, 4, HALF], f32)
    resid = sb("resid", [P, 2, KT, T], f32)
    mod_acc = sb("mod_acc", [P, 2, HALF], f32)
    u_hi = sb("u_hi", [P, KT, 2 * T], f32r)
    u_lo = sb("u_lo", [P, KT, 2 * T], f32r)
    scratch = sb("scratch", [P, KT, T], f32)
    silu = sb("silu", [P, 4 * T], f32)
    prod = sb("prod", [P, 4 * T], f32)
    mix_hi = sb("mix_hi", [P, KT, T], f32r)
    mix_lo = sb("mix_lo", [P, KT, T], f32r)
    kvn_hi = sb("kvn_hi", [P, KVR, 2 * T], f32r)
    kvn_lo = sb("kvn_lo", [P, KVR, 2 * T], f32r)
    region_q = sb("cq", [P, 10 * T], f32)
    region_kv = sb("ckv_region", [P, 8 * T], f32)
    std = sb("std", [P, T], f32)
    rstd = sb("rstd", [P, T], f32)
    par = sb("par", [P, N_PARAM], f32)
    con = sb("con", [P, P + 2 * T], f32)
    ones = sb("ones", [P, P], f32)
    mod_out = sb("mod_out", [P, LAYERS * NMOD * KT, 2], f32)
    gain_scale = sb("gain_scale", [P, KT], f32)
    cond = sb("cond", [P, KT, 2], f32)
    eps = sb("eps", [P, 1], f32)
    table = sb("table", [P, 2], f32)
    stat = sb("stat", [P, 4, 16], f32)
    mod_sum = sb("mod_sum", [P, 4, 2], f32)
    assert place[0] <= nc.sbuf_usable_end, place[0]

    hid_hi = sb("hid_hi", [P, 2 * BLOCK, 2 * T], f32r, where["mix_hi"])
    hid_lo = sb("hid_lo", [P, 2 * BLOCK, 2 * T], f32r, where["mix_hi"] + 16 * BLOCK * T)
    start_mod = [sb(f"start_mod{n}", [P, 4, HALF], f32, at) for n, at in enumerate(
        [where["mod_raw"], where["mod_raw"] + 16 * HALF, where["mix_hi"], where["mix_hi"] + 16 * HALF,
         where["mix_hi"] + 32 * HALF, where["cq"], where["ckv_region"]])]
    start_mod.append(start_mod[1])
    cq = region_q[:, 0:QR * T].rearrange("p (k t) -> p k t", k=QR)
    q_f = sb("q_f", [P, 2 * T], f32, where["cq"])
    rope_a = sb("rope_a", [P, 2 * T], f32, where["cq"] + 8 * T)
    rope_b = sb("rope_b", [P, 2 * T], f32, where["cq"] + 16 * T)
    q_hi = sb("q_hi", [P, 2 * T], f32r, where["cq"] + 24 * T)
    q_lo = sb("q_lo", [P, 2 * T], f32r, where["cq"] + 32 * T)
    ckv = region_kv[:, 0:4 * T].rearrange("p (k t) -> p k t", k=KVR)
    ckv_sq = region_kv[:, 4 * T:8 * T].rearrange("p (k t) -> p k t", k=KVR)
    k_hi = sb("k_hi", [P, 2, 2 * T], f32r, where["ckv_region"])
    k_lo = sb("k_lo", [P, 2, 2 * T], f32r, where["ckv_region"] + 16 * T)
    context_sq = sb("context_sq", [P, KT, T], f32, where["mix_hi"])
    cq_sq = sb("cq_sq", [P, QR, T], f32, where["mix_hi"])
    inv_cnt = sb("inv_cnt", [P, 4, T], f32, where["mix_lo"])
    kv_std = sb("kv_std", [P, 2 * T], f32, where["scratch"])
    kv_rstd = sb("kv_rstd", [P, 2 * T], f32, where["scratch"] + 8 * T)
    kr_f = sb("kr_f", [P, 2 * T], f32, where["scratch"] + 16 * T)
    v_hi = sb("v_hi", [P, 2, 2 * T], f32r, where["scratch"])
    v_lo = sb("v_lo", [P, 2, 2 * T], f32r, where["scratch"] + 16 * T)
    qn_hi = sb("qn_hi", [P, QR, T], f32r, where["resid"] + 4 * KT * T)
    qn_lo = sb("qn_lo", [P, QR, T], f32r, where["resid"] + 4 * KT * T + 4 * QR * T)
    probs = [sb("probs0", [P, 2, 2 * T], f32, where["u_hi"]),
             sb("probs1", [P, 2, 2 * T], f32, where["u_hi"] + 16 * T)]
    pt_hi = sb("pt_hi", [P, 2, 4, T], f32r, where["u_lo"])
    pt_lo = sb("pt_lo", [P, 2, 4, T], f32r, where["u_lo"] + 32 * T)
    pad_x = sb("pad_x", [P, 4, PW], f32, where["mod_raw"])
    win2 = sb("win2", [P, 4, PW], f32, where["mod_raw"] + 16 * PW)
    win4 = sb("win4", [P, 3, PW], f32, where["mod_raw"] + 32 * PW)
    win8 = sb("win8", [P, 2, PW], f32, where["mod_raw"] + 44 * PW)
    win16 = sb("win16", [P, 1, PW], f32, where["mod_raw"] + 52 * PW)
    start_row = sb("start_row", [2, 4, HALF], f32, where["silu"])
    p_hi = sb("p_hi", [P, 4, T], f32r, where["silu"])
    p_lo = sb("p_lo", [P, 4, T], f32r, where["silu"] + 16 * T)
    z_pad = sb("z_pad", [P, 2, T + 2], f32, where["scratch"])
    conv_1 = sb("conv_1", [P, 2, T], f32, where["scratch"] + 3072)
    conv_2 = sb("conv_2", [P, 2, T], f32, where["scratch"] + 5120)

    def col(name, k=0, n=1):
        return par[:, PARAM[name] + k:PARAM[name] + k + n]

    def shift(layer, kind, c, k=0, n=1, which=0):
        at = layer * NMOD * KT + (3 * kind + which) * KT + k
        return mod_out[:, at:at + n, c]

    JOINS = [(0, (0, 0)), (1, (0, 0)), (0, (0, 1)), (1, (0, 1)), (0, (0, 2)), (0, (1, 0)), (0, (1, 1)), (0, (1, 2)),
             (0, None)]
    RESULT = {2: 33, 3: 33, 4: 41, 5: 73, 6: 105, 7: 113, 8: 145}
    SQUARED = ((0, 2), (2, 4), (4, 6), (6, 7), (7, 8))
    KIND = [(0, 0), (0, 2), (1, 0), (1, 2)]
    ctx = ExitStack()
    with ctx:
        psum = ctx.enter_context(nc.psum_tensor("psum", [P, 8, 512], f32))
        F_GATE, F_UP, MODB, SSQ = 0, 2, 6, 7
        DOWN = (4, 5, 0, 1, 2, 3, 4, 5)
        GATE, UP = 4, 5

        def sem(name):
            return ctx.enter_context(nc.semaphore(name))

        raw_arrived = [sem(f"raw_arrived{s}") for s in range(RING)]
        hi_ready = sem("hi_ready")
        lo_ready = [sem(f"lo_ready{s}") for s in range(RING)]
        multiplied = sem("multiplied")
        mod_arrived = [sem("mod_arrived0"), sem("mod_arrived1")]
        start_arrived = [sem(f"start_arrived{n}") for n in range(2 * START_HALVES)]
        start_used = sem("start_used")
        start_rows, start_turned = sem("start_rows"), sem("start_turned")
        mod_reduced, mod_summed = sem("mod_reduced"), sem("mod_summed")
        mod_written = sem("mod_written")
        inputs_in = sem("inputs_in")
        context_in = sem("context_in")
        params_in = sem("params_in")
        consts_in = sem("consts_in")
        inv_in = sem("inv_in")
        consts_set = sem("consts_set")
        cond_ready = sem("cond_ready")
        acc_ready, taken, sq_done, ssq_done, std_done, rstd_done = (
            sem(n) for n in ("acc_ready", "taken", "sq_done", "ssq_done", "std_done", "rstd_done"))
        sq_summed = sem("sq_summed")
        t_done, u_hi_done, u_lo_done = sem("t_done"), sem("u_hi_done"), sem("u_lo_done")
        silu_done, prod_done, hid_hi_done, hid_lo_done = (
            sem(n) for n in ("silu_done", "prod_done", "hid_hi_done", "hid_lo_done"))
        dve_step, mod_step, tap_step = sem("dve_step"), sem("mod_step"), sem("tap_step")
        pool_step = sem("pool_step")
        pad_zeroed, pool_copied, pooled, p_hi_done, p_lo_done = (
            sem(n) for n in ("pad_zeroed", "pool_copied", "pooled", "p_hi_done", "p_lo_done"))
        kv_sq_done, kv_ssq_done, kv_std_done, kv_t_done, kv_hi_done, kv_lo_done = (
            sem(n) for n in ("kv_sq_done", "kv_ssq_done", "kv_std_done", "kv_t_done", "kv_hi_done", "kv_lo_done"))
        q_sq_done, q_ssq_done, q_std_done, q_t_done, qn_hi_done, qn_lo_done = (
            sem(n) for n in ("q_sq_done", "q_ssq_done", "q_std_done", "q_t_done", "qn_hi_done", "qn_lo_done"))
        kr_done, kr_hi_done, kr_lo_done = sem("kr_done"), sem("kr_hi_done"), sem("kr_lo_done")
        q_proj, k_proj, q_nope, q_roped, q_hi_done, q_lo_done = (
            sem(n) for n in ("q_proj", "k_proj", "q_nope", "q_roped", "q_hi_done", "q_lo_done"))
        k_hi_done, k_lo_done, v_hi_done, v_lo_done = (sem(n) for n in ("k_hi_done", "k_lo_done", "v_hi_done", "v_lo_done"))
        v_proj = sem("v_proj")
        scored, neg_max, exp_done, p_normal, p_turned, pt_hi_done, pt_lo_done = (
            sem(n) for n in ("scored", "neg_max", "exp_done", "p_normal", "p_turned", "pt_hi_done", "pt_lo_done"))
        pv_done, attn_hi_done, attn_lo_done = sem("pv_done"), sem("attn_hi_done"), sem("attn_lo_done")
        pool_hi_done, pool_lo_done = sem("pool_hi_done"), sem("pool_lo_done")
        c_copied, z_done, conv_done, conv_hi_done, conv_lo_done = (
            sem(n) for n in ("c_copied", "z_done", "conv_done", "conv_hi_done", "conv_lo_done"))
        stored = sem("stored")

        block = ctx.enter_context(nc.Block())

        def turned_hi(act, r, a):
            for b in range(2):
                n = 4 * r + 2 * a + b
                act.wait_ge(p_turned, n + 1)
                act.activation(pt_hi[:, a, 2 * b:2 * b + 2, :],
                               psum[:, 4 + 2 * a + b, :].rearrange("p (k t) -> p k t", k=2),
                               ACT.Copy).then_inc(pt_hi_done, 1)

        def turned_lo(dve, r, a):
            for b in range(2):
                n = 4 * r + 2 * a + b
                dve.wait_ge(pt_hi_done, n + 1)
                dve.tensor_tensor(pt_lo[:, a, 2 * b:2 * b + 2, :],
                                  psum[:, 4 + 2 * a + b, :].rearrange("p (k t) -> p k t", k=2),
                                  pt_hi[:, a, 2 * b:2 * b + 2, :].bitcast(f32), SUB).then_inc(pt_lo_done, 1)

        @block.sync
        def _(sp):
            def load(n, i=0):
                slot, uses = ring(n, i)
                if n >= RING:
                    sp.wait_ge(lo_ready[slot], uses - 1)
                sp.dma_start(raw[:, slot, :], stream[i * RING + n]).then_inc(raw_arrived[slot], 16)

            def load_start_mod(half):
                for n in (2 * half, 2 * half + 1):
                    if n == 2 * START_HALVES - 1:
                        sp.wait_ge(start_used, 2)
                    sp.dma_start(start_mod[n][:, :, :], w_mod[n]).then_inc(start_arrived[n], 16)

            sp.dma_start(par[:, :], params).then_inc(params_in, 16)
            load_start_mod(0)
            load_start_mod(1)
            sp.dma_start(resid[:, 0, :, :], x_h).then_inc(inputs_in, 16)
            sp.dma_start(con[:, :], consts).then_inc(consts_in, 16)
            load_start_mod(2)
            load(0)
            load_start_mod(3)
            load(1)
            sp.dma_start(resid[:, 1, :, :], x_g).then_inc(context_in, 16)
            load(2)
            for kh in range(2):
                sp.wait_ge(start_used, (1, 2 * START_HALVES)[kh])
                sp.dma_start(mod_raw[:, kh, :, :], w_mod[2 * START_HALVES + kh]).then_inc(mod_arrived[kh], 16)
            with sp.Fori(0, 11) as i:
                for j in range(RING):
                    load(3 + j, i)
            sp.wait_ge(multiplied, MIX)
            sp.dma_start(inv_cnt[:, :, :], inv_count).then_inc(inv_in, 16)
            with sp.Fori(0, 4) as i:
                for j in range(RING):
                    load(36 + j, i)
            sp.wait_ge(p_lo_done, 1)
            for kh in range(2):
                sp.dma_start(mod_raw[:, kh, :, :], w_mod[MOD[1][0] * 2 + kh]).then_inc(mod_arrived[kh], 16)
            with sp.Fori(0, 38) as i:
                for j in range(RING):
                    load(48 + j, i)
            for n in (162, 163):
                load(n)
            for j in range(KT // 2):
                sp.wait_ge(t_done, 8 * KT + 2 * j + 2)
                sp.dma_start(out[:, 2 * j:2 * j + 2, :], scratch[:, 2 * j:2 * j + 2, :]).then_inc(stored, 16)
            sp.wait_ge(stored, 16 * (KT // 2))

        @block.scalar
        def _(act):
            def split_hi(n, i=0):
                slot, uses = ring(n, i)
                if n >= RING:
                    act.wait_ge(multiplied, i * RING + (n - RING + 1))
                act.wait_ge(raw_arrived[slot], uses * 16)
                act.activation(w_hi[:, slot, :], raw[:, slot, :], ACT.Copy).then_inc(hi_ready, 1)

            def fetch(func):
                act.activation(table[:, 0:1] if func == ACT.Silu else table[:, 1:2], eps[:, :], func)

            def load_mod(half, kh, i=0, per=1):
                act.wait_ge(mod_step, i * (per * mod_ops(half)) + (mod_steps_before(half) + mod_ops(half) // 2 * (kh + 1)))
                act.dma_start(mod_raw[:, kh, :, :],
                              w_mod[i * (2 * per) + (2 * half + 2 + kh)]).then_inc(mod_arrived[kh], 16)

            def square_stream(e, between=None):
                who = JOINS[e][0]
                if e == 0:
                    act.wait_ge(inputs_in, 16)
                else:
                    act.wait_ge(u_lo_done, KT * e)
                for j, (k, end) in enumerate(SQUARED):
                    if e >= 2:
                        act.wait_ge(taken, RESULT[e] - KT + end)
                    act.activation(scratch[:, k:end, :], resid[:, who, k:end, :], ACT.Square).then_inc(sq_done, 1)
                    if j == 1 and between is not None:
                        split_hi(between)

            def deviation(e):
                act.wait_ge(ssq_done, e + 1)
                if e > 0:
                    act.wait_ge(rstd_done, e)
                act.activation(std[:, :], psum[:, SSQ, 0:T], ACT.Sqrt, bias=eps[:, :],
                               scale=1.0 / D).then_inc(std_done, 1)

            def modulated_hi(e, between=None):
                who, norm = JOINS[e]
                for j in range(KT):
                    act.wait_ge(t_done, KT * e + j + 1)
                    act.activation(u_hi[:, j, who * T:who * T + T], scratch[:, j, :], ACT.Identity,
                                   bias=shift(*norm, who, j)).then_inc(u_hi_done, 1)
                    if j == 3 and between is not None:
                        split_hi(between)
                    if e == 0 and 2 <= j < 7:
                        k, end = SQUARED[j - 2]
                        if k == 0:
                            act.wait_ge(context_in, 16)
                        act.activation(context_sq[:, k:end, :], resid[:, 1, k:end, :], ACT.Square).then_inc(sq_done, 1)

            def silu_gate(p):
                if p == 0:
                    act.activation(silu[:, :].rearrange("p (a t) -> p a t", a=2), psum[:, F_GATE:F_GATE + 2, :],
                                   ACT.Silu).then_inc(silu_done, 1)
                else:
                    act.activation(silu[:, 0:2 * T], psum[:, F_GATE, :], ACT.Silu).then_inc(silu_done, 1)

            def hidden_hi(p, step, i=0):
                act.wait_ge(prod_done, i * BLOCK + (STEPS * p + step + 1))
                width = 2 * T if p == 0 else T
                at = step % BLOCK * 2
                act.activation(hid_hi[:, at:at + 2, 0:width], prod[:, 0:2 * width].rearrange("p (a t) -> p a t", a=2),
                               ACT.Copy).then_inc(hid_hi_done, 1)

            def ffn_pass(p):
                first, ahead, positions = MOD[p]
                b = PASS[p] + 2
                with act.Fori(0, 3) as i:
                    k = i * 3

                    def mod_load(position, kh):
                        if position in positions:
                            half, per = mod_slot(p, position)
                            load_mod(half, kh, i, per)

                    if positions:
                        load_mod(first + ahead - 1, 0, i, len(positions))
                    act.wait_ge(multiplied, i * 9 + (b + 1))
                    silu_gate(p)
                    split_hi(b + 3, k)
                    if positions:
                        load_mod(first + ahead - 1, 1, i, len(positions))
                    hidden_hi(p, 1, i)
                    split_hi(b + 4, k)
                    mod_load(0, 0)
                    act.wait_ge(multiplied, i * 9 + (b + 3))
                    silu_gate(p)
                    split_hi(b + 5, k)
                    mod_load(0, 1)
                    hidden_hi(p, 2, i)
                    split_hi(b + 6, k)
                    mod_load(1, 0)
                    split_hi(b + 7, k)
                    mod_load(1, 1)
                    split_hi(b + 8, k)
                    mod_load(2, 0)
                    mod_load(2, 1)
                    split_hi(b + 9, k)
                    mod_load(3, 0)
                    act.wait_ge(multiplied, i * 9 + (b + 8))
                    silu_gate(p)
                    split_hi(b + 10, k)
                    mod_load(3, 1)
                    hidden_hi(p, 3, i)
                    split_hi(b + 11, k)
                b += 27
                act.wait_ge(multiplied, b + 1)
                silu_gate(p)
                if b + 3 < N_CHUNKS:
                    split_hi(b + 3)
                if p == 1:
                    for kh in range(2):
                        load_mod(MOD[2][0] - 1, kh)
                hidden_hi(p, STEPS - 1)
                fetch(ACT.Sqrt)
                if p < 3:
                    split_hi(b + 4)

            def ffn_step0(p):
                act.wait_ge(multiplied, PASS[p] + 1)
                silu_gate(p)
                split_hi(PASS[p] + 3)
                if MOD[p][1] == 2:
                    for kh in range(2):
                        load_mod(MOD[p][0], kh)
                hidden_hi(p, 0)
                split_hi(PASS[p] + 4)

            def pool_copy(i):
                if i > 0:
                    act.wait_ge(multiplied, MIX + i + 1)
                act.activation(pad_x[:, 2 * i:2 * i + 2, PAD:PAD + T],
                               psum[:, 4 + i, :].rearrange("p (a t) -> p a t", a=2), ACT.Copy).then_inc(pool_copied, 1)

            def query_copy(i, chunk, bank):
                act.wait_ge(multiplied, chunk + 1)
                view = psum[:, bank, :].rearrange("p (a t) -> p a t", a=2)
                act.activation(cq[:, 2 * i:2 * i + 2, :], view, ACT.Copy)
                act.activation(cq_sq[:, 2 * i:2 * i + 2, :], view, ACT.Square).then_inc(q_sq_done, 1)

            act.wait_ge(params_in, 16)
            act.activation(cond[:, :, :], col("cond", 0, 2 * KT).rearrange("p (k c) -> p k c", c=2),
                           ACT.Silu).then_inc(cond_ready, 1)
            act.wait_ge(consts_set, 2)
            for half in range(START_HALVES):
                act.wait_ge(start_used, 2 * half + 2)
                act.activation(start_row[:, half, :], psum[0:2, half, :], ACT.Copy).then_inc(start_rows, 1)
                if half == 0:
                    square_stream(0)
                    deviation(0)
                if half == 2:
                    split_hi(0)
            modulated_hi(0, 1)
            split_hi(2)
            deviation(1)
            fetch(ACT.Silu)
            modulated_hi(1)
            ffn_step0(0)
            ffn_pass(0)
            square_stream(2)
            deviation(2)
            split_hi(MIX + 1)
            modulated_hi(2, MIX + 2)

            square_stream(3)
            act.wait_ge(multiplied, MIX + 1)
            act.wait_ge(pad_zeroed, 1)
            pool_copy(0)
            split_hi(MIX + 3)
            deviation(3)
            split_hi(MIX + 4)
            pool_copy(1)
            modulated_hi(3, MIX + 5)
            query_copy(0, MIX + 2, 2)
            query_copy(1, MIX + 3, 3)
            split_hi(MIX + 6)
            query_copy(2, MIX + 4, 4)
            act.wait_ge(q_ssq_done, 1)
            act.activation(std[:, :], psum[:, SSQ, 0:T], ACT.Sqrt, bias=eps[:, :],
                           scale=1.0 / (QR * P)).then_inc(q_std_done, 1)
            split_hi(MIX + 7)
            act.wait_ge(multiplied, MIX + 6)
            for i, bank in enumerate((6, 0)):
                act.activation(ckv[:, i, :], psum[:, bank, :], ACT.Copy)
                act.activation(ckv_sq[:, i, :], psum[:, bank, :], ACT.Square).then_inc(kv_sq_done, 1)
            for i in range(QR):
                act.wait_ge(q_t_done, i + 1)
                act.activation(qn_hi[:, i, :], cq_sq[:, i, :], ACT.Copy).then_inc(qn_hi_done, 1)
            act.wait_ge(kv_ssq_done, 1)
            act.wait_ge(u_lo_done, 4 * KT)
            act.activation(kv_std[:, :], psum[:, 5, :], ACT.Sqrt, bias=eps[:, :],
                           scale=1.0 / (KVR * P)).then_inc(kv_std_done, 1)
            split_hi(MIX + 8)
            for i in range(KVR):
                act.wait_ge(kv_t_done, i + 1)
                act.activation(kvn_hi[:, i, :], ckv_sq[:, i, :], ACT.Copy).then_inc(kv_hi_done, 1)
            fetch(ACT.Exp)
            act.wait_ge(kr_done, 1)
            act.wait_ge(kv_lo_done, KVR)
            for a in range(2):
                act.activation(k_hi[NOPE:NOPE + ROPE, a, :], kr_f[NOPE:NOPE + ROPE, :],
                               ACT.Copy).then_inc(kr_hi_done, 1)

            def projected_hi(r):
                for a in range(2):
                    act.wait_ge(k_proj, r + 1)
                    act.activation(k_hi[0:NOPE, a, :], psum[a * NOPE:a * NOPE + NOPE, 2, :], ACT.Copy).then_inc(k_hi_done, 1)
                if r == 0:
                    act.wait_ge(multiplied, MIX + 8)
                else:
                    act.wait_ge(v_proj, r)
                act.wait_ge(kr_lo_done, 2)
                act.activation(v_hi[:, r % 2, :], psum[:, 3, :], ACT.Copy).then_inc(v_hi_done, 1)

            def queries_hi(r):
                if r == 0:
                    act.wait_ge(q_proj, 1)
                else:
                    act.wait_ge(multiplied, MIX + 8 + r)
                if r > 0:
                    act.wait_ge(q_lo_done, r)
                act.activation(q_f[0:NOPE, :], psum[0:NOPE, 0, :], ACT.Copy).then_inc(q_nope, 1)
                act.wait_ge(q_nope, r + 1)
                act.wait_ge(q_roped, r + 1)
                act.activation(q_hi[0:NOPE + ROPE, :], q_f[0:NOPE + ROPE, :], ACT.Copy).then_inc(q_hi_done, 1)

            queries_hi(0)
            projected_hi(0)
            split_hi(MIX + 9)
            for r in range(PAIRS):
                for a in range(2):
                    for qt in range(2):
                        n = 4 * r + 2 * a + qt
                        act.wait_ge(neg_max, n + 1)
                        if r > 0:
                            act.wait_ge(p_turned, 4 * (r - 1) + 2 * a + 2)
                        act.activation(probs[a][:, qt, :], psum[:, 4 + 2 * a + qt, :], ACT.Exp,
                                       bias=stat[:, 0, n:n + 1], scale=ATTN_SCALE,
                                       accum_out=stat[:, 1, n:n + 1]).then_inc(exp_done, 1)
                if r + 1 < PAIRS:
                    split_hi(MIX + 10 + r)
                if r + 1 < PAIRS:
                    projected_hi(r + 1)
                for a in range(2):
                    turned_hi(act, r, a)
                if r + 1 < PAIRS:
                    queries_hi(r + 1)
                if r + 2 == PAIRS:
                    split_hi(MIX + 13)
                    act.wait_ge(multiplied, MIX + 12)
                    for g in range(4):
                        act.activation(mix_hi[:, g, :], psum[:, 1 + g // 2, (g % 2) * T:(g % 2) * T + T], ACT.Identity,
                                       scale=col("pool_scale", g)).then_inc(pool_hi_done, 1)
                act.wait_ge(pv_done, r + 1)
                for a in range(2):
                    act.activation(mix_hi[a * VD:a * VD + VD, 4 + r, :], psum[a * VD:a * VD + VD, 3, a * T:a * T + T],
                                   ACT.Copy).then_inc(attn_hi_done, 1)
                if r == 0:
                    act.wait_ge(pooled, 1)
                    act.activation(p_hi[:, :, :], win2[:, :, PAD:PAD + T], ACT.Copy).then_inc(p_hi_done, 1)
                if r + 2 == PAIRS:
                    split_hi(MIX + 14)

            for n in range(MIX + 15, MIX + 17):
                split_hi(n)
            fetch(ACT.Sqrt)
            square_stream(4, MIX + 17)
            deviation(4)
            modulated_hi(4)
            split_hi(PASS[1] + 2)
            ffn_step0(1)
            ffn_pass(1)
            square_stream(5)
            deviation(5)
            split_hi(PASS[2] + 1)
            modulated_hi(5)
            split_hi(PASS[2] + 2)
            ffn_step0(2)
            ffn_pass(2)
            square_stream(6)
            deviation(6)
            split_hi(CONV + 1)
            modulated_hi(6)
            split_hi(CONV + 2)

            with act.Fori(0, KT // 2) as i:
                act.wait_ge(multiplied, i * RING + (CONV + 1))
                act.activation(silu[:, 0:2 * T], psum[:, GATE, :], ACT.Copy).then_inc(c_copied, 1)
                split_hi(CONV + 3, i)
                split_hi(CONV + 4, i)
                split_hi(CONV + 5, i)
                act.wait_ge(conv_done, i + 1)
                act.activation(mix_hi[:, bass.ds(i * 2, 2), :], prod[:, 0:2 * T].rearrange("p (a t) -> p a t", a=2),
                               ACT.Copy).then_inc(conv_hi_done, 1)
            for n in range(CONV + 15, CONV + 17):
                split_hi(n)
            fetch(ACT.Sqrt)
            square_stream(7, CONV + 17)
            deviation(7)
            modulated_hi(7)
            split_hi(PASS[3] + 2)
            ffn_step0(3)
            ffn_pass(3)
            square_stream(8)
            deviation(8)

        @block.vector
        def _(dve):
            steps = [0]

            def settle(ins):
                steps[0] += 1
                ins.then_inc(dve_step, 1)
                dve.wait_ge(dve_step, steps[0])

            def split_lo(n, i=0):
                slot, uses = ring(n, i)
                dve.wait_ge(hi_ready, i * RING + (n + 1))
                dve.tensor_tensor(w_lo[:, slot, :], raw[:, slot, :], w_hi[:, slot, :].bitcast(f32),
                                  SUB).then_inc(lo_ready[slot], 1)

            def add_squares(e, k):
                if k in (4, 5):
                    j = k - 3
                    dve.wait_ge(sq_done, len(SQUARED) * e + j + 1)
                    ins = dve.tensor_tensor(scratch[:, 0:2, :], scratch[:, 0:2, :], scratch[:, 2 * j:2 * j + 2, :], ADD)
                    if j == 1:
                        settle(ins)
                    else:
                        ins.then_inc(sq_summed, 1)

            def gather(which):
                first_chunk, norm = {"mix": (MIX + 12, (0, 1)), "conv": (CONV + 12, (1, 1))}[which]
                dve.wait_ge(taken, TAKEN[which])
                for k in range(KT):
                    if k % 2 == 0:
                        dve.wait_ge(multiplied, first_chunk + k // 2 + 1)
                    dve.scalar_tensor_tensor(resid[:, 0, k, :], psum[:, k // 2, k % 2 * T:k % 2 * T + T],
                                             shift(*norm, 0, k, 1, 2), resid[:, 0, k, :], MUL, ADD).then_inc(taken, 1)
                    if which == "mix" and k == 1:
                        split_lo(MIX + 15)
                    add_squares({"mix": 4, "conv": 7}[which], k)

            def gather_down(p, k, i=0, last=False):
                if not last:
                    if k == 0:
                        dve.wait_ge(taken, i * KT + TAKEN[p])
                    if k < KT - 1:
                        dve.wait_ge(acc_ready, i * 7 + (27 * p + k + 1))
                    else:
                        dve.wait_ge(multiplied, i * 9 + (PASS[p] + 9))
                else:
                    if k == 0:
                        dve.wait_ge(taken, TAKEN[p] + 3 * KT)
                    if k % 4 == 3:
                        dve.wait_ge(multiplied, PASS[p] + 32 + k // 4)
                    else:
                        dve.wait_ge(acc_ready, 27 * p + 21 + k - k // 4 + 1)
                for who in range(2 if p == 0 else 1):
                    ins = dve.scalar_tensor_tensor(resid[:, who, k, :], psum[:, DOWN[k], who * T:who * T + T],
                                                   shift(*KIND[p], who, k, 1, 2), resid[:, who, k, :], MUL, ADD)
                ins.then_inc(taken, 1)

            def inverse_rms(e):
                dve.wait_ge(std_done, e + 1)
                dve.reciprocal(rstd[:, :], std[:, :]).then_inc(rstd_done, 1)

            def modulate(e):
                who, norm = JOINS[e]
                if e >= 2:
                    dve.wait_ge(taken, RESULT[e])
                if norm is not None:
                    layer, kind = norm
                    gain = gain_scale[:, :]
                    settle(dve.scalar_tensor_tensor(gain, shift(layer, kind, who, 0, KT, 1), 1.0,
                                                    col("norm_g", (layer * 3 + kind) * KT, KT), ADD, MUL))
                else:
                    gain = col("final_norm_g", 0, KT)
                if e > 0:
                    inverse_rms(e)
                dve.wait_ge(rstd_done, e + 1)

                def scaled(j):
                    dve.scalar_tensor_tensor(scratch[:, j, :], resid[:, who, j, :], gain[:, j:j + 1],
                                             rstd[:, :], MUL, MUL).then_inc(t_done, 1)

                scaled(0)
                for j in range(KT):
                    if j + 1 < KT:
                        scaled(j + 1)
                    if norm is None:
                        continue
                    dve.wait_ge(u_hi_done, KT * e + j + 1)
                    at = slice(who * T, who * T + T)
                    dve.scalar_tensor_tensor(u_lo[:, j, at], scratch[:, j, :], shift(*norm, who, j),
                                             u_hi[:, j, at].bitcast(f32), ADD, SUB).then_inc(u_lo_done, 1)

            def write_mod(half, i=0, per=1):
                done = i * per + (half - START_HALVES + 1)
                dve.wait_ge(mod_reduced, done)
                for c in range(conditions(half)):
                    last = dve.reduce_sum(mod_sum[:, :, c], psum[:, MODB + c, :].rearrange("p (k q) -> p k q", k=4), AX.X)
                last.then_inc(mod_summed, 1)
                dve.wait_ge(mod_summed, done)
                for c in range(conditions(half)):
                    last = dve.tensor_tensor(mod_out[:, bass.ds(i * (4 * per) + half * 4, 4), c], mod_sum[:, :, c],
                                             par[:, bass.ds(i * (4 * per) + (half * 4 + PARAM["b_mod"]), 4)], ADD)
                last.then_inc(mod_written, 1)
                dve.wait_ge(mod_written, i * per + (half - START_HALVES + 2))

            def sum_mod(half, i=0, per=1):
                base, conds = mod_steps_before(half), conditions(half)
                for kt in range(KT):
                    kh, k = kt // 4, kt % 4
                    if k == 0:
                        dve.wait_ge(mod_arrived[kh], i * (16 * per) + (half - START_HALVES + 1) * 16)
                    for c in range(conds):
                        at = base + kt * conds + c
                        w = mod_raw[:, kh, k, :]
                        if kt == 0:
                            ins = dve.tensor_scalar(mod_acc[:, c, :], w, cond[:, kt, c:c + 1], None, MUL)
                        else:
                            dve.wait_ge(mod_step, i * (per * KT * conds) + (at - conds + 1))
                            ins = dve.scalar_tensor_tensor(mod_acc[:, c, :], w, cond[:, kt, c:c + 1],
                                                           mod_acc[:, c, :], MUL, ADD)
                        ins.then_inc(mod_step, 1)

            def hidden(p, step, i=0):
                n = i * BLOCK + (STEPS * p + step + 1)
                at = step % BLOCK * 2
                width = 2 * T if p == 0 else T
                tiles = [x[:, 0:2 * width].rearrange("p (a t) -> p a t", a=2) for x in (silu, prod)]
                up = (psum[:, F_UP:F_UP + 2, :] if p == 0
                      else psum[:, F_UP, :].rearrange("p (a t) -> p a t", a=2))
                dve.wait_ge(silu_done, n)
                if (p, step) != (0, 0):
                    dve.wait_ge(hid_lo_done, i * BLOCK + (STEPS * p + step))
                dve.scalar_tensor_tensor(tiles[1], tiles[0], 0.5, up, MUL, MUL).then_inc(prod_done, 1)
                dve.wait_ge(hid_hi_done, n)
                dve.tensor_tensor(hid_lo[:, at:at + 2, 0:width], tiles[1],
                                  hid_hi[:, at:at + 2, 0:width].bitcast(f32), SUB).then_inc(hid_lo_done, 1)

            def ffn_pass(p):
                first, ahead, positions = MOD[p]
                b = PASS[p] + 2
                with dve.Fori(0, 3) as i:
                    k = i * 3

                    def split(j):
                        if p > 0 and (b + j) % RING == 1:
                            split_lo(b + j, k)

                    def modulation(position):
                        if position in positions:
                            half, per = mod_slot(p, position)
                            write_mod(half - 1, i, per)
                            sum_mod(half, i, per)

                    split(3)
                    dve.wait_ge(multiplied, i * 9 + (b + 2))
                    hidden(p, 1, i)
                    split(4)
                    modulation(0)
                    dve.wait_ge(multiplied, i * 9 + (b + 4))
                    hidden(p, 2, i)
                    split(6)
                    modulation(1)
                    split(7)
                    for j in range(4):
                        gather_down(p, j, i)
                    modulation(2)
                    for j in range(4, KT):
                        gather_down(p, j, i)
                    split(9)
                    modulation(3)
                    split(10)
                    dve.wait_ge(multiplied, i * 9 + (b + 9))
                    hidden(p, 3, i)
                    modulation(4)
                dve.wait_ge(multiplied, b + 29)
                hidden(p, STEPS - 1)
                if positions:
                    write_mod(first + ahead - 1 + 3 * len(positions))
                for j in range(KT):
                    gather_down(p, j, last=True)
                    add_squares({0: 2, 1: 5, 2: 6, 3: 8}[p], j)

            dve.memset(ones[:, :], 1.0).then_inc(consts_set, 1)
            dve.memset(eps[:, :], EPS).then_inc(consts_set, 1)
            dve.memset(mod_sum[:, :, :], 0.0).then_inc(taken, 1)
            inverse_rms(0)
            dve.wait_ge(params_in, 16)
            dve.wait_ge(consts_in, 16)
            dve.wait_ge(start_turned, 1)
            for c in range(2):
                last = dve.tensor_tensor(mod_out[:, 0:4 * START_HALVES, c],
                                         psum[:, MODB, 0:8 * START_HALVES].rearrange("p (k c) -> p k c", c=2)[:, :, c],
                                         col("b_mod", 0, 4 * START_HALVES), ADD)
            last.then_inc(mod_written, 1)
            dve.wait_ge(mod_written, 1)
            modulate(0)

            dve.wait_ge(sq_done, 2 * len(SQUARED))
            settle(dve.tensor_tensor(context_sq[:, 0:4, :], context_sq[:, 0:4, :], context_sq[:, 4:8, :], ADD))
            dve.tensor_tensor(context_sq[:, 0:2, :], context_sq[:, 0:2, :], context_sq[:, 2:4, :], ADD).then_inc(sq_summed, 1)
            modulate(1)
            dve.wait_ge(cond_ready, 1)
            sum_mod(4)
            dve.wait_ge(multiplied, PASS[0] + 2)
            hidden(0, 0)
            ffn_pass(0)
            modulate(2)

            modulate(3)
            dve.wait_ge(u_lo_done, 4 * KT)
            dve.wait_ge(q_std_done, 1)
            settle(dve.reciprocal(rstd[:, :], std[:, :]))
            for i in range(QR):
                dve.scalar_tensor_tensor(cq_sq[:, i, :], cq[:, i, :], col("q_norm_g", i), rstd[:, :],
                                         MUL, MUL).then_inc(q_t_done, 1)
            dve.wait_ge(kv_std_done, 1)
            settle(dve.reciprocal(kv_rstd[:, :], kv_std[:, :]))
            for i in range(KVR):
                dve.scalar_tensor_tensor(ckv_sq[:, i, :], ckv[:, i, :], col("kv_norm_g", i), kv_rstd[:, :],
                                         MUL, MUL).then_inc(kv_t_done, 1)
            dve.wait_ge(multiplied, MIX + 7)
            rope_rows, swap_rows = slice(NOPE, NOPE + ROPE), slice(NOPE + ROPE, P)
            kr_a, kr_b = prod[rope_rows, 0:T], prod[rope_rows, T:2 * T]
            dve.tensor_tensor(kr_a, psum[rope_rows, 1, 0:T], con[rope_rows, P:P + T], MUL)
            settle(dve.tensor_tensor(kr_b, psum[swap_rows, 1, 0:T], con[swap_rows, P:P + T], MUL))
            dve.tensor_tensor(kr_f[rope_rows, 0:T], kr_a, kr_b, ADD)
            dve.tensor_copy(kr_f[rope_rows, T:2 * T], psum[rope_rows, 1, T:2 * T]).then_inc(kr_done, 1)
            for a in range(2):
                dve.wait_ge(kr_hi_done, a + 1)
                dve.tensor_tensor(k_lo[rope_rows, a, :], kr_f[rope_rows, :], k_hi[rope_rows, a, :].bitcast(f32),
                                  SUB).then_inc(kr_lo_done, 1)

            def projected_lo(r):
                for a in range(2):
                    dve.wait_ge(k_hi_done, 2 * r + 2)
                    dve.tensor_tensor(k_lo[0:NOPE, a, :], psum[a * NOPE:a * NOPE + NOPE, 2, :],
                                      k_hi[0:NOPE, a, :].bitcast(f32),
                                      SUB).then_inc(k_lo_done, 1)
                dve.wait_ge(v_hi_done, r + 1)
                dve.tensor_tensor(v_lo[:, r % 2, :], psum[:, 3, :], v_hi[:, r % 2, :].bitcast(f32),
                                  SUB).then_inc(v_lo_done, 1)

            def queries_lo(r):
                if r == 0:
                    dve.wait_ge(q_proj, 1)
                else:
                    dve.wait_ge(multiplied, MIX + 8 + r)
                dve.tensor_tensor(rope_a[rope_rows, :], psum[rope_rows, 0, :], con[rope_rows, P:P + 2 * T], MUL)
                settle(dve.tensor_tensor(rope_b[rope_rows, :], psum[swap_rows, 0, :], con[swap_rows, P:P + 2 * T], MUL))
                dve.tensor_tensor(q_f[rope_rows, :], rope_a[rope_rows, :], rope_b[rope_rows, :],
                                  ADD).then_inc(q_roped, 1)
                dve.wait_ge(q_hi_done, r + 1)
                dve.tensor_tensor(q_lo[0:NOPE + ROPE, :], q_f[0:NOPE + ROPE, :], q_hi[0:NOPE + ROPE, :].bitcast(f32),
                                  SUB).then_inc(q_lo_done, 1)

            queries_lo(0)
            projected_lo(0)
            for r in range(PAIRS):
                for n in range(4 * r, 4 * r + 4):
                    dve.wait_ge(scored, n + 1)
                    settle(dve.reduce_max(stat[:, 2, n:n + 1], psum[:, 4 + n % 4, :], AX.X))
                    dve.tensor_scalar(stat[:, 0, n:n + 1], stat[:, 2, n:n + 1], -ATTN_SCALE, None,
                                      MUL).then_inc(neg_max, 1)
                for a in range(2):
                    for qt in range(2):
                        n = 4 * r + 2 * a + qt
                        dve.wait_ge(exp_done, n + 1)
                        settle(dve.reciprocal(stat[:, 3, n:n + 1], stat[:, 1, n:n + 1]))
                        dve.tensor_scalar(probs[a][:, qt, :], probs[a][:, qt, :], stat[:, 3, n:n + 1], None,
                                          MUL).then_inc(p_normal, 1)
                if r + 1 < PAIRS:
                    projected_lo(r + 1)
                for a in range(2):
                    turned_lo(dve, r, a)
                if r + 1 < PAIRS:
                    queries_lo(r + 1)
                if r + 2 == PAIRS:
                    for g in range(4):
                        dve.wait_ge(pool_hi_done, g // 2 * 2 + 2)
                        dve.scalar_tensor_tensor(mix_lo[:, g, :], psum[:, 1 + g // 2, (g % 2) * T:(g % 2) * T + T],
                                                 col("pool_scale", g), mix_hi[:, g, :].bitcast(f32), MUL,
                                                 SUB).then_inc(pool_lo_done, 1)
                dve.wait_ge(attn_hi_done, 2 * r + 2)
                for a in range(2):
                    rows = slice(a * VD, a * VD + VD)
                    last = dve.tensor_tensor(mix_lo[rows, 4 + r, :], psum[rows, 3, a * T:a * T + T],
                                             mix_hi[rows, 4 + r, :].bitcast(f32), SUB)
                last.then_inc(attn_lo_done, 1)

            gather("mix")
            modulate(4)

            for p in (1, 2):
                sum_mod(MOD[p][0])
                dve.wait_ge(multiplied, PASS[p] + 2)
                hidden(p, 0)
                write_mod(MOD[p][0])
                sum_mod(MOD[p][0] + 1)
                ffn_pass(p)
                modulate(4 + p)

            dve.wait_ge(u_lo_done, 7 * KT)
            settle(dve.memset(z_pad[:, :, :], 0.0))
            with dve.Fori(0, KT // 2) as i:
                dve.wait_ge(c_copied, i + 1)
                dve.wait_ge(multiplied, i * RING + (CONV + 2))
                dve.tensor_tensor(z_pad[:, :, 1:1 + T], silu[:, 0:2 * T].rearrange("p (a t) -> p a t", a=2),
                                  psum[:, UP, :].rearrange("p (a t) -> p a t", a=2), MUL).then_inc(z_done, 1)
                dve.wait_ge(z_done, i + 1)

                def tap(a, d):
                    return par[:, bass.ds(i * 6 + (PARAM["conv_w"] + 3 * a + d), 1)]

                for a in range(2):
                    dve.tensor_scalar(conv_1[:, a, :], z_pad[:, a, 0:T], tap(a, 0), None, MUL).then_inc(tap_step, 1)
                for d, src, dst in ((1, conv_1, conv_2), (2, conv_2, conv_1)):
                    for a in range(2):
                        dve.wait_ge(tap_step, i * 6 + (2 * d - 1 + a))
                        dve.scalar_tensor_tensor(dst[:, a, :], z_pad[:, a, d:d + T], tap(a, d), src[:, a, :],
                                                 MUL, ADD).then_inc(tap_step, 1)
                dve.wait_ge(tap_step, i * 6 + 6)
                dve.wait_ge(multiplied, i * RING + (CONV + 3))
                dve.tensor_tensor(prod[:, 0:2 * T].rearrange("p (a t) -> p a t", a=2), conv_1[:, :, :],
                                  psum[:, 6, :].rearrange("p (a t) -> p a t", a=2), MUL).then_inc(conv_done, 1)
                dve.wait_ge(conv_hi_done, i + 1)
                at = bass.ds(i * 2, 2)
                dve.tensor_tensor(mix_lo[:, at, :], prod[:, 0:2 * T].rearrange("p (a t) -> p a t", a=2),
                                  mix_hi[:, at, :].bitcast(f32), SUB).then_inc(conv_lo_done, 1)
            gather("conv")
            modulate(7)

            dve.wait_ge(multiplied, PASS[3] + 2)
            hidden(3, 0)
            ffn_pass(3)
            modulate(8)

        @block.gpsimd
        def _(pool):
            steps = [0]

            def settle(ins):
                steps[0] += 1
                ins.then_inc(pool_step, 1)
                pool.wait_ge(pool_step, steps[0])

            def split_lo(n, i=0):
                slot, uses = ring(n, i)
                pool.wait_ge(hi_ready, i * RING + (n + 1))
                pool.tensor_tensor(w_lo[:, slot, :], raw[:, slot, :], w_hi[:, slot, :].bitcast(f32),
                                   SUB).then_inc(lo_ready[slot], 1)

            def add_squares(e):
                pool.wait_ge(sq_done, len(SQUARED) * (e + 1))
                settle(pool.tensor_tensor(scratch[:, 0:4, :], scratch[:, 0:4, :], scratch[:, 4:8, :], ADD))
                pool.tensor_tensor(scratch[:, 0:2, :], scratch[:, 0:2, :], scratch[:, 2:4, :], ADD).then_inc(sq_summed, 1)

            def pass_lo(p):
                split_lo(PASS[p] + 3)
                split_lo(PASS[p] + 4)
                with pool.Fori(0, 9) as i:
                    for n in range(PASS[p] + 5, PASS[p] + 8):
                        if p == 0 or n % RING != 1:
                            split_lo(n, i)
                for n in range(PASS[p] + 32, min(PASS[p] + 35, N_CHUNKS)):
                    split_lo(n)

            add_squares(0)
            for n in range(RING):
                split_lo(n)
            pass_lo(0)
            pool.wait_ge(mod_step, mod_steps_before(BOTH))
            pool.memset(pad_x[:, :, :], 0.0).then_inc(pad_zeroed, 1)
            split_lo(MIX + 2)
            add_squares(3)
            for n in range(MIX + 3, MIX + 8):
                split_lo(n)
            for i in range(QR):
                pool.wait_ge(qn_hi_done, i + 1)
                pool.tensor_tensor(qn_lo[:, i, :], cq_sq[:, i, :], qn_hi[:, i, :].bitcast(f32),
                                  SUB).then_inc(qn_lo_done, 1)
            for i in range(KVR):
                pool.wait_ge(kv_hi_done, i + 1)
                pool.tensor_tensor(kvn_lo[:, i, :], ckv_sq[:, i, :], kvn_hi[:, i, :].bitcast(f32),
                                   SUB).then_inc(kv_lo_done, 1)
            split_lo(MIX + 8)
            pool.wait_ge(pool_copied, 2)
            settle(pool.tensor_tensor(win2[:, :, 1:PW], pad_x[:, :, 0:PW - 1], pad_x[:, :, 1:PW], ADD))
            settle(pool.tensor_tensor(win4[:, :, 2:PW - 1], win2[:, 1:4, 1:PW - 2], win2[:, 1:4, 3:PW], ADD))
            settle(pool.tensor_tensor(win8[:, :, 4:PW - 3], win4[:, 1:3, 2:PW - 5], win4[:, 1:3, 6:PW - 1], ADD))
            settle(pool.tensor_tensor(win16[:, :, 8:PW - 7], win8[:, 1:2, 4:PW - 11], win8[:, 1:2, 12:PW - 3], ADD))
            pool.wait_ge(inv_in, 16)
            inner = slice(PAD, PAD + T)
            for g, w in enumerate((win2[:, 0, :], win4[:, 0, :], win8[:, 0, :], win16[:, 0, :])):
                last = pool.tensor_tensor(win2[:, g, inner], w[:, inner], inv_cnt[:, g, :], MUL)
            settle(last)
            pool.tensor_tensor(win2[:, :, inner], win2[:, :, inner], pad_x[:, :, inner], SUB).then_inc(pooled, 1)
            split_lo(MIX + 9)
            split_lo(MIX + 10)
            pool.wait_ge(p_hi_done, 1)
            pool.tensor_tensor(p_lo[:, :, :], win2[:, :, inner], p_hi[:, :, :].bitcast(f32), SUB).then_inc(p_lo_done, 1)
            for n in range(MIX + 11, MIX + 19):
                if n != MIX + 15:
                    split_lo(n)
            pass_lo(1)
            split_lo(PASS[2] + 2)
            pass_lo(2)
            for n in range(CONV + 2, CONV + 6):
                split_lo(n)
            with pool.Fori(0, 3) as i:
                for j in range(RING):
                    split_lo(CONV + 6 + j, i)
            for n in range(CONV + 15, CONV + 19):
                split_lo(n)
            pass_lo(3)

        @block.tensor
        def _(pe):
            def three(out, w_at, x_at, first, last, shared=False, start=None):
                begin = first if start is None else start
                pe.matmul(out, w_at[0], x_at[0], start=begin, stop=False, skip_group_check=shared)
                pe.matmul(out, w_at[1], x_at[0], start=False, stop=False, skip_group_check=shared)
                return pe.matmul(out, w_at[0], x_at[1], start=False, stop=last, skip_group_check=shared)

            def fresh_tile(join, clears, outs, slot, x, k):
                pe.wait_ge(u_hi_done, KT * join + k + 1)
                for a in range(2):
                    w_at = weights(slot, k * 256 + a * P)
                    pe.matmul(outs[a], w_at[0], x[0], start=k == 0 and clears[a], stop=False, skip_group_check=True)
                    pe.matmul(outs[a], w_at[1], x[0], start=False, stop=False, skip_group_check=True)
                pe.wait_ge(u_lo_done, KT * join + k + 1)
                for a in range(2):
                    last = pe.matmul(outs[a], weights(slot, k * 256 + a * P)[0], x[1], start=False, stop=k == KT - 1,
                                     skip_group_check=True)
                return last

            def weights(slot, at):
                return w_hi[:, slot, at:at + P], w_lo[:, slot, at:at + P]

            def arrived(n, i=0):
                slot, uses = ring(n, i)
                pe.wait_ge(lo_ready[slot], uses)
                return slot

            def stream_in(k, who, width=T):
                at = slice(who * T, who * T + width)
                return u_hi[:, k, at], u_lo[:, k, at]

            def project(n, bank, who, i=0, fresh=None):
                slot = arrived(n, i)
                if fresh is None:
                    for a in range(2):
                        for k in range(KT):
                            last = three(psum[:, bank, a * T:a * T + T], weights(slot, k * 256 + a * P),
                                         stream_in(k, who), k == 0, k == KT - 1)
                else:
                    for k in range(KT):
                        last = fresh_tile(fresh, (True, False), [psum[:, bank, a * T:a * T + T] for a in range(2)],
                                          slot, stream_in(k, who), k)
                last.then_inc(multiplied, 1)

            def ffn_project(p, n, bank, i=0, fresh=None):
                if p > 0:
                    project(n, bank, 0, i, fresh)
                    return
                slot = arrived(n, i)
                for a in range(2):
                    for k in range(KT):
                        last = three(psum[:, bank + a, :], weights(slot, k * 256 + a * P), stream_in(k, 0, 2 * T),
                                     k == 0, k == KT - 1)
                last.then_inc(multiplied, 1)

            def down(p, n, tiles, i=0, middle=None):
                width = 2 * T if p == 0 else T
                step = STEPS * p + (3 if tiles == 6 else STEPS)
                if tiles == 6:
                    order = [[(j, k) for j in (0, 1) for k in range(4)] + [(2, 0), (2, 1), (2, 2), None]
                             + [(j, k) for j in (0, 1) for k in (4, 5)] + [(2, 3)],
                             [(2, 4), (2, 5)] + [(j, k) for j in (3, 4) for k in range(6)] + [(5, 0), (5, 1)],
                             [(5, k) for k in range(2, 6)] + [(j, k) for j in (6, 7) for k in range(6)]]
                else:
                    order = [[(j, k) for j in range(4) for k in (0, 1)] + [None] + [(j, k) for j in range(4) for k in (2, 3)],
                             [(j, k) for j in range(4, 8) for k in range(4)]]
                for c, uses in enumerate(order):
                    slot = arrived(n + c, i * 3)
                    for use in uses:
                        if use is None:
                            pe.wait_ge(hid_lo_done, i * BLOCK + step)
                            continue
                        j, k = use
                        if k == 0:
                            if j == 0:
                                pe.wait_ge(taken, i * KT + (TAKEN[p] if tiles == 6 else TAKEN[p] + 3 * KT))
                                pe.wait_ge(hid_lo_done, i * BLOCK + (step - 1))
                            if j == 2:
                                pe.wait_ge(silu_done, i * BLOCK + step)
                            if j >= 6:
                                pe.wait_ge(taken, i * KT + (TAKEN[p] + (0 if tiles == 6 else 3 * KT) + j - 5))
                        at = (j * tiles + k) % 16 * P
                        last = three(psum[:, DOWN[j], 0:width], weights(slot, at),
                                     (hid_hi[:, k, 0:width], hid_lo[:, k, 0:width]),
                                     k == 0, k == tiles - 1)
                        if k == tiles - 1 and use is not uses[-1]:
                            last.then_inc(acc_ready, 1)
                        if middle is not None and (j, k) == (3, tiles - 1):
                            middle()
                    last.then_inc(multiplied, 1)

            def sum_squares(e):
                pe.wait_ge(sq_summed, e + 1)
                tiles = (0, 1) if e in (0, 1, 3) else (0, 1, 6, 7)
                for j in tiles:
                    if j >= 6:
                        pe.wait_ge(sq_done, len(SQUARED) * e + j - 2)
                    last = pe.matmul(psum[:, SSQ, 0:T], ones[:, :], (context_sq if e == 1 else scratch)[:, j, :],
                                     start=j == 0, stop=j == tiles[-1])
                last.then_inc(ssq_done, 1)

            def reduce_mod(half, i=0, per=1):
                pe.wait_ge(mod_step, i * (per * mod_ops(half)) + mod_steps_before(half + 1))
                for c in range(conditions(half)):
                    for k in range(4):
                        last = pe.transpose(psum[:, MODB + c, k * P:k * P + P], mod_acc[:, c, k * P:k * P + P], con[:, 0:P])
                last.then_inc(mod_reduced, 1)

            def ffn_step0(p, fresh):
                project(PASS[p], F_GATE, 0, fresh=fresh)
                project(PASS[p] + 1, F_UP, 0)

            def ffn_step(p, b, step, i=0, c=0):
                pe.wait_ge(silu_done, i * BLOCK + (STEPS * p + step))
                if step == 3:
                    pe.wait_ge(taken, i * KT + (TAKEN[p] + 4))
                ffn_project(p, b, F_GATE, i * 3 if step < STEPS - 1 else 0)
                pe.wait_ge(prod_done, i * BLOCK + (STEPS * p + step))
                if step == 3:
                    pe.wait_ge(taken, i * KT + (TAKEN[p] + 6))
                ffn_project(p, b + 1, F_UP, i * 3 if step < STEPS - 1 else 0)

            def ffn_pass(p):
                first, ahead, positions = MOD[p]
                b = PASS[p] + 2
                with pe.Fori(0, 3) as i:

                    def reduced(position):
                        if position in positions:
                            half, per = mod_slot(p, position)
                            reduce_mod(half - 1, i, per)

                    ffn_step(p, b, 1, i)
                    reduced(0)
                    ffn_step(p, b + 2, 2, i)
                    reduced(1)
                    down(p, b + 4, 6, i, lambda: reduced(2))
                    reduced(3)
                    ffn_step(p, b + 7, 3, i)
                    reduced(4)
                ffn_step(p, b + 27, STEPS - 1)
                if positions:
                    reduce_mod(first + ahead - 1 + 3 * len(positions))
                down(p, b + 29, 4)

            pe.wait_ge(consts_set, 2)
            pe.wait_ge(cond_ready, 1)
            for half in range(START_HALVES):
                for kh in range(2):
                    pe.wait_ge(start_arrived[2 * half + kh], 16)
                    for k in range(4):
                        last = pe.matmul(psum[0:2, half, :], cond[:, kh * 4 + k, :], start_mod[2 * half + kh][:, k, :],
                                         start=kh == 0 and k == 0, stop=kh == 1 and k == 3)
                    last.then_inc(start_used, 1)
                if half == 2:
                    sum_squares(0)
            pe.wait_ge(consts_in, 16)
            for half in range(START_HALVES):
                pe.wait_ge(start_rows, half + 1)
                for k in range(4):
                    at = half * 8 + 2 * k
                    last = pe.transpose(psum[:, MODB, at:at + 2], start_row[:, half, k * P:k * P + P], con[0:2, 0:2])
            last.then_inc(start_turned, 1)

            for who in range(2):
                for c, bank in enumerate((F_GATE, F_UP)):
                    slot = arrived(c)
                    for k in range(KT):
                        last = fresh_tile(who, (True, True), [psum[:, bank + a, who * T:who * T + T] for a in range(2)],
                                          slot, stream_in(k, who), k)
                        if (who, c, k) == (0, 1, 2):
                            sum_squares(1)
                    if who == 1:
                        last.then_inc(multiplied, 1)
            pe.wait_ge(std_done, 2)
            ffn_pass(0)
            sum_squares(2)

            project(MIX, 4, 0, fresh=2)
            project(MIX + 1, 5, 0)
            sum_squares(3)
            project(MIX + 2, 2, 0)
            project(MIX + 3, 3, 0)
            pe.wait_ge(pool_copied, 1)
            project(MIX + 4, 4, 0)
            pe.wait_ge(u_lo_done, 4 * KT)
            slot = arrived(MIX + 5)
            for a, bank in enumerate((6, 0)):
                for k in range(KT):
                    last = three(psum[:, bank, :], weights(slot, k * 256 + a * P), stream_in(k, 0, 2 * T),
                                 k == 0, k == KT - 1)
                if a == 0:
                    for i in range(QR):
                        if i % 2 == 0:
                            pe.wait_ge(q_sq_done, i // 2 + 1)
                        q_last = pe.matmul(psum[:, SSQ, 0:T], ones[:, :], cq_sq[:, i, :], start=i == 0, stop=i == QR - 1)
                    q_last.then_inc(q_ssq_done, 1)
            last.then_inc(multiplied, 1)
            slot = arrived(MIX + 6)
            for k in range(KT):
                last = three(psum[:, 1, :], weights(slot, k * P), stream_in(k, 0, 2 * T), k == 0, k == KT - 1)
                if k == KT // 2:
                    pe.wait_ge(pool_copied, 2)
                    pe.wait_ge(kv_sq_done, 2)
                    for i in range(KVR):
                        kv_last = pe.matmul(psum[:, 5, :], ones[:, :], ckv_sq[:, i, :], start=i == 0, stop=i == KVR - 1)
                    kv_last.then_inc(kv_ssq_done, 1)
            last.then_inc(multiplied, 1)

            def project_pair(r):
                slot = arrived(MIX + 7 + r)
                kv_at = QR * 256
                if r == 0:
                    pe.wait_ge(kv_lo_done, KVR)
                else:
                    pe.wait_ge(k_lo_done, 2 * r)
                for k in range(KVR):
                    last = three(psum[:, 2, :], weights(slot, kv_at + k * 256), (kvn_hi[:, k, :], kvn_lo[:, k, :]),
                                 k == 0, k == KVR - 1)
                last.then_inc(k_proj, 1)
                if r == 1:
                    pe.wait_ge(v_lo_done, 1)
                if r > 1:
                    pe.wait_ge(attn_lo_done, r - 1)
                for t in range(4):
                    for k in range(KVR):
                        at = kv_at + k * 256
                        cols = [w[:, slot, at + 2 * NOPE:at + 2 * NOPE + 2 * VD] for w in (w_hi, w_lo)]
                        rows = [w[:, k, t * P:t * P + P] for w in (kvn_hi, kvn_lo)]
                        last = three(psum[:, 3, t * P:t * P + P], rows, cols,
                                     k == 0, k == KVR - 1)
                last.then_inc(multiplied if r == 0 else v_proj, 1)

            def project_queries(r):
                slot = arrived(MIX + 7 + r)
                if r > 0:
                    pe.wait_ge(q_lo_done, r)
                for a in range(2):
                    for k in range(QR):
                        if r == 0 and a == 0:
                            pe.wait_ge(qn_lo_done, k + 1)
                        last = three(psum[:, 0, a * T:a * T + T], weights(slot, k * 256 + a * P),
                                     (qn_hi[:, k, :], qn_lo[:, k, :]), k == 0, k == QR - 1)
                last.then_inc(q_proj if r == 0 else multiplied, 1)

            def score_pair(r):
                rows = slice(0, NOPE + ROPE)
                pe.wait_ge(q_lo_done, r + 1)
                if r == 0:
                    pe.wait_ge(kr_lo_done, 2)
                else:
                    pe.wait_ge(pt_lo_done, 4 * r)
                for a in range(2):
                    pe.wait_ge(k_lo_done, 2 * r + a + 1)
                    for qt in range(2):
                        at = slice(a * T + qt * P, a * T + qt * P + P)
                        last = three(psum[:, 4 + 2 * a + qt, :], (q_hi[rows, at], q_lo[rows, at]),
                                     (k_hi[rows, a, :], k_lo[rows, a, :]), True, True)
                        last.then_inc(scored, 1)

            def turn_pair(r):
                for a in range(2):
                    pe.wait_ge(p_normal, 4 * r + 2 * a + 2)
                    for b in range(2):
                        for kt in range(2):
                            for qt in range(2):
                                at = kt * T + qt * P
                                key = (2 * b + kt) * P
                                last = pe.transpose(psum[:, 4 + 2 * a + b, at:at + P], probs[a][:, qt, key:key + P],
                                                    con[:, 0:P])
                        last.then_inc(p_turned, 1)

            def attend_pair(r):
                pe.wait_ge(v_lo_done, min(r + 2, PAIRS))
                for a in range(2):
                    for kt in range(4):
                        pe.wait_ge(pt_lo_done, 4 * r + 2 * a + kt // 2 + 1)
                        last = three(psum[:, 3, a * T:a * T + T],
                                     (v_hi[:, r % 2, kt * P:kt * P + P], v_lo[:, r % 2, kt * P:kt * P + P]),
                                     (pt_hi[:, a, kt, :], pt_lo[:, a, kt, :]), kt == 0, kt == 3)
                last.then_inc(pv_done, 1)

            def project_out_chunk(base, i, tiles):
                slot = arrived(base + i)
                for k in tiles:
                    if base == MIX + 12 and i == 0 and k < 4:
                        pe.wait_ge(pool_lo_done, 4)
                    if base == MIX + 12 and k >= 4:
                        pe.wait_ge(attn_lo_done, k - 3)
                    if base == CONV + 12 and k % 2 == 0:
                        pe.wait_ge(conv_lo_done, k // 2 + 1)
                    for a in range(2):
                        last = three(psum[:, i, a * T:a * T + T], weights(slot, k * 256 + a * P),
                                     (mix_hi[:, k, :], mix_lo[:, k, :]), k == 0, k == KT - 1, True, k == 0 and a == 0)
                if tiles[-1] == KT - 1:
                    last.then_inc(multiplied, 1)

            project_queries(0)
            project_pair(0)
            score_pair(0)
            for r in range(PAIRS):
                if r + 1 < PAIRS:
                    project_pair(r + 1)
                    turn_pair(r)
                    project_queries(r + 1)
                    attend_pair(r)
                    if r + 2 == PAIRS:
                        slot = arrived(MIX + 11)
                        pe.wait_ge(p_lo_done, 1)
                        pe.wait_ge(k_lo_done, 2 * PAIRS)
                        for g in range(4):
                            last = three(psum[:, 1 + g // 2, (g % 2) * T:(g % 2) * T + T], weights(slot, g * P),
                                         (p_hi[:, g, :], p_lo[:, g, :]), True, True)
                        last.then_inc(multiplied, 1)
                    score_pair(r + 1)
                else:
                    project_out_chunk(MIX + 12, 0, range(4))
                    project_out_chunk(MIX + 12, 1, range(4))
                    turn_pair(r)
                    project_out_chunk(MIX + 12, 2, range(4))
                    attend_pair(r)
            for i in range(3):
                project_out_chunk(MIX + 12, i, range(4, KT))
            project_out_chunk(MIX + 12, 3, range(KT))
            sum_squares(4)

            for p in (1, 2):
                ffn_step0(p, 3 + p)
                reduce_mod(MOD[p][0])
                ffn_pass(p)
                sum_squares(4 + p)

            for k, bank in enumerate((GATE, UP, 6)):
                project(CONV + k, bank, 0, fresh=6 if k == 0 else None)
            with pe.Fori(0, KT // 2 - 1) as i:
                pe.wait_ge(c_copied, i + 1)
                project(CONV + 3, GATE, 0, i)
                pe.wait_ge(z_done, i + 1)
                project(CONV + 4, UP, 0, i)
                pe.wait_ge(conv_done, i + 1)
                project(CONV + 5, 6, 0, i)
            for i in range(4):
                project_out_chunk(CONV + 12, i, range(KT))
            sum_squares(7)
            ffn_step0(3, 7)
            ffn_pass(3)
            sum_squares(8)


def _tiles(a):
    return a.reshape(a.shape[0] // P, P, a.shape[1]).transpose(1, 0, 2)


def _ffn_chunks(gate, up, down):
    gate, up, down = _tiles(gate), _tiles(up), _tiles(down)
    chunks = []
    for block in range(0, STEPS, BLOCK):
        last = min(block + BLOCK, STEPS)
        for s in range(block, last):
            chunks += [w[:, :, 256 * s:256 * s + 256].reshape(P, CH) for w in (gate, up)]
        w = down[:, 2 * block:2 * last].reshape(P, 2 * (last - block), KT, P).transpose(0, 2, 1, 3).reshape(P, -1)
        chunks += [w[:, c:c + CH] for c in range(0, w.shape[1], CH)]
    return chunks


def _column_chunks(w):
    w = _tiles(w)
    return [np.ascontiguousarray(w[:, :, c:c + 256]).reshape(P, CH) for c in range(0, w.shape[2], 256)]


def _padded(w):
    w = w.reshape(P, -1)
    return np.concatenate([w, np.zeros((P, CH - w.shape[1]), w.dtype)], axis=1)


def _swap(w):
    return np.concatenate([w[..., 8:16], w[..., 0:8], w[..., 24:32], w[..., 16:24]], axis=-1)


def kernel(**inputs):
    import concourse.bacc as _bacc
    from concourse.bass_utils import run_bass_kernel_spmd as _run

    a = {k: np.asarray(v) for k, v in inputs.items()}
    w_in = a["ab_w_in"][0]
    pool_in, cq_in, ckv_in, kr_in = w_in[:, 0:512], w_in[:, 512:1280], w_in[:, 1280:1536], w_in[:, 1536:1568]
    kr = _tiles(np.concatenate([np.zeros((D, NOPE), w_in.dtype), kr_in, _swap(kr_in)], axis=1))
    w_uq = a["w_uq"][0].reshape(QR * P, HEADS, NOPE + ROPE)
    w_uq = np.concatenate([w_uq, _swap(w_uq[:, :, NOPE:])], axis=2)
    w_ukv = a["w_ukv"][0].reshape(KVR * P, HEADS, NOPE + VD)
    heads = []
    for r in range(PAIRS):
        q = _tiles(w_uq[:, 2 * r:2 * r + 2].reshape(QR * P, 256)).reshape(P, QR * 256)
        pair = w_ukv[:, 2 * r:2 * r + 2]
        pair = np.stack([pair[:, :, :NOPE], pair[:, :, NOPE:]], axis=1)
        kv = _tiles(pair.reshape(KVR * P, 256)).reshape(P, KVR * 256)
        heads.append(np.concatenate([q, kv], axis=1))
    b_c_val = [_column_chunks(a["conv_w_in"][0][:, D * m:D * m + D]) for m in range(3)]
    chunks = _ffn_chunks(a["ffn_w_gate"][0, 0], a["ffn_w_up"][0, 0], a["ffn_w_down"][0, 0])
    cq_chunks = _column_chunks(cq_in)
    chunks += _column_chunks(pool_in) + cq_chunks + _column_chunks(ckv_in) + [_padded(kr)] + heads
    chunks += [_padded(a["pool_w"][0].transpose(1, 0, 2))] + _column_chunks(a["ab_w_out"][0])
    chunks += _ffn_chunks(a["ffn_w_gate"][0, 1], a["ffn_w_up"][0, 1], a["ffn_w_down"][0, 1])
    chunks += _ffn_chunks(a["ffn_w_gate"][1, 0], a["ffn_w_up"][1, 0], a["ffn_w_down"][1, 0])
    for i in range(4):
        chunks += [b_c_val[1][i], b_c_val[2][i], b_c_val[0][i]]
    chunks += _column_chunks(a["conv_w_out"][0])
    chunks += _ffn_chunks(a["ffn_w_gate"][1, 1], a["ffn_w_up"][1, 1], a["ffn_w_down"][1, 1])
    stream = np.stack(chunks)
    w_mod = a["w_mod"].reshape(LAYERS, 2, 4, P, HALVES, HALF).transpose(0, 4, 1, 3, 2, 5)
    w_mod = np.ascontiguousarray(w_mod).reshape(LAYERS * HALVES * 2, P, 4, HALF)

    def feature_major(x):
        return np.ascontiguousarray(x.reshape(T, KT, P).transpose(2, 1, 0))

    def columns(v):
        return v.reshape(-1, P).T

    cond = np.stack([a["c"][0], a["c_ctx"]]).reshape(2, KT, P).transpose(2, 1, 0).reshape(P, 2 * KT)
    conv_w = a["conv_w"][0].reshape(3, KT, P).transpose(2, 1, 0).reshape(P, 3 * KT)
    params = np.ascontiguousarray(np.concatenate(
        [columns(a["norm_g"]), columns(a["b_mod"]), columns(a["pool_scale"]), columns(a["q_norm_g"]),
         columns(a["kv_norm_g"]), conv_w, columns(a["final_norm_g"]), cond], axis=1))

    f = np.float32
    freqs = np.power(f(10000.0), -np.arange(0, 16, 2, dtype=f) / f(16))
    token = np.arange(T)
    table = np.zeros((P, T), f)
    for d in range(ROPE):
        pos = (token // 64 if d < 16 else token % 64).astype(f)
        angle = (pos * freqs[d % 8]).astype(f)
        table[NOPE + d] = np.cos(angle)
        table[NOPE + ROPE + d] = np.sin(angle) if d % 16 >= 8 else -np.sin(angle)
    consts = np.ascontiguousarray(np.concatenate([np.eye(P, dtype=f), table, table], axis=1))
    inv = np.zeros((4, T), f)
    for g, w in enumerate(WINDOWS):
        lo, hi = np.clip(token - w // 2, 0, T - 1), np.clip(token + (w - w // 2 - 1), 0, T - 1)
        inv[g] = f(1) / (hi - lo + 1).astype(f)
    inv = np.ascontiguousarray(np.broadcast_to(inv, (P, 4, T)))

    nc = _bacc.Bacc("TRN2", target_bir_lowering=False, num_devices=1)
    arrays = {"in_stream": stream, "in_w_mod": w_mod, "in_x": feature_major(a["x"][0]),
              "in_ctx": feature_major(a["ctx"][0]), "in_params": params, "in_consts": consts, "in_inv": inv}
    aps = [nc.dram_tensor(k, v.shape, mybir.dt.from_np(v.dtype), kind="ExternalInput").ap() for k, v in arrays.items()]
    result = nc.dram_tensor("out_h", (P, KT, T), mybir.dt.float32, kind="ExternalOutput").ap()
    build(nc, *aps, result)
    got = _run(nc, [arrays], core_ids=[0]).results[0]["out_h"]
    return np.ascontiguousarray(got.transpose(2, 1, 0)).reshape(1, T, D)
```
